# Optimizing a Trainium2 kernel written in Bass

```python
import math
import jax, jax.numpy as jnp
from jax import lax
import numpy as np

D_MODEL = 1024
BATCH = 1
SEQ = 2048
DEPTH = 1

HEAD_DIM = 64
DIFF_HEADS = 4
DIFF_V_DIM = 2 * HEAD_DIM
SWA_Q_HEADS = 8
SWA_KV_HEADS = 2
SWA_GROUP = SWA_Q_HEADS // SWA_KV_HEADS
WINDOW = 128
Q_BLOCK = 128
ROPE_THETA = 10000.0
N_GROUPS = 4
EXPERTS_PER_GROUP = 8
N_EXPERTS = N_GROUPS * EXPERTS_PER_GROUP
TOP_K_IN_GROUP = 2
EXPERT_FF = 512
EXPERT_BLOCK = 256
EPS = 1e-6
NEG = -1e30

DIFF_QK_COLS = DIFF_HEADS * 2 * HEAD_DIM
DIFF_V_COLS = DIFF_HEADS * DIFF_V_DIM
SWA_Q_COLS = SWA_Q_HEADS * HEAD_DIM
SWA_KV_COLS = SWA_KV_HEADS * HEAD_DIM
IN_COLS = 2 * DIFF_QK_COLS + DIFF_V_COLS + SWA_Q_COLS + 2 * SWA_KV_COLS
MIX_WIDTH = DIFF_V_COLS + SWA_Q_COLS
SPLITS = [DIFF_QK_COLS, 2 * DIFF_QK_COLS, 2 * DIFF_QK_COLS + DIFF_V_COLS,
          2 * DIFF_QK_COLS + DIFF_V_COLS + SWA_Q_COLS,
          2 * DIFF_QK_COLS + DIFF_V_COLS + SWA_Q_COLS + SWA_KV_COLS]

kernel_name = "hymba_diffattn_swasink_hiermoe"

def rms_norm(x, g):
    xf = x.astype(jnp.float32)
    y = xf * lax.rsqrt(jnp.mean(xf * xf, axis=-1, keepdims=True) + EPS)
    return (y * g.astype(jnp.float32)).astype(x.dtype)

def rope_tables(seq):
    inv = 1.0 / (ROPE_THETA ** (jnp.arange(0, HEAD_DIM, 2, dtype=jnp.float32) / HEAD_DIM))
    ang = jnp.arange(seq, dtype=jnp.float32)[:, None] * inv[None, :]
    return jnp.cos(ang), jnp.sin(ang)

def apply_rope(x, cos, sin):
    half = x.shape[-1] // 2
    shape = (1, x.shape[1]) + (1,) * (x.ndim - 3) + (half,)
    c = cos.reshape(shape).astype(x.dtype)
    s = sin.reshape(shape).astype(x.dtype)
    x1, x2 = x[..., :half], x[..., half:]
    return jnp.concatenate([x1 * c - x2 * s, x1 * s + x2 * c], axis=-1)

def diff_attention(q, k, v, lam, subln_g, lambda_init):
    B, S = q.shape[0], q.shape[1]
    nq = S // Q_BLOCK
    scale = HEAD_DIM ** -0.5
    qb = q.reshape(B, nq, Q_BLOCK, DIFF_HEADS, 2, HEAD_DIM).transpose(1, 0, 2, 3, 4, 5)
    kpos = jnp.arange(S)

    def block(args):
        qblk, i = args
        s = jnp.einsum('bqhcd,bkhcd->bhcqk', qblk, k).astype(jnp.float32) * scale
        qpos = i * Q_BLOCK + jnp.arange(Q_BLOCK)
        causal = kpos[None, :] <= qpos[:, None]
        p = jax.nn.softmax(jnp.where(causal, s, NEG), axis=-1)
        a = p[:, :, 0] - lam * p[:, :, 1]
        return jnp.einsum('bhqk,bkhd->bqhd', a.astype(v.dtype), v)

    o = lax.map(block, (qb, jnp.arange(nq)))
    o = o.transpose(1, 0, 2, 3, 4).reshape(B, S, DIFF_HEADS, DIFF_V_DIM)
    o = rms_norm(o, subln_g) * (1.0 - lambda_init)
    return o.reshape(B, S, DIFF_V_COLS)

def swa_sink_attention(q, k, v, sinks):
    B, S = q.shape[0], q.shape[1]
    nb = S // WINDOW
    scale = HEAD_DIM ** -0.5
    qb = q.reshape(B, nb, WINDOW, SWA_KV_HEADS, SWA_GROUP, HEAD_DIM)

    def with_prev(t):
        t = t.reshape(B, nb, WINDOW, SWA_KV_HEADS, HEAD_DIM)
        prev = jnp.concatenate([jnp.zeros_like(t[:, :1]), t[:, :-1]], axis=1)
        return jnp.concatenate([prev, t], axis=2)

    kw, vw = with_prev(k), with_prev(v)
    s = jnp.einsum('bnqkgd,bnjkd->bnkgqj', qb, kw).astype(jnp.float32) * scale
    qi = jnp.arange(WINDOW)[:, None]
    kj = jnp.arange(2 * WINDOW)[None, :]
    rel = qi + WINDOW - kj
    band = (rel >= 0) & (rel < WINDOW)
    blk = jnp.arange(nb)[:, None, None]
    valid = band[None] & ((blk * WINDOW + kj[None] - WINDOW) >= 0)
    s = jnp.where(valid[None, :, None, None], s, NEG)
    sink = jnp.broadcast_to(
        sinks.astype(jnp.float32).reshape(SWA_KV_HEADS, SWA_GROUP)[None, None, :, :, None, None],
        s.shape[:-1] + (1,))
    p = jax.nn.softmax(jnp.concatenate([s, sink], axis=-1), axis=-1)[..., :-1]
    o = jnp.einsum('bnkgqj,bnjkd->bnqkgd', p.astype(v.dtype), vw)
    return o.reshape(B, S, SWA_Q_COLS)

def hier_moe(xn, w_rg, b_rg, w_re, b_re, w_gate, w_up, w_down):
    B, S, D = xn.shape
    T = B * S
    xt = xn.reshape(T, D)
    pg = jax.nn.softmax((xt @ w_rg).astype(jnp.float32) + b_rg.astype(jnp.float32), axis=-1)
    p_top, g_idx = lax.top_k(pg, 1)
    el = ((xt @ w_re).astype(jnp.float32) + b_re.astype(jnp.float32)).reshape(T, N_GROUPS, EXPERTS_PER_GROUP)
    el_sel = jnp.take_along_axis(el, g_idx[:, :, None], axis=1)[:, 0]
    v2, i2 = lax.top_k(el_sel, TOP_K_IN_GROUP)
    gates = jax.nn.softmax(v2, axis=-1) * p_top
    expert_id = (g_idx * EXPERTS_PER_GROUP + i2).astype(jnp.int32)

    A = T * TOP_K_IN_GROUP
    NB = -(-A // EXPERT_BLOCK) + N_EXPERTS
    P = NB * EXPERT_BLOCK
    e_flat = expert_id.reshape(A)
    g_flat = gates.reshape(A)
    tok_flat = jnp.arange(A, dtype=jnp.int32) // TOP_K_IN_GROUP
    order = jnp.argsort(e_flat)
    e_s, g_s, tok_s = e_flat[order], g_flat[order], tok_flat[order]
    counts = jnp.bincount(e_flat, length=N_EXPERTS).astype(jnp.int32)
    start = jnp.cumsum(counts) - counts
    padded = ((counts + EXPERT_BLOCK - 1) // EXPERT_BLOCK) * EXPERT_BLOCK
    pad_end = jnp.cumsum(padded)
    pad_start = pad_end - padded
    dest = pad_start[e_s] + (jnp.arange(A, dtype=jnp.int32) - start[e_s])
    slot_tok = jnp.full((P,), T, jnp.int32).at[dest].set(tok_s)
    slot_gate = jnp.zeros((P,), jnp.float32).at[dest].set(g_s)
    block_start = jnp.arange(NB, dtype=jnp.int32) * EXPERT_BLOCK
    block_expert = jnp.minimum(jnp.searchsorted(pad_end, block_start, side='right'),
                               N_EXPERTS - 1).astype(jnp.int32)
    x_pad = jnp.concatenate([xt, jnp.zeros((1, D), xt.dtype)], axis=0)
    xs = x_pad[slot_tok].reshape(NB, EXPERT_BLOCK, D)

    def run_block(args):
        xb, e = args
        h = jax.nn.silu(xb @ w_gate[e]) * (xb @ w_up[e])
        return h @ w_down[e]

    ys = lax.map(run_block, (xs, block_expert)).reshape(P, D)
    out = jnp.zeros((T + 1, D), jnp.float32).at[slot_tok].add(ys.astype(jnp.float32) * slot_gate[:, None])[:T]
    return out.reshape(B, S, D).astype(xn.dtype)

def setup_inputs(seed: int = 0) -> dict:
    key = jax.random.key(seed)
    ks = jax.random.split(key, 20)
    f32 = jnp.float32
    L, D = DEPTH, D_MODEL
    nrm = lambda k, shape, s: jax.random.normal(k, shape, f32) * s
    return {
        "x": nrm(ks[0], (BATCH, SEQ, D), 1.0),
        "norm1_g": 1.0 + nrm(ks[1], (L, D), 0.05),
        "w_in": nrm(ks[2], (L, D, IN_COLS), D ** -0.5),
        "lambda_q1": nrm(ks[3], (L, HEAD_DIM), 0.1),
        "lambda_k1": nrm(ks[4], (L, HEAD_DIM), 0.1),
        "lambda_q2": nrm(ks[5], (L, HEAD_DIM), 0.1),
        "lambda_k2": nrm(ks[6], (L, HEAD_DIM), 0.1),
        "subln_g": 1.0 + nrm(ks[7], (L, DIFF_V_DIM), 0.05),
        "sinks": nrm(ks[8], (L, SWA_Q_HEADS), 0.5),
        "w_out": nrm(ks[9], (L, MIX_WIDTH, D), MIX_WIDTH ** -0.5),
        "norm2_g": 1.0 + nrm(ks[10], (L, D), 0.05),
        "w_router_group": nrm(ks[11], (L, D, N_GROUPS), D ** -0.5),
        "b_router_group": nrm(ks[12], (L, N_GROUPS), 0.01),
        "w_router_expert": nrm(ks[13], (L, D, N_EXPERTS), D ** -0.5),
        "b_router_expert": nrm(ks[14], (L, N_EXPERTS), 0.01),
        "w_gate": nrm(ks[15], (L, N_EXPERTS, D, EXPERT_FF), D ** -0.5),
        "w_up": nrm(ks[16], (L, N_EXPERTS, D, EXPERT_FF), D ** -0.5),
        "w_down": nrm(ks[17], (L, N_EXPERTS, EXPERT_FF, D), EXPERT_FF ** -0.5),
        "final_g": 1.0 + nrm(ks[18], (D,), 0.05),
    }

def reference(x, norm1_g, w_in, lambda_q1, lambda_k1, lambda_q2, lambda_k2, subln_g, sinks,
              w_out, norm2_g, w_router_group, b_router_group, w_router_expert, b_router_expert,
              w_gate, w_up, w_down, final_g):
    B, S, D = x.shape
    cos, sin = rope_tables(S)
    for l in range(DEPTH):
        lambda_init = 0.8 - 0.6 * math.exp(-0.3 * l)
        n1 = rms_norm(x, norm1_g[l])
        qkv = n1 @ w_in[l]
        dq, dk, dv, sq, sk, sv = jnp.split(qkv, SPLITS, axis=-1)
        dq = apply_rope(dq.reshape(B, S, DIFF_HEADS, 2, HEAD_DIM), cos, sin)
        dk = apply_rope(dk.reshape(B, S, DIFF_HEADS, 2, HEAD_DIM), cos, sin)
        dv = dv.reshape(B, S, DIFF_HEADS, DIFF_V_DIM)
        lam = (jnp.exp(jnp.sum(lambda_q1[l].astype(jnp.float32) * lambda_k1[l].astype(jnp.float32)))
               - jnp.exp(jnp.sum(lambda_q2[l].astype(jnp.float32) * lambda_k2[l].astype(jnp.float32)))
               + lambda_init)
        o_diff = diff_attention(dq, dk, dv, lam, subln_g[l], lambda_init)
        sq = apply_rope(sq.reshape(B, S, SWA_Q_HEADS, HEAD_DIM), cos, sin)
        sk = apply_rope(sk.reshape(B, S, SWA_KV_HEADS, HEAD_DIM), cos, sin)
        sv = sv.reshape(B, S, SWA_KV_HEADS, HEAD_DIM)
        o_swa = swa_sink_attention(sq, sk, sv, sinks[l])
        x = x + jnp.concatenate([o_diff, o_swa], axis=-1) @ w_out[l]
        n2 = rms_norm(x, norm2_g[l])
        x = x + hier_moe(n2, w_router_group[l], b_router_group[l], w_router_expert[l],
                         b_router_expert[l], w_gate[l], w_up[l], w_down[l])
    return rms_norm(x, final_g)


_drawn_inputs = setup_inputs


def setup_inputs(seed=0):
    import zlib

    import numpy as np

    out = dict(_drawn_inputs(seed))
    spreads = {}
    factors = {'lambda_q2': 200.0,
     'sinks': 25.583,
     'b_router_group': 3.837,
     'b_router_expert': 3.902,
     'lambda_q1': 2.896}
    for name, (base, spread) in spreads.items():
        noise = np.random.default_rng([zlib.crc32(name.encode()), seed]).standard_normal(out[name].shape)
        drawn = base * np.exp(spread * noise) if base else spread * noise
        out[name] = __import__('jax').numpy.asarray(drawn.astype(out[name].dtype))
    for name, factor in factors.items():
        out[name] = (out[name] * factor).astype(out[name].dtype)
    return out
```

```python
import math
from contextlib import ExitStack

import numpy as np
import concourse.bass as bass
from concourse import mybir

F32 = mybir.dt.float32
BF16 = mybir.dt.bfloat16
I32 = mybir.dt.int32
ALU = mybir.AluOpType
ACT = mybir.ActivationFunctionType
AX = mybir.AxisListType

P = 128
D = 1024
KD = D // P
SEQ = 2048
TILES = SEQ // P
HD = 64
DIFF_HEADS = 4
SWA_HEADS = 8
KV_HEADS = 2
IN_COLS = 2304
ROPE_HEADS = 26
QK_BLOCKS = ROPE_HEADS // 2
V_COLS = 640
EPS = 1e-6
NEG = -1e30


def row_broadcast(ap, width):
    return bass.AP(ap.tensor, ap.offset, [[0, P], [1, width]])


def over_pairs(eng, tile, last=TILES // 2):
    for s in range(2):
        tile(s, s)
    with eng.Fori(1, last - 1) as i:
        for s in range(2):
            tile(i * 2 + s, s)
    for s in range(2):
        tile(2 * last - 2 + s, s)


def static(t):
    return isinstance(t, int)


def projection(nc, sem, x, norm1_g, w_in, rope, ident_d, qk_d, v_d):
    with ExitStack() as ctx:
        def sb(name, shape, dt=F32):
            return ctx.enter_context(nc.sbuf_tensor(name, shape, dt))

        def ps(name, shape):
            return ctx.enter_context(nc.psum_tensor(name, shape, F32))

        w_sb = sb("w_in_sb", [P, KD, IN_COLS])
        ident = sb("ident1", [P, P])
        g_bc = sb("g1_bc", [P, D])
        rope_sb = sb("rope_sb", [P, TILES, 4, HD])
        x_sb = sb("x_sb", [P, 2, D])
        sq = sb("sq1", [P, D])
        ss = sb("ss1", [P, 2])
        power = sb("power1", [P, 2])
        var = sb("var1", [P, 2])
        rstd = sb("rstd1", [P, 2])
        n1 = sb("n1", [P, 2, D])
        n1T = sb("n1T", [P, 2, KD, P])
        cosx = sb("cosx", [P, 2, ROPE_HEADS, HD])
        roped = sb("roped", [P, 2, ROPE_HEADS, HD])
        vrow = sb("vrow", [P, 2, V_COLS])
        qkT = sb("qkT", [P, 2, QK_BLOCKS, P])

        proj = ps("proj", [P, 4, 512])
        n1t_ps = ps("n1t_ps", [P, KD, P])
        qkt_ps = ps("qkt_ps", [P, 2, 4, P])

        const_in = sem("p1_const_in")
        rope_in = sem("p1_rope_in")
        w_in_s = [sem(f"p1_w_in{g}") for g in range(5)]
        x_in = [sem("p1_x_in0"), sem("p1_x_in1")]
        ss_ready = sem("p1_ss_ready")
        var_ready = sem("p1_var_ready")
        rstd_ready = sem("p1_rstd_ready")
        power_ready = sem("p1_power_ready")
        n1_ready = sem("p1_n1_ready")
        n1t_turned = sem("p1_n1t_turned")
        n1t_ready = sem("p1_n1t_ready")
        proj_ready = sem("p1_proj_ready")
        rope_read = sem("p1_rope_read")
        roped_ready = sem("p1_roped_ready")
        v_ready = sem("p1_v_ready")
        qkt_turned = sem("p1_qkt_turned")
        qkt_ready = sem("p1_qkt_ready")
        stored = [sem("p1_stored0"), sem("p1_stored1")]

        w_v = w_in.rearrange("(k p) n -> p k n", p=P)
        GROUPS = [(0, 512, 0, 8, 0, 0), (512, 512, 8, 8, 2, 1), (1024, 512, None, 0, 0, 2),
                  (1536, 512, 16, 8, 0, 3), (2048, 256, 24, 2, 2, 0)]
        BATCH = [(0, 4), (4, 4), (8, 4), (12, 1)]

        with nc.Block() as block:
            @block.sync
            def _(sp):
                sp.dma_start(x_sb[:, 0, :], x[0:P, :]).then_inc(x_in[0], 16)
                sp.dma_start(ident[:, :], ident_d).then_inc(const_in, 16)
                sp.dma_start(g_bc[:, :], row_broadcast(norm1_g, D)).then_inc(const_in, 16)
                sp.dma_start(x_sb[:, 1, :], x[P:2 * P, :]).then_inc(x_in[1], 16)
                for g, (c0, w, _, _, _, _) in enumerate(GROUPS):
                    sp.dma_start(w_sb[:, :, c0:c0 + w], w_v[:, :, c0:c0 + w]).then_inc(w_in_s[g], 16)
                    if g == 0:
                        sp.dma_start(rope_sb[:, :, :, :].rearrange("p t k d -> p t (k d)"),
                                     rope.rearrange("(t p) c -> p t c", p=P)).then_inc(rope_in, 16)

                def store(t, s):
                    sp.wait_ge(qkt_ready, t * 4 + 4)
                    sp.dma_start(qk_d[:, :, bass.ts(t, P)].rearrange("b p t -> p b t"), qkT[:, s, :, :])\
                        .then_inc(stored[s], 16)
                    sp.wait_ge(v_ready, t * 2 + 2)
                    sp.dma_start(v_d[bass.ts(t, P), :], vrow[:, s, :]).then_inc(stored[s], 16)

                def tile(t, s):
                    if not (static(t) and t >= TILES - 2):
                        sp.wait_ge(n1_ready, t + 1)
                        sp.dma_start(x_sb[:, s, :], x[bass.ts(t + 2, P), :]).then_inc(x_in[s], 16)
                    if not (static(t) and t == 0):
                        store(t - 1, 1 - s)

                over_pairs(sp, tile)
                store(TILES - 1, 1)
                for s in range(2):
                    sp.wait_ge(stored[s], 16 * TILES)

            @block.scalar
            def _(act):
                def mean_square(t, s):
                    act.wait_ge(x_in[s], (t // 2 if static(t) else (t - s) // 2) * 16 + 16)
                    if not (static(t) and t < 2):
                        act.wait_ge(n1_ready, t - 1)
                    act.activation(sq[:, :], x_sb[:, s, :], ACT.Square, scale=1.0 / math.sqrt(D),
                                   accum_out=ss[:, s:s + 1]).then_inc(ss_ready, 1)

                def copy_n1t(t, s):
                    act.wait_ge(n1t_turned, t + 1)
                    act.copy(n1T[:, s, :, :], n1t_ps[:, :, :]).then_inc(n1t_ready, 1)

                def copy_qkt(t, s):
                    if not (static(t) and t < 2):
                        act.wait_ge(stored[s], (t - s) * 16)
                    for b, (first, n) in enumerate(BATCH):
                        act.wait_ge(qkt_turned, t * 4 + (b + 1))
                        act.copy(qkT[:, s, first:first + n, :], qkt_ps[:, b % 2, 0:n, :]).then_inc(qkt_ready, 1)

                def tile(t, s):
                    if not (static(t) and t == TILES - 1):
                        mean_square(t + 1, 1 - s)
                        copy_n1t(t + 1, 1 - s)
                    if not (static(t) and t < 2):
                        act.wait_ge(stored[s], (t - s) * 16)
                    act.wait_ge(proj_ready, t * 5 + 3)
                    act.copy(vrow[:, s, 0:512], proj[:, 2, :]).then_inc(v_ready, 1)
                    act.wait_ge(proj_ready, t * 5 + 5)
                    act.wait_ge(rope_read, t * 4 + 4)
                    act.copy(vrow[:, s, 512:640], proj[:, 0, 128:256]).then_inc(v_ready, 1)
                    if not (static(t) and t == 0):
                        copy_qkt(t - 1, 1 - s)

                mean_square(0, 0)
                copy_n1t(0, 0)
                over_pairs(act, tile)
                copy_qkt(TILES - 1, 1)

            @block.vector
            def _(dve):
                def normalize(t, s):
                    dve.wait_ge(rstd_ready, t + 1)
                    if not (static(t) and t < 2):
                        dve.wait_ge(n1t_turned, t - 1)
                    dve.scalar_tensor_tensor(out=n1[:, s, :], in0=x_sb[:, s, :], scalar=rstd[:, s:s + 1],
                                             in1=g_bc[:, :], op0=ALU.mult, op1=ALU.mult).then_inc(n1_ready, 1)

                def tile(t, s):
                    if not (static(t) and t == TILES - 1):
                        normalize(t + 1, 1 - s)
                    if static(t) and t == 0:
                        dve.wait_ge(rope_in, 16)
                    if not (static(t) and t < 2):
                        dve.wait_ge(qkt_turned, t * 4 - 4)
                    for g, (_, _, head, heads, table, bank) in enumerate(GROUPS):
                        if head is None:
                            continue
                        dve.wait_ge(proj_ready, t * 5 + (g + 1))
                        src = proj[:, bank, 0:heads * HD].rearrange("p (h d) -> p h d", d=HD)
                        cos = rope_sb[:, t:t + 1, table, :] if static(t) else rope_sb[:, bass.ds(t, 1), table, :]
                        sin = rope_sb[:, t:t + 1, table + 1, :] if static(t) else rope_sb[:, bass.ds(t, 1), table + 1, :]
                        dve.tensor_tensor(cosx[:, s, head:head + heads, :], src,
                                          cos.to_broadcast([P, heads, HD]), ALU.mult)
                        dve.tensor_tensor(roped[:, s, head:head + heads, 0:32], src[:, :, 32:64],
                                          sin[:, :, 0:32].to_broadcast([P, heads, 32]), ALU.mult)
                        dve.tensor_tensor(roped[:, s, head:head + heads, 32:64], src[:, :, 0:32],
                                          sin[:, :, 32:64].to_broadcast([P, heads, 32]), ALU.mult)\
                            .then_inc(rope_read, 1)

                dve.wait_ge(const_in, 32)
                normalize(0, 0)
                over_pairs(dve, tile)

            @block.gpsimd
            def _(pool):
                def inverse_root(t, s):
                    pool.wait_ge(ss_ready, t + 1)
                    pool.tensor_tensor(var[:, s:s + 1], ss[:, s:s + 1], power[:, 1:2], ALU.add).then_inc(var_ready, 1)
                    pool.wait_ge(var_ready, t + 1)
                    if not (static(t) and t < 2):
                        pool.wait_ge(n1_ready, t - 1)
                    pool.tensor_tensor(rstd[:, s:s + 1], var[:, s:s + 1], power[:, 0:1], ALU.pow)\
                        .then_inc(rstd_ready, 1)

                def tile(t, s):
                    if not (static(t) and t == TILES - 1):
                        inverse_root(t + 1, 1 - s)
                    for n, (head, heads) in enumerate([(0, 8), (8, 8), (16, 8), (24, 2)]):
                        pool.wait_ge(rope_read, t * 4 + (n + 1))
                        pool.tensor_tensor(roped[:, s, head:head + heads, :], roped[:, s, head:head + heads, :],
                                           cosx[:, s, head:head + heads, :], ALU.add).then_inc(roped_ready, 1)

                pool.memset(power[:, 0:1], -0.5).then_inc(power_ready, 1)
                pool.memset(power[:, 1:2], EPS).then_inc(power_ready, 1)
                pool.wait_ge(power_ready, 2)
                inverse_root(0, 0)
                over_pairs(pool, tile)

            @block.tensor
            def _(pe):
                def turn_n1(t, s):
                    pe.wait_ge(n1_ready, t + 1)
                    for k in range(KD):
                        mm = pe.transpose(n1t_ps[:, k, :], n1[:, s, k * P:(k + 1) * P], ident[:, :])
                    mm.then_inc(n1t_turned, 1)

                def group(t, s, g):
                    c0, w, _, _, _, bank = GROUPS[g]
                    if static(t) and t == 0:
                        pe.wait_ge(w_in_s[g], 16)
                    if g == 0:
                        pe.wait_ge(n1t_ready, t + 1)
                        if not (static(t) and t == 0):
                            pe.wait_ge(rope_read, t * 4)
                            pe.wait_ge(v_ready, t * 2)
                    if g == 4:
                        pe.wait_ge(rope_read, t * 4 + 1)
                    for k in range(KD):
                        mm = pe.matmul(proj[:, bank, 0:w], n1T[:, s, k, :], w_sb[:, k, c0:c0 + w],
                                       start=(k == 0), stop=(k == KD - 1))
                    mm.then_inc(proj_ready, 1)

                def turn_qk(t, s):
                    pe.wait_ge(roped_ready, t * 4 + 4)
                    blocks = roped[:, s, :, :].rearrange("p (b h) d -> p b (h d)", h=2)
                    for b, (first, n) in enumerate(BATCH):
                        if not (static(t) and t * 4 + b < 2):
                            pe.wait_ge(qkt_ready, t * 4 + (b - 1))
                        for j in range(n):
                            mm = pe.transpose(qkt_ps[:, b % 2, j, :], blocks[:, first + j, :], ident[:, :])
                        mm.then_inc(qkt_turned, 1)

                def tile(t, s):
                    group(t, s, 0)
                    group(t, s, 1)
                    if not (static(t) and t == TILES - 1):
                        turn_n1(t + 1, 1 - s)
                    for g in (2, 3, 4):
                        group(t, s, g)
                    if not (static(t) and t == 0):
                        turn_qk(t - 1, 1 - s)

                pe.wait_ge(const_in, 32)
                turn_n1(0, 0)
                over_pairs(pe, tile)
                turn_qk(TILES - 1, 1)
def diff_attention(nc, sem, qk_d, v_d, lambdas, subln_g, ident_d, causal_d, mix_d):
    LAG = 6
    CHUNK = 512
    DV = 2 * HD
    STEPS = []
    for m, i in enumerate(range(TILES - 1, -1, -1)):
        keys = (i + 1) * P
        for j in range(-(-keys // CHUNK)):
            STEPS.append((i, j, min(CHUNK, keys - j * CHUNK), m))
    N = len(STEPS)
    FIRST = {m: min(n for n in range(N) if STEPS[n][3] == m) for m in range(TILES)}
    LAST = {m: max(n for n in range(N) if STEPS[n][3] == m) for m in range(TILES)}
    ENDS = {n: m for m, n in LAST.items()}
    RING = 8
    assert RING > LAG and N % RING == 0 and N % 2 == 0
    LAMBDA_INIT = 0.8 - 0.6 * math.exp(-0.3 * 0)

    with ExitStack() as ctx:
        def sb(name, shape, dt=F32):
            return ctx.enter_context(nc.sbuf_tensor(name, shape, dt))

        def ps(name, shape):
            return ctx.enter_context(nc.psum_tensor(name, shape, F32))

        ident = sb("ident2", [P, P])
        causal_f = sb("causal_f", [P, 2, P])
        causal = sb("causal", [P, 2, P], BF16)
        lam_in = sb("lam_in", [P, 4, HD])
        lam_prod = sb("lam_prod", [P, 2, HD])
        lam = sb("lam", [P, 6])
        g_bc = sb("subln_bc", [P, DV])
        g_out = sb("subln_out", [P, DV])
        power = sb("power2", [P, 2])
        qT = sb("qT", [P, 2, SEQ])
        kT = sb("kT", [P, 2, SEQ])
        v = sb("v_sb", [P, 2, TILES, DV])
        prob = sb("prob", [P, RING, 2, CHUNK])
        nmax = sb("nmax", [P, 2, 2, N])
        nrow = sb("nrow", [P, 2, 2, TILES])
        part = sb("part", [P, 2, 2, N])
        fac = sb("fac", [P, 2, 2, N])
        part_row = sb("part_row", [P, 2, 2, N])
        total = sb("total", [P, 2, 2, TILES])
        inv = sb("inv", [P, 2, 2, TILES])
        scale = sb("scale", [P, 2, 2, N])
        aT = sb("aT", [P, 2, CHUNK])
        osq = sb("osq", [P, 2, DV])
        oss = sb("oss", [P, 2])
        ovar = sb("ovar", [P, 2])
        orstd = sb("orstd", [P, 2])
        onorm = sb("onorm", [P, 2, DV])
        oT = sb("oT", [P, 2, P])

        score = ps("score", [P, 2, 2, CHUNK])
        aT_ps = ps("aT_ps", [P, CHUNK])
        o_ps = ps("o_ps", [P, 2, CHUNK])
        oT_ps = ps("oT_ps", [P, CHUNK])

        const_in = sem("p2_const_in")
        lam_step = sem("p2_lam_step")
        mask_ready = sem("p2_mask_ready")
        power_ready = sem("p2_power_ready")
        head_in = [sem("p2_head_in0"), sem("p2_head_in1")]
        head_done = sem("p2_head_done")
        score_ready = sem("p2_score_ready")
        score_free = sem("p2_score_free")
        max_ready = sem("p2_max_ready")
        row_ready = sem("p2_row_ready")
        fac_ready = sem("p2_fac_ready")
        stat_step = sem("p2_stat_step")
        scaled = sem("p2_scaled")
        a_ready = sem("p2_a_ready")
        a_turned = sem("p2_a_turned")
        aT_ready = sem("p2_aT_ready")
        pv_done = sem("p2_pv_done")
        oss_ready = sem("p2_oss_ready")
        ovar_ready = sem("p2_ovar_ready")
        orstd_ready = sem("p2_orstd_ready")
        on_ready = sem("p2_on_ready")
        o_turned = sem("p2_o_turned")
        oT_ready = sem("p2_oT_ready")
        stored = [sem("p2_stored0"), sem("p2_stored1")]

        def over_heads(eng, head):
            with eng.Fori(0, DIFF_HEADS // 2) as i:
                for hh in range(2):
                    head(i * 2 + hh, hh)

        SLOTS = N + LAG + 3

        with nc.Block() as block:
            @block.sync
            def _(sp):
                def load(h, hh):
                    sp.dma_start(qT[:, hh, :], qk_d[h, :, :]).then_inc(head_in[hh], 16)
                    sp.dma_start(kT[:, hh, :], qk_d[DIFF_HEADS + h, :, :]).then_inc(head_in[hh], 16)
                    sp.dma_start(v[:, hh, :, :], v_d[:, h * DV:(h + 1) * DV].rearrange("(t p) d -> p t d", p=P))\
                        .then_inc(head_in[hh], 16)

                sp.dma_start(causal_f[:, :, :], causal_d.rearrange("k p n -> p k n")).then_inc(const_in, 16)
                sp.dma_start(ident[:, :], ident_d).then_inc(const_in, 16)
                sp.dma_start(g_bc[:, :], row_broadcast(subln_g, DV)).then_inc(const_in, 16)
                for n, a in enumerate(lambdas):
                    sp.dma_start(lam_in[:, n, :], row_broadcast(a, HD)).then_inc(const_in, 16)
                for s in range(2):
                    sp.sem_inc(stored[s], 16)
                load(0, 0)
                load(1, 1)
                for h in range(DIFF_HEADS):
                    for m in range(TILES):
                        t = TILES - 1 - m
                        sp.wait_ge(oT_ready, h * TILES + m + 2)
                        sp.dma_start(mix_d[h, :, t * P:(t + 1) * P], oT[:, m % 2, :]).then_inc(stored[m % 2], 16)
                    if h + 2 < DIFF_HEADS:
                        sp.wait_ge(head_done, h + 1)
                        load(h + 2, h % 2)
                for s in range(2):
                    sp.wait_ge(stored[s], 16 + 16 * DIFF_HEADS * TILES // 2)

            @block.scalar
            def _(act):
                act.wait_ge(lam_step, 2)
                act.activation(lam[:, 2:4], lam[:, 0:2], ACT.Exp).then_inc(lam_step, 1)
                act.sem_inc(score_free, 4)
                act.sem_inc(oT_ready, 1)

                def head(h, hh):
                    for n in range(SLOTS):
                        if n - 1 in ENDS:
                            m = ENDS[n - 1]
                            a, b = FIRST[m], LAST[m] + 1
                            act.wait_ge(row_ready, h * TILES + (m + 1))
                            for c in range(2):
                                act.activation(fac[:, hh, c, a:b], nmax[:, hh, c, a:b], ACT.Exp, scale=-1.0,
                                               bias=nrow[:, hh, c, m:m + 1]).then_inc(fac_ready, 1)
                        if n < N:
                            w = STEPS[n][2]
                            act.wait_ge(max_ready, h * N + (n + 1))
                            act.wait_ge(a_turned, h * N + (n + 1))
                            for c in range(2):
                                act.activation(prob[:, n % RING, c, 0:w], score[:, n % 2, c, 0:w], ACT.Exp,
                                               bias=nmax[:, hh, c, n:n + 1], accum_out=part[:, hh, c, n:n + 1])\
                                    .then_inc(score_free, 1)
                        u = n - (LAG - 2)
                        if 0 <= u < N:
                            w, m = STEPS[u][2], STEPS[u][3]
                            act.wait_ge(stat_step, h * (5 * TILES) + (5 * m + 5))
                            act.activation(prob[:, u % RING, 1, 0:w], prob[:, u % RING, 1, 0:w], ACT.Copy,
                                           scale=scale[:, hh, 1, u:u + 1]).then_inc(scaled, 1)
                        if n - LAG - 1 in ENDS:
                            m = ENDS[n - LAG - 1]
                            act.wait_ge(pv_done, h * N + (LAST[m] + 3))
                            act.wait_ge(on_ready, h * TILES + (m + 1))
                            act.activation(osq[:, m % 2, :], o_ps[:, m % 2, 0:DV], ACT.Square, scale=1.0 / math.sqrt(DV),
                                           accum_out=oss[:, m % 2:m % 2 + 1]).then_inc(oss_ready, 1)
                        if n - LAG - 3 in ENDS:
                            m = ENDS[n - LAG - 3]
                            act.wait_ge(o_turned, h * TILES + (m + 3))
                            act.wait_ge(stored[m % 2], h * (8 * TILES) + 16 * (m // 2 + 1))
                            act.copy(oT[:, m % 2, :], oT_ps[:, 0:P]).then_inc(oT_ready, 1)

                over_heads(act, head)

            @block.gpsimd
            def _(pool):
                pool.memset(power[:, 0:1], -0.5).then_inc(power_ready, 1)
                pool.memset(power[:, 1:2], EPS).then_inc(power_ready, 1)
                pool.wait_ge(power_ready, 2)
                with pool.Fori(0, DIFF_HEADS * TILES // 2) as i:
                    for s in range(2):
                        pool.wait_ge(oss_ready, i * 2 + (s + 1))
                        pool.tensor_tensor(ovar[:, s:s + 1], oss[:, s:s + 1], power[:, 1:2], ALU.add)\
                            .then_inc(ovar_ready, 1)
                        pool.wait_ge(ovar_ready, i * 2 + (s + 1))
                        pool.tensor_tensor(orstd[:, s:s + 1], ovar[:, s:s + 1], power[:, 0:1], ALU.pow)\
                            .then_inc(orstd_ready, 1)

            @block.vector
            def _(dve):
                dve.wait_ge(const_in, 16 * 7)
                dve.tensor_copy(causal[:, :, :], causal_f[:, :, :]).then_inc(mask_ready, 1)
                dve.tensor_scalar(g_out[:, :], g_bc[:, :], 1.0 - LAMBDA_INIT, None, ALU.mult).then_inc(mask_ready, 1)
                pairs = lam_in[:, :, :].rearrange("p (a b) d -> p a b d", b=2)
                dve.tensor_tensor(lam_prod[:, :, :], pairs[:, :, 0, :], pairs[:, :, 1, :], ALU.mult)\
                    .then_inc(lam_step, 1)
                dve.wait_ge(lam_step, 1)
                dve.tensor_reduce(lam[:, 0:2], lam_prod[:, :, :], AX.X, ALU.add).then_inc(lam_step, 1)
                dve.wait_ge(lam_step, 3)
                dve.tensor_tensor(lam[:, 4:5], lam[:, 2:3], lam[:, 3:4], ALU.subtract).then_inc(lam_step, 1)
                dve.wait_ge(lam_step, 4)
                dve.tensor_scalar(lam[:, 5:6], lam[:, 4:5], -1.0, -LAMBDA_INIT, ALU.mult, ALU.add)\
                    .then_inc(lam_step, 1)
                dve.wait_ge(lam_step, 5)
                dve.wait_ge(mask_ready, 2)
                dve.sem_inc(aT_ready, 1)
                dve.sem_inc(on_ready, 2)

                def head(h, hh):
                    for n in range(SLOTS):
                        if n - 1 in ENDS:
                            m = ENDS[n - 1]
                            dve.wait_ge(max_ready, h * N + n)
                            dve.tensor_reduce(nrow[:, hh, :, m:m + 1], nmax[:, hh, :, FIRST[m]:n], AX.X, ALU.min)\
                                .then_inc(row_ready, 1)
                        if n - LAG - 2 in ENDS:
                            m = ENDS[n - LAG - 2]
                            dve.wait_ge(orstd_ready, h * TILES + (m + 1))
                            dve.wait_ge(o_turned, h * TILES + (m + 1))
                            dve.scalar_tensor_tensor(out=onorm[:, m % 2, :], in0=o_ps[:, m % 2, 0:DV],
                                                     scalar=orstd[:, m % 2:m % 2 + 1], in1=g_out[:, :],
                                                     op0=ALU.mult, op1=ALU.mult).then_inc(on_ready, 1)
                        u = n - LAG
                        if 0 <= u < N:
                            w = STEPS[u][2]
                            dve.wait_ge(a_turned, h * N + (u + 1 + RING))
                            dve.wait_ge(pv_done, h * N + (u + 1))
                            dve.tensor_copy(aT[:, u % 2, 0:w], aT_ps[:, 0:w]).then_inc(aT_ready, 1)
                        u = n - (LAG - 1)
                        if 0 <= u < N:
                            w = STEPS[u][2]
                            dve.wait_ge(scaled, h * N + (u + 1))
                            dve.scalar_tensor_tensor(out=prob[:, u % RING, 0, 0:w], in0=prob[:, u % RING, 0, 0:w],
                                                     scalar=scale[:, hh, 0, u:u + 1],
                                                     in1=prob[:, u % RING, 1, 0:w],
                                                     op0=ALU.mult, op1=ALU.add).then_inc(a_ready, 1)
                        if n < N:
                            w = STEPS[n][2]
                            dve.wait_ge(score_ready, h * N + (n + 1))
                            dve.tensor_reduce(nmax[:, hh, :, n:n + 1], score[:, n % 2, :, 0:w], AX.X, ALU.max,
                                              negate=True).then_inc(max_ready, 1)
                        if n - 1 in ENDS:
                            m = ENDS[n - 1]
                            a, b = FIRST[m], LAST[m] + 1
                            step = h * (5 * TILES) + 5 * m
                            dve.wait_ge(fac_ready, h * (2 * TILES) + (2 * m + 2))
                            dve.tensor_tensor(part_row[:, hh, :, a:b], part[:, hh, :, a:b], fac[:, hh, :, a:b],
                                              ALU.mult).then_inc(stat_step, 1)
                            dve.wait_ge(stat_step, step + 1)
                            dve.tensor_reduce(total[:, hh, :, m:m + 1], part_row[:, hh, :, a:b], AX.X, ALU.add)\
                                .then_inc(stat_step, 1)
                            dve.wait_ge(stat_step, step + 2)
                            dve.reciprocal(inv[:, hh, :, m:m + 1], total[:, hh, :, m:m + 1]).then_inc(stat_step, 1)
                            dve.wait_ge(stat_step, step + 3)
                            dve.tensor_scalar(scale[:, hh, 1, a:b], fac[:, hh, 1, a:b], inv[:, hh, 1, m:m + 1],
                                              lam[:, 5:6], ALU.mult, ALU.mult).then_inc(stat_step, 1)
                            dve.tensor_scalar(scale[:, hh, 0, a:b], fac[:, hh, 0, a:b], inv[:, hh, 0, m:m + 1],
                                              None, ALU.mult).then_inc(stat_step, 1)

                over_heads(dve, head)

            @block.tensor
            def _(pe):
                pe.sem_inc(a_turned, RING)
                pe.sem_inc(pv_done, 2)
                pe.sem_inc(o_turned, 2)
                pe.wait_ge(const_in, 16 * 7)
                pe.wait_ge(mask_ready, 2)

                def head(h, hh):
                    for n in range(SLOTS):
                        u = n - LAG
                        if 0 <= u < N:
                            pe.wait_ge(a_ready, h * N + (u + 1))
                            pe.wait_ge(aT_ready, h * N + (u + 1))
                            for b in range(STEPS[u][2] // P):
                                mm = pe.transpose(aT_ps[:, b * P:(b + 1) * P],
                                                  prob[:, u % RING, 0, b * P:(b + 1) * P], ident[:, :])
                            mm.then_inc(a_turned, 1)
                        if n < N:
                            i, j, w, m = STEPS[n]
                            if n == 0:
                                pe.wait_ge(head_in[hh], (h - hh) * 24 + 48)
                            pe.wait_ge(score_free, h * (2 * N) + (2 * n + 2))
                            diagonal = j * CHUNK + w == (i + 1) * P
                            for c in range(2):
                                r = slice(c * HD, (c + 1) * HD)
                                mm = pe.matmul(score[:, n % 2, c, 0:w], qT[r, hh, i * P:(i + 1) * P],
                                               kT[r, hh, j * CHUNK:j * CHUNK + w], start=True, stop=not diagonal)
                            if diagonal:
                                for c in range(2):
                                    mm = pe.matmul(score[:, n % 2, c, w - P:w], causal[:, 0, :], causal[:, 1, :],
                                                   start=False, stop=True)
                            mm.then_inc(score_ready, 1)
                        if 0 <= u < N:
                            i, j, w, m = STEPS[u]
                            if u == FIRST[m]:
                                pe.wait_ge(on_ready, h * TILES + (m + 1))
                            pe.wait_ge(aT_ready, h * N + (u + 2))
                            for b in range(w // P):
                                mm = pe.matmul(o_ps[:, m % 2, 0:DV], aT[:, u % 2, b * P:(b + 1) * P],
                                               v[:, hh, j * (CHUNK // P) + b, :], start=(u == FIRST[m] and b == 0),
                                               stop=(u == LAST[m] and b == w // P - 1))
                            mm.then_inc(pv_done, 1)
                        if n - LAG - 3 in ENDS:
                            m = ENDS[n - LAG - 3]
                            pe.wait_ge(on_ready, h * TILES + (m + 3))
                            pe.wait_ge(oT_ready, h * TILES + (m + 1))
                            pe.transpose(oT_ps[:, 0:P], onorm[:, m % 2, :], ident[:, :]).then_inc(o_turned, 1)
                    pe.sem_inc(head_done, 1)

                over_heads(pe, head)
def window_attention(nc, sem, qk_d, v_d, sinks, ident_d, band_d, mix_d):
    GROUP = SWA_HEADS // KV_HEADS
    WIN = 2 * P
    HEAD_AT = [0, 2, 1, 3]
    Q0, K0, V0 = 2 * DIFF_HEADS, 2 * DIFF_HEADS + SWA_HEADS // 2, DIFF_HEADS * 2 * HD

    with ExitStack() as ctx:
        def sb(name, shape, dt=F32):
            return ctx.enter_context(nc.sbuf_tensor(name, shape, dt))

        def ps(name, shape):
            return ctx.enter_context(nc.psum_tensor(name, shape, F32))

        ident = sb("ident3", [P, P])
        band_f = sb("band_f", [P, 5, P])
        band = sb("band", [P, 5, P], BF16)
        sink = sb("sink", [P, SWA_HEADS])
        sink_in = sb("sink_in", [P, SWA_HEADS])
        nsink = sb("nsink", [P, SWA_HEADS])
        kwin = sb("kwin", [P, 2, KV_HEADS, WIN])
        v = sb("v_swa", [P, 2, 2, KV_HEADS * HD])
        q = sb("q_swa", [P, 2, SWA_HEADS // 2, P])
        prob = sb("prob_swa", [P, 2, GROUP, WIN])
        nmax = sb("nmax_swa", [P, 2, GROUP])
        nrow = sb("nrow_swa", [P, 2, GROUP])
        part = sb("part_swa", [P, 2, GROUP])
        over = sb("over_swa", [P, 2, GROUP])
        esink = sb("esink", [P, 2, GROUP])
        total = sb("total_swa", [P, 2, GROUP])
        inv = sb("inv_swa", [P, 2, GROUP])
        pT = sb("pT_swa", [P, 2, GROUP, WIN])
        o = sb("o_swa", [P, 2, SWA_HEADS * HD])
        oT = sb("oT_swa", [P, 2, SWA_HEADS // 2, P])

        score = ps("score_swa", [P, 2, GROUP, WIN])
        pT_ps = ps("pT_ps_swa", [P, GROUP, WIN])
        o_ps = ps("o_ps_swa", [P, 512])
        oT_ps = ps("oT_ps_swa", [P, SWA_HEADS // 2, P])

        const_in = sem("p3_const_in")
        mask_ready = sem("p3_mask_ready")
        q_in = [sem("p3_q_in0"), sem("p3_q_in1")]
        score_ready = sem("p3_score_ready")
        score_free = sem("p3_score_free")
        nmax_ready = sem("p3_nmax_ready")
        nrow_ready = sem("p3_nrow_ready")
        exp_ready = sem("p3_exp_ready")
        total_ready = sem("p3_total_ready")
        inv_ready = sem("p3_inv_ready")
        p_turned = sem("p3_p_turned")
        pT_ready = sem("p3_pT_ready")
        pv_done = sem("p3_pv_done")
        o_ready = sem("p3_o_ready")
        o_turned = sem("p3_o_turned")
        oT_ready = sem("p3_oT_ready")
        stored = [sem("p3_stored0"), sem("p3_stored1")]

        def tile_pairs(eng, tile):
            for s in range(2):
                tile(s, s)
            with eng.Fori(1, TILES // 2) as i:
                for s in range(2):
                    tile(i * 2 + s, s)

        with nc.Block() as block:
            @block.sync
            def _(sp):
                for s in range(2):
                    sp.sem_inc(stored[s], 16)
                sp.dma_start(band_f[:, :, :], band_d.rearrange("k p n -> p k n")).then_inc(const_in, 16)
                sp.dma_start(ident[:, :], ident_d).then_inc(const_in, 16)
                sp.dma_start(sink_in[:, :], row_broadcast(sinks, SWA_HEADS)).then_inc(const_in, 16)

                def load(t, s):
                    a = P if static(t) and t == 0 else 0
                    win = WIN - a
                    first = 0 if a else t * P - P
                    sp.dma_start(q[:, s, :, :], qk_d[Q0:Q0 + SWA_HEADS // 2, :, bass.ts(t, P)]
                                 .rearrange("b p t -> p b t")).then_inc(q_in[s], 16)
                    for half in range(2):
                        sp.dma_start(kwin[half * HD:(half + 1) * HD, s, :, a:],
                                     qk_d[K0, :, bass.ds(first, win)].rearrange("(g d) t -> d g t", d=HD))\
                            .then_inc(q_in[s], 16)
                    sp.dma_start(v[:, s, a // P:, :], v_d[bass.ds(first, win), V0:V0 + KV_HEADS * HD]
                                 .rearrange("(b p) d -> p b d", p=P)).then_inc(q_in[s], 16)

                def store(t, s):
                    sp.wait_ge(oT_ready, t + 1)
                    sp.dma_start(mix_d[DIFF_HEADS:, :, bass.ts(t, P)].rearrange("b p t -> p b t"), oT[:, s, :, :])\
                        .then_inc(stored[s], 16)

                def tile(t, s):
                    if not (static(t) and t < 2):
                        sp.wait_ge(pv_done, t * 2 - 2)
                    load(t, s)
                    if not (static(t) and t < 2):
                        store(t - 2, s)

                tile_pairs(sp, tile)
                for s in range(2):
                    store(TILES - 2 + s, s)
                for s in range(2):
                    sp.wait_ge(stored[s], 16 + 16 * TILES // 2)

            @block.vector
            def _(dve):
                dve.memset(kwin[:, 0, :, 0:P], 0.0)
                dve.memset(v[:, 0, 0, :], 0.0).then_inc(mask_ready, 1)
                dve.wait_ge(const_in, 16 * 3)
                dve.tensor_copy(band[:, :, :], band_f[:, :, :]).then_inc(mask_ready, 1)
                for g in range(KV_HEADS):
                    at = slice(g * GROUP, (g + 1) * GROUP)
                    by_bank = sink_in[:, at].rearrange("p (a b) -> p b a", b=2)
                    dve.tensor_copy(sink[:, at].rearrange("p (b a) -> p b a", b=2), by_bank)
                    dve.tensor_scalar(nsink[:, at].rearrange("p (b a) -> p b a", b=2), by_bank, -1.0, None,
                                      ALU.mult).then_inc(mask_ready, 1)
                dve.wait_ge(mask_ready, 4)
                dve.sem_inc(pT_ready, 1)
                dve.sem_inc(o_ready, 1)

                def finish(t, g):
                    step, b = t * 2 + g, g
                    dve.wait_ge(p_turned, step + 1)
                    dve.tensor_copy(pT[:, b, 0:2, :], pT_ps[:, 0:2, :]).then_inc(pT_ready, 1)
                    dve.wait_ge(exp_ready, step + 1)
                    dve.tensor_tensor(total[:, b, :], part[:, b, :], esink[:, b, :], ALU.add)\
                        .then_inc(total_ready, 1)
                    dve.wait_ge(total_ready, step + 1)
                    dve.reciprocal(inv[:, b, :], total[:, b, :]).then_inc(inv_ready, 1)
                    dve.wait_ge(inv_ready, step + 1)

                def output(t, g, s):
                    step = t * 2 + g
                    dve.wait_ge(pv_done, step + 1)
                    dve.wait_ge(o_turned, t + 1)
                    dve.tensor_tensor(
                        o[:, s, g * GROUP * HD:(g + 1) * GROUP * HD].rearrange("p (a b d) -> p a b d", a=2, d=HD),
                        o_ps[:, 0:GROUP * HD].rearrange("p (a b d) -> p a b d", a=2, d=HD),
                        inv[:, g, :].rearrange("p (b a) -> p a b", b=2).unsqueeze(3)
                        .to_broadcast([P, 2, 2, HD]), ALU.mult).then_inc(o_ready, 1)

                def tile(t, s):
                    for g in range(KV_HEADS):
                        step = t * 2 + g
                        heads = slice(g * GROUP, (g + 1) * GROUP)
                        dve.wait_ge(score_ready, step + 1)
                        dve.tensor_reduce(nmax[:, g, :], score[:, g, :, :], AX.X, ALU.max, negate=True)\
                            .then_inc(nmax_ready, 1)
                        dve.wait_ge(nmax_ready, step + 1)
                        dve.tensor_tensor(nrow[:, g, :], nmax[:, g, :], nsink[:, heads], ALU.min)\
                            .then_inc(nrow_ready, 1)
                        dve.wait_ge(nrow_ready, step * 2 + 1)
                        dve.tensor_tensor(over[:, g, :], nrow[:, g, :], sink[:, heads], ALU.add)\
                            .then_inc(nrow_ready, 1)
                        if not (static(t) and t == 0 and g == 0):
                            pt, pg, psl = (t, 0, s) if g else (t - 1, 1, 1 - s)
                            finish(pt, pg)
                            output(pt, pg, psl)

                tile_pairs(dve, tile)
                finish(TILES - 1, 1)
                output(TILES - 1, 1, 1)

            @block.scalar
            def _(act):
                act.sem_inc(score_free, 2 * GROUP)
                act.sem_inc(pT_ready, 1)

                def copy_pT(t, g):
                    step = t * 2 + g
                    act.wait_ge(p_turned, step + 1)
                    act.copy(pT[:, g, 2:4, :], pT_ps[:, 2:4, :]).then_inc(pT_ready, 1)

                def copy_oT(t, s):
                    act.wait_ge(o_turned, t + 3)
                    act.wait_ge(stored[s], (t - s) * 8 + 16)
                    act.copy(oT[:, s, :, :], oT_ps[:, :, :]).then_inc(oT_ready, 1)

                def tile(t, s):
                    for g in range(KV_HEADS):
                        step = t * 2 + g
                        act.wait_ge(nrow_ready, step * 2 + 2)
                        if not (static(t) and t == 0):
                            act.wait_ge(p_turned, step - 1)
                            act.wait_ge(total_ready, step - 1)
                        for hd in range(GROUP):
                            act.activation(prob[:, g, hd, :], score[:, g, hd, :], ACT.Exp,
                                               bias=nrow[:, g, hd:hd + 1], accum_out=part[:, g, hd:hd + 1])\
                                .then_inc(score_free, 1)
                        act.activation(esink[:, g, :], over[:, g, :], ACT.Exp).then_inc(exp_ready, 1)
                        if not (static(t) and t == 0 and g == 0):
                            pt, pg = (t, 0) if g else (t - 1, 1)
                            copy_pT(pt, pg)
                        if g == 1 and not (static(t) and t == 0):
                            copy_oT(t - 1, 1 - s)

                tile_pairs(act, tile)
                copy_pT(TILES - 1, 1)
                copy_oT(TILES - 1, 1)

            @block.tensor
            def _(pe):
                pe.sem_inc(o_turned, 2)
                pe.wait_ge(const_in, 16 * 3)
                pe.wait_ge(mask_ready, 4)

                def turn_p(t, g):
                    step = t * 2 + g
                    pe.wait_ge(score_free, (step + 3) * GROUP)
                    pe.wait_ge(pT_ready, step * 2 + 2)
                    for hd in range(GROUP):
                        for b in range(2):
                            mm = pe.transpose(pT_ps[:, hd, b * P:(b + 1) * P], prob[:, g, hd, b * P:(b + 1) * P],
                                              ident[:, :])
                    mm.then_inc(p_turned, 1)

                def times_v(t, g, s):
                    step = t * 2 + g
                    pe.wait_ge(pT_ready, step * 2 + 4)
                    pe.wait_ge(o_ready, step + 1)
                    for at in range(GROUP):
                        hd = HEAD_AT[at]
                        for b in range(2):
                            vv = v[:, s, b, g * HD:(g + 1) * HD]
                            mm = pe.matmul(o_ps[:, hd * HD:(hd + 1) * HD], pT[:, g, at, b * P:(b + 1) * P], vv,
                                           start=(b == 0), stop=(b == 1))
                    mm.then_inc(pv_done, 1)

                def turn_o(t, s):
                    pe.wait_ge(o_ready, t * 2 + 3)
                    if not (static(t) and t == 0):
                        pe.wait_ge(oT_ready, t)
                    for b in range(SWA_HEADS // 2):
                        mm = pe.transpose(oT_ps[:, b, :], o[:, s, b * P:(b + 1) * P], ident[:, :])
                    mm.then_inc(o_turned, 1)

                def tile(t, s):
                    for g in range(KV_HEADS):
                        step = t * 2 + g
                        later = not (static(t) and t == 0 and g == 0)
                        pt, pg = (t, 0) if g else (t - 1, 1)
                        if later:
                            turn_p(pt, pg)
                        if g == 0:
                            pe.wait_ge(q_in[s], (t - s) * 32 + 64)
                        pe.wait_ge(score_free, (step + 1) * GROUP)
                        for at in range(GROUP):
                            hq = g * GROUP + HEAD_AT[at]
                            r = slice((hq % 2) * HD, (hq % 2 + 1) * HD)
                            mm = pe.matmul(score[:, g, at, :], q[r, s, hq // 2, :],
                                           kwin[r, s, g, :], start=True, stop=False)
                            mask = band[:, 1:3, :] if static(t) and t == 0 else band[:, 3:5, :]
                            mm = pe.matmul(score[:, g, at, :], band[:, 0, :], mask, start=False, stop=True)
                        mm.then_inc(score_ready, 1)
                        if later:
                            times_v(pt, pg, s if g else 1 - s)
                        if g == 1 and not (static(t) and t == 0):
                            turn_o(t - 1, 1 - s)

                tile_pairs(pe, tile)
                turn_p(TILES - 1, 1)
                times_v(TILES - 1, 1, 1)
                turn_o(TILES - 1, 1)
N_GROUPS = 4
N_EXPERTS = 32
PER_GROUP = N_EXPERTS // N_GROUPS
LOGITS = N_GROUPS + N_EXPERTS


def output_projection(nc, sem, x, mix_d, w_out, norm2_g, w_rg, b_rg, w_re, b_re, ident_d, h_sb, logits, n2_d):
    with ExitStack() as ctx:
        def sb(name, shape, dt=F32):
            return ctx.enter_context(nc.sbuf_tensor(name, shape, dt))

        def ps(name, shape):
            return ctx.enter_context(nc.psum_tensor(name, shape, F32))

        ident = sb("ident4", [P, P])
        w_sb = sb("w_out_sb", [P, KD, D])
        wr_sb = sb("w_router_sb", [P, KD, LOGITS])
        br_sb = sb("b_router_sb", [P, LOGITS])
        g_bc = sb("g2_bc", [P, D])
        power = sb("power4", [P, 2])
        mixT = sb("mixT", [P, 2, KD, P])
        x_sb = sb("x4_sb", [P, 2, D])
        sq = sb("sq4", [P, 2, D])
        ss = sb("ss4", [P, 2])
        var = sb("var4", [P, 2])
        rstd = sb("rstd4", [P, 2])
        n2 = sb("n2", [P, 2, D])
        n2T = sb("n2T", [P, 2, KD, P])

        proj = ps("proj4", [P, 2, 2, 512])
        n2t_ps = ps("n2t_ps", [P, KD, P])
        lg_ps = ps("lg_ps", [P, LOGITS])

        const_in = sem("p4_const_in")
        power_ready = sem("p4_power_ready")
        w_in_s = [sem(f"p4_w_in{k}") for k in range(2)]
        tile_in = [sem("p4_tile_in0"), sem("p4_tile_in1")]
        proj_ready = sem("p4_proj_ready")
        h_ready = sem("p4_h_ready")
        ss_ready = sem("p4_ss_ready")
        var_ready = sem("p4_var_ready")
        rstd_ready = sem("p4_rstd_ready")
        n2_ready = sem("p4_n2_ready")
        n2_turned = sem("p4_n2_turned")
        n2T_ready = sem("p4_n2T_ready")
        lg_ready = sem("p4_lg_ready")
        lg_done = sem("p4_lg_done")
        stored = [sem("p4_stored0"), sem("p4_stored1")]

        with nc.Block() as block:
            @block.sync
            def _(sp):
                def load(t, s):
                    sp.dma_start(mixT[:, s, :, :], mix_d[:, :, bass.ts(t, P)].rearrange("b p t -> p b t"))\
                        .then_inc(tile_in[s], 16)
                    sp.dma_start(x_sb[:, s, :], x[bass.ts(t, P), :]).then_inc(tile_in[s], 16)

                load(0, 0)
                wv = w_out.rearrange("(k p) n -> p k n", p=P)
                for k in range(2):
                    sp.dma_start(w_sb[:, k * 4:k * 4 + 4, :], wv[:, k * 4:k * 4 + 4, :]).then_inc(w_in_s[k], 16)
                load(1, 1)
                sp.dma_start(ident[:, :], ident_d).then_inc(const_in, 16)
                sp.dma_start(g_bc[:, :], row_broadcast(norm2_g, D)).then_inc(const_in, 16)
                sp.dma_start(wr_sb[:, :, 0:N_GROUPS], w_rg.rearrange("(k p) n -> p k n", p=P)).then_inc(const_in, 16)
                sp.dma_start(wr_sb[:, :, N_GROUPS:], w_re.rearrange("(k p) n -> p k n", p=P)).then_inc(const_in, 16)
                sp.dma_start(br_sb[:, 0:N_GROUPS], row_broadcast(b_rg, N_GROUPS)).then_inc(const_in, 16)
                sp.dma_start(br_sb[:, N_GROUPS:], row_broadcast(b_re, N_EXPERTS)).then_inc(const_in, 16)

                def store(t, s):
                    sp.wait_ge(n2_ready, t + 1)
                    sp.dma_start(n2_d[bass.ts(t, P), :], n2[:, s, :]).then_inc(stored[s], 16)

                def tile(t, s):
                    if not (static(t) and t >= TILES - 2):
                        sp.wait_ge(h_ready, t + 1)
                        load(t + 2, s)
                    store(t, s)

                over_pairs(sp, tile)
                for s in range(2):
                    sp.wait_ge(stored[s], 8 * TILES)

            @block.vector
            def _(dve):
                def residual(t, s):
                    dve.wait_ge(proj_ready, t + 1)
                    h = h_sb[:, t:t + 1, :] if static(t) else h_sb[:, bass.ds(t, 1), :]
                    dve.tensor_tensor(h, proj[:, s, :, :].rearrange("p (o a) b -> p o (a b)", o=1),
                                      x_sb[:, s:s + 1, :], ALU.add).then_inc(h_ready, 1)

                def normalize(t, s):
                    dve.wait_ge(rstd_ready, t + 1)
                    if not (static(t) and t < 2):
                        dve.wait_ge(n2_turned, t - 1)
                        dve.wait_ge(stored[s], (t - s) * 8)
                    h = h_sb[:, t:t + 1, :] if static(t) else h_sb[:, bass.ds(t, 1), :]
                    dve.scalar_tensor_tensor(out=n2[:, s:s + 1, :], in0=h, scalar=rstd[:, s:s + 1],
                                             in1=g_bc[:, :].rearrange("p (o a) -> p o a", o=1),
                                             op0=ALU.mult, op1=ALU.mult).then_inc(n2_ready, 1)

                def take_logits(t, s):
                    dve.wait_ge(lg_ready, t + 1)
                    out = logits[:, t:t + 1, :] if static(t) else logits[:, bass.ds(t, 1), :]
                    dve.tensor_tensor(out, lg_ps[:, :].rearrange("p (o a) -> p o a", o=1),
                                      br_sb[:, :].rearrange("p (o a) -> p o a", o=1), ALU.add).then_inc(lg_done, 1)

                def tile(t, s):
                    residual(t, s)
                    if static(t) and t == 0:
                        dve.wait_ge(const_in, 96)
                    dve.wait_ge(h_ready, t + 1)
                    normalize(t, s)
                    if not (static(t) and t == 0):
                        take_logits(t - 1, 1 - s)

                over_pairs(dve, tile)
                take_logits(TILES - 1, 1)

            @block.scalar
            def _(act):
                def tile(t, s):
                    act.wait_ge(h_ready, t + 1)
                    if not (static(t) and t < 2):
                        act.wait_ge(n2_ready, t - 1)
                    h = h_sb[:, t:t + 1, :] if static(t) else h_sb[:, bass.ds(t, 1), :]
                    act.activation(sq[:, s:s + 1, :], h, ACT.Square, scale=1.0 / math.sqrt(D),
                                   accum_out=ss[:, s:s + 1]).then_inc(ss_ready, 1)
                    act.wait_ge(n2_turned, t + 1)
                    act.copy(n2T[:, s, :, :], n2t_ps[:, :, :]).then_inc(n2T_ready, 1)

                over_pairs(act, tile)

            @block.gpsimd
            def _(pool):
                pool.memset(power[:, 0:1], -0.5).then_inc(power_ready, 1)
                pool.memset(power[:, 1:2], EPS).then_inc(power_ready, 1)
                pool.wait_ge(power_ready, 2)

                def tile(t, s):
                    pool.wait_ge(ss_ready, t + 1)
                    pool.tensor_tensor(var[:, s:s + 1], ss[:, s:s + 1], power[:, 1:2], ALU.add).then_inc(var_ready, 1)
                    pool.wait_ge(var_ready, t + 1)
                    pool.tensor_tensor(rstd[:, s:s + 1], var[:, s:s + 1], power[:, 0:1], ALU.pow)\
                        .then_inc(rstd_ready, 1)

                over_pairs(pool, tile)

            @block.tensor
            def _(pe):
                def project(t, s):
                    pe.wait_ge(tile_in[s], (t - s) * 16 + 32)
                    if not (static(t) and t < 2):
                        pe.wait_ge(h_ready, t - 1)
                    for k in range(KD):
                        if static(t) and t == 0 and k % 4 == 0:
                            pe.wait_ge(w_in_s[k // 4], 16)
                        for half in range(2):
                            mm = pe.matmul(proj[:, s, half, :], mixT[:, s, k, :],
                                           w_sb[:, k, half * 512:(half + 1) * 512], start=(k == 0), stop=(k == KD - 1))
                    mm.then_inc(proj_ready, 1)

                def turn(t, s):
                    pe.wait_ge(n2_ready, t + 1)
                    if not (static(t) and t == 0):
                        pe.wait_ge(n2T_ready, t)
                    for k in range(KD):
                        mm = pe.transpose(n2t_ps[:, k, :], n2[:, s, k * P:(k + 1) * P], ident[:, :])
                    mm.then_inc(n2_turned, 1)

                def route(t, s):
                    pe.wait_ge(n2T_ready, t + 1)
                    if not (static(t) and t == 0):
                        pe.wait_ge(lg_done, t)
                    for k in range(KD):
                        mm = pe.matmul(lg_ps[:, :], n2T[:, s, k, :], wr_sb[:, k, :], start=(k == 0), stop=(k == KD - 1))
                    mm.then_inc(lg_ready, 1)

                def tile(t, s):
                    project(t, s)
                    if static(t) and t == 0:
                        pe.wait_ge(const_in, 96)
                    else:
                        turn(t - 1, 1 - s)
                    if not (static(t) and t <= 1):
                        route(t - 2, s)

                over_pairs(pe, tile)
                turn(TILES - 1, 1)
                route(TILES - 2, 0)
                route(TILES - 1, 1)
BLOCKS = 64
MAX_TOK = 1e30


def routing(nc, sem, logits, tables_d, gates, dest, slots, starts):
    G, E, PG = N_GROUPS, N_EXPERTS, PER_GROUP
    T = TILES
    VDIFF = 23
    BEFORE = VDIFF + 2 + T
    NBLK = BEFORE + 3
    with ExitStack() as ctx:
        def sb(name, shape, dt=F32):
            return ctx.enter_context(nc.sbuf_tensor(name, shape, dt))

        def ps(name, shape):
            return ctx.enter_context(nc.psum_tensor(name, shape, F32))

        tri = sb("tri", [P, P])
        ones = sb("ones5", [P, P])
        iota = sb("iota5", [P, P])
        tok = sb("tok5", [P, P])
        gmax = sb("gmax", [P, T])
        gdiff = sb("gdiff", [P, T, G])
        gexp = sb("gexp", [P, T, G])
        gsum = sb("gsum", [P, T])
        ptop = sb("ptop", [P, T])
        geq = sb("geq", [P, T, G])
        gidx = sb("gidx", [P, T])
        ghot = sb("ghot", [P, T, G])
        el = sb("el", [P, T, E])
        eq = sb("eq", [P, T, E])
        top = sb("top", [P, 2, T])
        eidx = sb("eidx", [P, 2, T])
        hot = sb("hot", [P, 2, T, E])
        both = sb("both", [P, T, E])
        before = sb("before", [P, T + 1, E])
        vdiff = sb("vdiff", [P, T])
        vexp = sb("vexp", [P, T])
        vsum = sb("vsum", [P, T])
        vinv = sb("vinv", [P, T])
        rank_i = sb("rank_i", [P, T, E], I32)
        pos_i = sb("pos_i", [P, T, E], I32)
        blk_i = sb("blk_i", [P, T, E], I32)
        posf = sb("posf", [P, T, E])
        blkf = sb("blkf", [P, T, E])
        count_i = sb("count_i", [P, 1], I32)
        nb_i = sb("nb_i", [P, 1], I32)
        nb = sb("nb", [P, 1])
        start_row = sb("start_row", [P, E + 1])
        prod = sb("prod5", [P, 2, T, E])
        pos_k = sb("pos_k", [P, 2, T])
        blk_k = sb("blk_k", [P, 2, T])
        destf = sb("destf", [P, 2, T])
        at_pos = sb("at_pos", [P, 2, P])
        at_blk = sb("at_blk", [P, 2, BLOCKS + 1])

        rank_ps = ps("rank_ps", [P, T * E])
        count_ps = ps("count_ps", [P, 1])
        start_ps = ps("start_ps", [P, E + 1])
        slot_ps = ps("slot_ps", [P, BLOCKS + 1])

        const_in = sem("p5_const_in")
        step = sem("p5_step")
        act_step = sem("p5_act_step")
        pe_step = sem("p5_pe_step")
        pair_ready = sem("p5_pair_ready")
        pair_used = sem("p5_pair_used")

        with nc.Block() as block:
            @block.sync
            def _(sp):
                for n, a in enumerate((tri, ones, iota, tok)):
                    sp.dma_start(a[:, :], tables_d[n, :, :]).then_inc(const_in, 16)

            @block.scalar
            def _(act):
                act.wait_ge(step, 2)
                act.activation(gexp[:, :, :], gdiff[:, :, :], ACT.Exp).then_inc(act_step, 1)
                act.wait_ge(step, VDIFF)
                act.activation(vexp[:, :], vdiff[:, :], ACT.Exp).then_inc(act_step, 1)

            @block.tensor
            def _(pe):
                pe.wait_ge(const_in, 64)
                pe.wait_ge(step, BEFORE)
                pe.matmul(rank_ps[:, :], tri[:, :], both[:, :, :], start=True, stop=False)
                pe.matmul(rank_ps[:, :], ones[:, :], before[:, 0:T, :], start=False, stop=True).then_inc(pe_step, 1)
                pe.matmul(count_ps[0:E, :], before[:, T, :], ones[:, 0:1], start=True, stop=True).then_inc(pe_step, 1)
                pe.wait_ge(step, NBLK)
                pe.matmul(start_ps[:, :], nb[0:E, :].to_broadcast([E, P]), tri[0:E, 0:E + 1], start=True, stop=True)\
                    .then_inc(pe_step, 1)
                for n in range(2 * T):
                    pe.wait_ge(pair_ready, n + 1)
                    pe.matmul(slot_ps[:, :], at_pos[:, n % 2, :], at_blk[:, n % 2, :], start=(n == 0),
                              stop=(n == 2 * T - 1)).then_inc(pair_used, 1)

            @block.vector
            def _(dve):
                done = [0]

                def then(ins):
                    done[0] += 1
                    ins.then_inc(step, 1)
                    dve.wait_ge(step, done[0])

                gl = logits[:, :, 0:G]

                def bc(a, n):
                    return a.unsqueeze(2).to_broadcast([P, T, n])

                def iota_bc(n):
                    return iota[:, 0:n].unsqueeze(1).to_broadcast([P, T, n])

                dve.wait_ge(const_in, 64)
                then(dve.tensor_reduce(gmax[:, :], gl, AX.X, ALU.max))
                then(dve.tensor_tensor(gdiff[:, :, :], gl, bc(gmax[:, :], G), ALU.subtract))
                then(dve.tensor_tensor(geq[:, :, :], gl, bc(gmax[:, :], G), ALU.is_equal))
                then(dve.scalar_tensor_tensor(out=geq[:, :, :], in0=geq[:, :, :], scalar=-float(P),
                                              in1=iota_bc(G), op0=ALU.mult, op1=ALU.add))
                then(dve.tensor_reduce(gidx[:, :], geq[:, :, :], AX.X, ALU.min))
                then(dve.tensor_scalar(gidx[:, :], gidx[:, :], float(P), None, ALU.add))
                then(dve.tensor_tensor(ghot[:, :, :], iota_bc(G), bc(gidx[:, :], G), ALU.is_equal))
                then(dve.tensor_scalar(ghot[:, :, :], ghot[:, :, :], MAX_TOK, -MAX_TOK, ALU.mult, ALU.add))
                then(dve.tensor_tensor(el[:, :, :].rearrange("p t (g e) -> p t g e", g=G),
                                       logits[:, :, G:].rearrange("p t (g e) -> p t g e", g=G),
                                       ghot[:, :, :].unsqueeze(3).to_broadcast([P, T, G, PG]), ALU.add))
                for k in range(2):
                    then(dve.tensor_reduce(top[:, k, :], el[:, :, :], AX.X, ALU.max))
                    then(dve.tensor_tensor(eq[:, :, :], el[:, :, :], bc(top[:, k, :], E), ALU.is_equal))
                    then(dve.scalar_tensor_tensor(out=eq[:, :, :], in0=eq[:, :, :], scalar=-float(P),
                                                  in1=iota_bc(E), op0=ALU.mult, op1=ALU.add))
                    then(dve.tensor_reduce(eidx[:, k, :], eq[:, :, :], AX.X, ALU.min))
                    then(dve.tensor_scalar(eidx[:, k, :], eidx[:, k, :], float(P), None, ALU.add))
                    then(dve.tensor_tensor(hot[:, k, :, :], iota_bc(E), bc(eidx[:, k, :], E), ALU.is_equal))
                    if k == 0:
                        then(dve.scalar_tensor_tensor(out=el[:, :, :], in0=hot[:, 0, :, :], scalar=-2 * MAX_TOK,
                                                      in1=el[:, :, :], op0=ALU.mult, op1=ALU.add))
                then(dve.tensor_tensor(vdiff[:, :], top[:, 1, :], top[:, 0, :], ALU.subtract))
                assert done[0] == VDIFF
                then(dve.tensor_tensor(both[:, :, :], hot[:, 0, :, :], hot[:, 1, :, :], ALU.add))
                then(dve.memset(before[:, 0, :], 0.0))
                for t in range(T):
                    then(dve.tensor_tensor(before[:, t + 1, :], before[:, t, :], both[:, t, :], ALU.add))
                assert done[0] == BEFORE
                dve.wait_ge(pe_step, 2)
                then(dve.tensor_scalar(count_i[0:E, :], count_ps[0:E, :], float(P - 1), None, ALU.add))
                then(dve.tensor_scalar(nb_i[0:E, :], count_i[0:E, :], 7, None, ALU.arith_shift_right))
                then(dve.tensor_scalar(nb[0:E, :], nb_i[0:E, :], 1.0, None, ALU.max))
                assert done[0] == NBLK
                then(dve.tensor_copy(rank_i[:, :, :], rank_ps[:, :].rearrange("p (t e) -> p t e", t=T)))
                then(dve.tensor_scalar(pos_i[:, :, :], rank_i[:, :, :], P - 1, None, ALU.bitwise_and))
                then(dve.tensor_scalar(blk_i[:, :, :], rank_i[:, :, :], 7, None, ALU.arith_shift_right))
                then(dve.tensor_copy(posf[:, :, :], pos_i[:, :, :]))
                dve.wait_ge(pe_step, 3)
                then(dve.tensor_copy(start_row[:, :], start_ps[:, :]))
                then(dve.tensor_copy(starts[:, :], start_row[:, :]))
                then(dve.tensor_tensor(blkf[:, :, :], blk_i[:, :, :],
                                       start_row[:, 0:E].unsqueeze(1).to_broadcast([P, T, E]), ALU.add))
                for a, out in ((posf, pos_k), (blkf, blk_k)):
                    then(dve.tensor_tensor(prod[:, :, :, :], hot[:, :, :, :],
                                           a[:, :, :].unsqueeze(1).to_broadcast([P, 2, T, E]), ALU.mult))
                    then(dve.tensor_reduce(out[:, :, :], prod[:, :, :, :], AX.X, ALU.add))
                then(dve.scalar_tensor_tensor(out=destf[:, :, :], in0=blk_k[:, :, :], scalar=float(P),
                                              in1=pos_k[:, :, :], op0=ALU.mult, op1=ALU.add))
                then(dve.tensor_copy(dest[:, :, :], destf[:, :, :]))
                for n in range(2 * T):
                    k, t = n % 2, n // 2
                    if n >= 2:
                        dve.wait_ge(pair_used, n - 1)
                    dve.tensor_scalar(at_pos[:, n % 2, :], iota[:, :], pos_k[:, k, t:t + 1], None, ALU.is_equal)
                    dve.tensor_scalar(at_blk[:, n % 2, :], iota[:, 0:BLOCKS + 1], blk_k[:, k, t:t + 1],
                                      tok[:, t:t + 1], ALU.is_equal, ALU.mult).then_inc(pair_ready, 1)
                dve.wait_ge(act_step, 2)
                then(dve.tensor_reduce(gsum[:, :], gexp[:, :, :], AX.X, ALU.add))
                then(dve.reciprocal(ptop[:, :], gsum[:, :]))
                then(dve.tensor_scalar(vsum[:, :], vexp[:, :], 1.0, None, ALU.add))
                then(dve.reciprocal(vinv[:, :], vsum[:, :]))
                then(dve.tensor_tensor(gates[:, 0, :], ptop[:, :], vinv[:, :], ALU.mult))
                then(dve.tensor_tensor(gates[:, 1, :], gates[:, 0, :], vexp[:, :], ALU.mult))
                dve.wait_ge(pair_used, 2 * T)
                then(dve.tensor_copy(slots[:, :], slot_ps[:, :]))
FF = 512
KF = FF // P


def experts(nc, sem, n2_d, w_gate, w_up, w_down, ident_d, slots, starts, y_d):
    with ExitStack() as ctx:
        def sb(name, shape, dt=F32):
            return ctx.enter_context(nc.sbuf_tensor(name, shape, dt))

        def ps(name, shape):
            return ctx.enter_context(nc.psum_tensor(name, shape, F32))

        ident = sb("ident6", [P, P])
        wg = sb("wg", [P, 2, KD, FF])
        wu = sb("wu", [P, 2, KD, FF])
        wd = sb("wd", [P, 2, KF, D])
        idx = sb("idx6", [P, 1], I32)
        x = sb("x6", [P, D])
        xT = sb("xT6", [P, KD, P])
        act_g = sb("act_g", [P, FF])
        hid = sb("hid", [P, FF])
        hT = sb("hT", [P, KF, P])
        y = sb("y6", [P, D])
        zero = sb("zero6", [P, D])

        xT_ps = ps("xT_ps", [P, KD, P])
        g_ps = ps("g_ps", [P, FF])
        u_ps = ps("u_ps", [P, FF])
        hT_ps = ps("hT_ps", [P, KF, P])
        y_ps = ps("y_ps", [P, 2, 512])

        ident_in = sem("p6_ident_in")
        wg_in = [sem("p6_wg_in0"), sem("p6_wg_in1")]
        wu_in = [sem("p6_wu_in0"), sem("p6_wu_in1")]
        wd_in = [sem("p6_wd_in0"), sem("p6_wd_in1")]
        idx_ready = sem("p6_idx_ready")
        gathering = sem("p6_gathering")
        x_in = sem("p6_x_in")
        x_turned = sem("p6_x_turned")
        xT_ready = sem("p6_xT_ready")
        g_done = sem("p6_g_done")
        u_done = sem("p6_u_done")
        silu_ready = sem("p6_silu_ready")
        hid_ready = sem("p6_hid_ready")
        h_turned = sem("p6_h_turned")
        hT_ready = sem("p6_hT_ready")
        y_done = sem("p6_y_done")
        y_ready = sem("p6_y_ready")
        zero_ready = sem("p6_zero_ready")
        cleared = sem("p6_cleared")
        all_stored = sem("p6_all_stored")
        y_stored = sem("p6_y_stored")

        def block_count(eng):
            return eng.value_load(starts[0:1, N_EXPERTS:N_EXPERTS + 1], min_val=1, max_val=BLOCKS)

        with nc.Block() as block:
            @block.sync
            def _(sp):
                sp.dma_start(ident[:, :], ident_d).then_inc(ident_in, 16)

                def load(e, s, first):
                    one = bass.ds(e, 1)
                    if not first:
                        used = sp.value_load(starts[0:1, bass.ds(e - 1, 1)], min_val=1, max_val=BLOCKS)
                        sp.wait_ge(g_done, used)
                    sp.dma_start(wg[:, s, :, :], w_gate[one, :, :].rearrange("o (k p) n -> p (o k) n", p=P))\
                        .then_inc(wg_in[s], 16)
                    if not first:
                        sp.wait_ge(u_done, used)
                    sp.dma_start(wu[:, s, :, :], w_up[one, :, :].rearrange("o (k p) n -> p (o k) n", p=P))\
                        .then_inc(wu_in[s], 16)
                    if not first:
                        sp.wait_ge(y_done, used)
                    sp.dma_start(wd[:, s, :, :], w_down[one, :, :].rearrange("o (k p) n -> p (o k) n", p=P))\
                        .then_inc(wd_in[s], 16)

                for s in range(2):
                    load(s, s, True)
                with sp.Fori(1, N_EXPERTS // 2) as i:
                    for s in range(2):
                        load(i * 2 + s, s, False)

            @block.gpsimd
            def _(pool):
                nb = block_count(pool)
                with pool.Fori(0, nb + 1) as b:
                    pool.wait_ge(x_turned, b + 1)
                    pool.tensor_copy(idx[:, :], slots[:, bass.ds(b, 1)]).then_inc(idx_ready, 1)
                    pool.wait_ge(idx_ready, b + 1)
                    pool.sem_inc(gathering, 1)
                    pool.indirect_dma_start(x[:, :], None, n2_d, bass.IndirectOffsetOnAxis(ap=idx[:, 0:1], axis=0))\
                        .then_inc(x_in, 16)
                pool.wait_ge(x_in, (nb + 1) * 16)
                pool.sem_inc(gathering, 1)

            @block.scalar
            def _(act):
                nb = block_count(act)
                act.sem_inc(y_ready, 1)
                act.sem_inc(y_stored, 16)

                def copy_xT(b):
                    act.wait_ge(x_turned, b + 2)
                    act.copy(xT[:, :, :], xT_ps[:, :, :]).then_inc(xT_ready, 1)

                act.wait_ge(zero_ready, 1)
                with act.Fori(nb, BLOCKS + 1) as b:
                    act.dma_start(y_d[bass.ds(b * P, P), :], zero[:, :]).then_inc(cleared, 16)
                copy_xT(0)
                with act.Fori(0, nb) as b:
                    act.sem_inc(cleared, 16)
                    act.wait_ge(g_done, b + 1)
                    act.wait_ge(hid_ready, b + 1)
                    act.activation(act_g[:, :], g_ps[:, :], ACT.Silu).then_inc(silu_ready, 1)
                    copy_xT(b + 1)
                    act.wait_ge(y_done, b + 1)
                    act.wait_ge(y_stored, b * 16 + 16)
                    act.copy(y[:, 512:], y_ps[:, 1, :]).then_inc(y_ready, 1)
                    act.wait_ge(y_ready, b * 2 + 4)
                    act.dma_start(y_d[bass.ds(b * P, P), :], y[:, :]).then_inc(y_stored, 16)
                act.wait_ge(y_stored, nb * 16 + 16)
                act.sem_inc(all_stored, 1)
                act.wait_ge(cleared, 16 * (BLOCKS + 1))

            @block.vector
            def _(dve):
                nb = block_count(dve)
                dve.memset(zero[:, :], 0.0).then_inc(zero_ready, 1)
                dve.sem_inc(hid_ready, 1)
                dve.sem_inc(y_ready, 1)
                with dve.Fori(0, nb) as b:
                    dve.wait_ge(silu_ready, b + 1)
                    dve.wait_ge(u_done, b + 1)
                    dve.tensor_tensor(hid[:, :], act_g[:, :], u_ps[:, :], ALU.mult).then_inc(hid_ready, 1)
                    dve.wait_ge(h_turned, b + 1)
                    dve.tensor_copy(hT[:, :, :], hT_ps[:, :, :]).then_inc(hT_ready, 1)
                    dve.wait_ge(y_done, b + 1)
                    dve.wait_ge(y_stored, b * 16 + 16)
                    dve.tensor_copy(y[:, 0:512], y_ps[:, 0, :]).then_inc(y_ready, 1)

            @block.tensor
            def _(pe):
                def turn_x(b):
                    pe.wait_ge(x_in, b * 16 + 16)
                    for k in range(KD):
                        mm = pe.transpose(xT_ps[:, k, :], x[:, k * P:(k + 1) * P], ident[:, :])
                    mm.then_inc(x_turned, 1)

                def one_block(b, i, s):
                    pe.wait_ge(xT_ready, b + 1)
                    pe.wait_ge(hid_ready, b + 1)
                    pe.wait_ge(wg_in[s], i * 16 + 16)
                    for k in range(KD):
                        mm = pe.matmul(g_ps[:, :], xT[:, k, :], wg[:, s, k, :], start=(k == 0), stop=(k == KD - 1))
                    mm.then_inc(g_done, 1)
                    pe.wait_ge(wu_in[s], i * 16 + 16)
                    for k in range(KD):
                        mm = pe.matmul(u_ps[:, :], xT[:, k, :], wu[:, s, k, :], start=(k == 0), stop=(k == KD - 1))
                    mm.then_inc(u_done, 1)
                    turn_x(b + 1)
                    pe.wait_ge(hid_ready, b + 2)
                    for k in range(KF):
                        mm = pe.transpose(hT_ps[:, k, :], hid[:, k * P:(k + 1) * P], ident[:, :])
                    mm.then_inc(h_turned, 1)
                    pe.wait_ge(wd_in[s], i * 16 + 16)
                    pe.wait_ge(hT_ready, b + 1)
                    pe.wait_ge(y_ready, b * 2 + 2)
                    for k in range(KF):
                        for half in range(2):
                            mm = pe.matmul(y_ps[:, half, :], hT[:, k, :], wd[:, s, k, half * 512:(half + 1) * 512],
                                           start=(k == 0), stop=(k == KF - 1))
                    mm.then_inc(y_done, 1)

                pe.sem_inc(x_turned, 1)
                pe.wait_ge(ident_in, 16)
                turn_x(0)
                with pe.Fori(0, N_EXPERTS // 2) as i:
                    for s in range(2):
                        e = i * 2 + s
                        first = pe.value_load(starts[0:1, bass.ds(e, 1)], min_val=0, max_val=BLOCKS - 1)
                        last = pe.value_load(starts[0:1, bass.ds(e + 1, 1)], min_val=1, max_val=BLOCKS)
                        with pe.Fori(first, last) as b:
                            one_block(b, i, s)


def combine(nc, sem, y_d, final_g, h_sb, gates, dest, out):
    with ExitStack() as ctx:
        def sb(name, shape, dt=F32):
            return ctx.enter_context(nc.sbuf_tensor(name, shape, dt))

        g_bc = sb("gf_bc", [P, D])
        power = sb("power7", [P, 2])
        idx = sb("idx7", [P, 2, 2, 1], I32)
        gate = sb("gate7", [P, 2, 2, 1])
        y = sb("y7", [P, 2, 2, D])
        acc = sb("acc7", [P, 2, D])
        sq = sb("sq7", [P, 2, D])
        ss = sb("ss7", [P, 2])
        var = sb("var7", [P, 2])
        rstd = sb("rstd7", [P, 2])
        o = sb("o7", [P, 2, D])

        const_in = sem("p7_const_in")
        power_ready = sem("p7_power_ready")
        idx_ready = sem("p7_idx_ready")
        gathering = sem("p7_gathering")
        y_in = [sem("p7_y_in0"), sem("p7_y_in1")]
        acc_step = sem("p7_acc_step")
        ss_ready = sem("p7_ss_ready")
        var_ready = sem("p7_var_ready")
        rstd_ready = sem("p7_rstd_ready")
        o_ready = sem("p7_o_ready")
        stored = [sem("p7_stored0"), sem("p7_stored1")]

        with nc.Block() as block:
            @block.sync
            def _(sp):
                sp.dma_start(g_bc[:, :], row_broadcast(final_g, D)).then_inc(const_in, 16)

                def tile(t, s):
                    sp.wait_ge(o_ready, t + 1)
                    sp.dma_start(out[bass.ts(t, P), :], o[:, s, :]).then_inc(stored[s], 16)

                over_pairs(sp, tile)
                for s in range(2):
                    sp.wait_ge(stored[s], 8 * TILES)

            @block.gpsimd
            def _(pool):
                pool.memset(power[:, 0:1], -0.5).then_inc(power_ready, 1)
                pool.memset(power[:, 1:2], EPS).then_inc(power_ready, 1)
                pool.wait_ge(power_ready, 2)

                def gather(t, s):
                    if not (static(t) and t < 2):
                        pool.wait_ge(acc_step, t * 2 - 2)
                    one = bass.ds(t, 1)
                    pool.tensor_copy(idx[:, s, :, :], dest[:, :, one]).then_inc(idx_ready, 1)
                    pool.tensor_copy(gate[:, s, :, :], gates[:, :, one]).then_inc(idx_ready, 1)
                    pool.wait_ge(idx_ready, t * 2 + 2)
                    pool.sem_inc(gathering, 1)
                    for k in range(2):
                        pool.indirect_dma_start(y[:, s, k, :], None, y_d,
                                                bass.IndirectOffsetOnAxis(ap=idx[:, s, k, :], axis=0))\
                            .then_inc(y_in[s], 16)

                def tile(t, s):
                    if not (static(t) and t == TILES - 1):
                        gather(t + 1, 1 - s)
                    pool.wait_ge(ss_ready, t + 1)
                    pool.tensor_tensor(var[:, s:s + 1], ss[:, s:s + 1], power[:, 1:2], ALU.add).then_inc(var_ready, 1)
                    pool.wait_ge(var_ready, t + 1)
                    pool.tensor_tensor(rstd[:, s:s + 1], var[:, s:s + 1], power[:, 0:1], ALU.pow)\
                        .then_inc(rstd_ready, 1)

                gather(0, 0)
                over_pairs(pool, tile)

            @block.scalar
            def _(act):
                def tile(t, s):
                    act.wait_ge(acc_step, t * 2 + 2)
                    if not (static(t) and t < 2):
                        act.wait_ge(o_ready, t - 1)
                    act.activation(sq[:, s, :], acc[:, s, :], ACT.Square, scale=1.0 / math.sqrt(D),
                                   accum_out=ss[:, s:s + 1]).then_inc(ss_ready, 1)

                over_pairs(act, tile)

            @block.vector
            def _(dve):
                def normalize(t, s):
                    dve.wait_ge(rstd_ready, t + 1)
                    if not (static(t) and t < 2):
                        dve.wait_ge(stored[s], (t - s) * 8)
                    dve.scalar_tensor_tensor(out=o[:, s, :], in0=acc[:, s, :], scalar=rstd[:, s:s + 1],
                                             in1=g_bc[:, :], op0=ALU.mult, op1=ALU.mult).then_inc(o_ready, 1)

                def tile(t, s):
                    dve.wait_ge(y_in[s], (t - s) * 16 + 32)
                    if not (static(t) and t < 2):
                        dve.wait_ge(o_ready, t - 1)
                    h = h_sb[:, t:t + 1, :] if static(t) else h_sb[:, bass.ds(t, 1), :]
                    dve.scalar_tensor_tensor(out=acc[:, s:s + 1, :], in0=y[:, s, 0:1, :], scalar=gate[:, s, 0, :],
                                             in1=h, op0=ALU.mult, op1=ALU.add).then_inc(acc_step, 1)
                    dve.wait_ge(acc_step, t * 2 + 1)
                    dve.scalar_tensor_tensor(out=acc[:, s, :], in0=y[:, s, 1, :], scalar=gate[:, s, 1, :],
                                             in1=acc[:, s, :], op0=ALU.mult, op1=ALU.add).then_inc(acc_step, 1)
                    if not (static(t) and t == 0):
                        normalize(t - 1, 1 - s)

                dve.wait_ge(const_in, 16)
                over_pairs(dve, tile)
                normalize(TILES - 1, 1)
def build(nc, x, norm1_g, w_in, lambda_q1, lambda_k1, lambda_q2, lambda_k2, subln_g, sinks, w_out, norm2_g,
          w_router_group, b_router_group, w_router_expert, b_router_expert, w_gate, w_up, w_down, final_g,
          rope, ident, causal, band, tables, out):
    qk_d = nc.dram_tensor("qk_scratch", [QK_BLOCKS, P, SEQ], F32).ap()
    v_d = nc.dram_tensor("v_scratch", [SEQ, V_COLS], F32).ap()
    mix_d = nc.dram_tensor("mix_scratch", [KD, P, SEQ], F32).ap()
    n2_d = nc.dram_tensor("n2_scratch", [SEQ, D], F32).ap()
    y_d = nc.dram_tensor("y_scratch", [(BLOCKS + 1) * P, D], F32).ap()
    with ExitStack() as ctx:
        def sb(name, shape, dt=F32):
            return ctx.enter_context(nc.sbuf_tensor(name, shape, dt))

        def sem(name):
            return ctx.enter_context(nc.semaphore(name))

        projection(nc, sem, x, norm1_g, w_in, rope, ident, qk_d, v_d)
        diff_attention(nc, sem, qk_d, v_d, (lambda_q1, lambda_k1, lambda_q2, lambda_k2), subln_g, ident, causal, mix_d)
        window_attention(nc, sem, qk_d, v_d, sinks, ident, band, mix_d)
        h_sb = sb("h_sb", [P, TILES, D])
        logits = sb("logits", [P, TILES, LOGITS])
        gates = sb("gates", [P, 2, TILES])
        dest = sb("dest", [P, 2, TILES], I32)
        slots = sb("slots", [P, BLOCKS + 1], I32)
        starts = sb("starts", [P, N_EXPERTS + 1], I32)
        output_projection(nc, sem, x, mix_d, w_out, norm2_g, w_router_group, b_router_group, w_router_expert,
                          b_router_expert, ident, h_sb, logits, n2_d)
        routing(nc, sem, logits, tables, gates, dest, slots, starts)
        experts(nc, sem, n2_d, w_gate, w_up, w_down, ident, slots, starts, y_d)
        combine(nc, sem, y_d, final_g, h_sb, gates, dest, out)


def constants():
    inv = (1.0 / (10000.0 ** (np.arange(0, HD, 2, dtype=np.float32) / np.float32(HD)))).astype(np.float32)
    ang = np.arange(SEQ, dtype=np.float32)[:, None] * inv[None, :]
    c, s, q = np.cos(ang), np.sin(ang), np.float32(HD ** -0.5)
    rope = np.concatenate([c * q, c * q, -s * q, s * q, c, c, -s, s], axis=1).astype(np.float32)
    r = np.arange(P)
    eye = np.eye(P, dtype=np.float32)
    own = np.where(r[None, :] > r[:, None], NEG, 0.0)
    ahead = np.where(r[None, :] <= r[:, None], NEG, 0.0)
    none = np.full((P, P), NEG)
    tables = [r[:, None] < r[None, :], np.ones((P, P)), np.broadcast_to(r[None, :], (P, P)),
              r[:, None] + P * r[None, :]]
    return {
        "rope": rope,
        "ident": eye,
        "causal": np.stack([eye, own]).astype(np.float32),
        "band": np.stack([eye, none, own, ahead, own]).astype(np.float32),
        "tables": np.stack(tables).astype(np.float32),
    }


_INS = ["x", "norm1_g", "w_in", "lambda_q1", "lambda_k1", "lambda_q2", "lambda_k2", "subln_g", "sinks", "w_out",
        "norm2_g", "w_router_group", "b_router_group", "w_router_expert", "b_router_expert", "w_gate", "w_up",
        "w_down", "final_g"]


def kernel(**inputs):
    import concourse.bacc as _bacc
    from concourse.bass_utils import run_bass_kernel_spmd as _run

    nc = _bacc.Bacc("TRN2", target_bir_lowering=False, num_devices=1)
    arrays, args = {}, {}

    def declare(name, a):
        arrays[f"in_{name}"] = a
        args[name] = nc.dram_tensor(f"in_{name}", a.shape, mybir.dt.from_np(a.dtype), kind="ExternalInput").ap()

    for name in _INS:
        a = np.ascontiguousarray(inputs[name])
        declare(name, a if name == "final_g" else a[0])
    for name, a in constants().items():
        declare(name, a)
    out = nc.dram_tensor("out_0", [SEQ, D], F32, kind="ExternalOutput").ap()
    build(nc, out=out, **args)
    r = _run(nc, [arrays], core_ids=[0])
    return r.results[0]["out_0"].reshape(1, SEQ, D)
```

```python
import math
from contextlib import ExitStack

import numpy as np
import concourse.bass as bass
from concourse import mybir

F32 = mybir.dt.float32
F32R = mybir.dt.float32r
BF16 = mybir.dt.bfloat16
I32 = mybir.dt.int32
ALU = mybir.AluOpType
ACT = mybir.ActivationFunctionType
AX = mybir.AxisListType

P = 128
D = 1024
KD = D // P
SEQ = 2048
TILES = SEQ // P
HD = 64
DIFF_HEADS = 4
SWA_HEADS = 8
KV_HEADS = 2
IN_COLS = 2304
ROPE_HEADS = 26
QK_BLOCKS = ROPE_HEADS // 2
V_COLS = 640
EPS = 1e-6
NEG = -1e30


def row_broadcast(ap, width):
    return bass.AP(ap.tensor, ap.offset, [[0, P], [1, width]])


def over_pairs(eng, tile, last=TILES // 2):
    for s in range(2):
        tile(s, s)
    with eng.Fori(1, last - 1) as i:
        for s in range(2):
            tile(i * 2 + s, s)
    for s in range(2):
        tile(2 * last - 2 + s, s)


def static(t):
    return isinstance(t, int)


def split_product(pe, out, hi, lo, w_hi, w_lo, first, last):
    pe.matmul(out, hi, w_lo, start=first, stop=False)
    pe.matmul(out, lo, w_hi, start=False, stop=False)
    return pe.matmul(out, hi, w_hi, start=False, stop=last)


def split_weights(nc, sem, name, src, hi, lo, width):
    RING = 3
    K, N = hi.shape[1], hi.shape[2]
    pieces = N // width
    with ExitStack() as ctx:
        raw = ctx.enter_context(nc.sbuf_tensor(f"{name}_raw", [P, RING, K, width], F32))
        raw_in = [sem(f"{name}_raw_in{r}") for r in range(RING)]
        hi_ready = sem(f"{name}_hi_ready")
        lo_ready = sem(f"{name}_lo_ready")

        with nc.Block() as block:
            @block.sync
            def _(sp):
                for n in range(pieces):
                    if n >= RING:
                        sp.wait_ge(lo_ready, n - RING + 1)
                    sp.dma_start(raw[:, n % RING, :, :], src[:, :, n * width:(n + 1) * width])\
                        .then_inc(raw_in[n % RING], 16)

            @block.scalar
            def _(act):
                for n in range(pieces):
                    act.wait_ge(raw_in[n % RING], 16 * (n // RING + 1))
                    act.copy(hi[:, :, n * width:(n + 1) * width], raw[:, n % RING, :, :]).then_inc(hi_ready, 1)

            @block.vector
            def _(dve):
                for n in range(pieces):
                    dve.wait_ge(hi_ready, n + 1)
                    dve.tensor_tensor(lo[:, :, n * width:(n + 1) * width], raw[:, n % RING, :, :],
                                      hi[:, :, n * width:(n + 1) * width], ALU.subtract).then_inc(lo_ready, 1)


def projection(nc, sem, x, norm1_g, w_in, rope, ident_d, qk_d, v_d):
    with ExitStack() as ctx:
        def sb(name, shape, dt=F32):
            return ctx.enter_context(nc.sbuf_tensor(name, shape, dt))

        def ps(name, shape):
            return ctx.enter_context(nc.psum_tensor(name, shape, F32))

        w_hi = sb("w_in_hi", [P, KD, IN_COLS], F32R)
        w_lo = sb("w_in_lo", [P, KD, IN_COLS], F32R)
        split_weights(nc, sem, "w_in", w_in.rearrange("(k p) n -> p k n", p=P), w_hi, w_lo, 256)
        ident = sb("ident1", [P, P])
        g_bc = sb("g1_bc", [P, D])
        rope_sb = sb("rope_sb", [P, 2, 4, HD])
        x_sb = sb("x_sb", [P, 2, D])
        sq = sb("sq1", [P, D], BF16)
        ss = sb("ss1", [P, 2])
        power = sb("power1", [P, 2])
        var = sb("var1", [P, 2])
        rstd = sb("rstd1", [P, 2])
        n1T_hi = sb("n1T_hi", [P, 2, KD, P], F32R)
        n1T_lo = sb("n1T_lo", [P, 2, KD, P], F32R)
        cosx = sb("cosx", [P, 2, 8, HD])
        roped = sb("roped", [P, 2, ROPE_HEADS, HD])
        vrow = sb("vrow", [P, 2, V_COLS])
        qkT = sb("qkT", [P, 2, 2, 4, P], F32R)

        proj = ps("proj", [P, 4, 512])
        n1t_ps = ps("n1t_ps", [P, KD, P])
        qkt_ps = ps("qkt_ps", [P, 2, 4, P])

        const_in = sem("p1_const_in")
        rope_in = [sem("p1_rope_in0"), sem("p1_rope_in1")]
        x_in = [sem("p1_x_in0"), sem("p1_x_in1")]
        ss_ready = sem("p1_ss_ready")
        var_ready = sem("p1_var_ready")
        rstd_ready = sem("p1_rstd_ready")
        power_ready = sem("p1_power_ready")
        n1_ready = sem("p1_n1_ready")
        passed = sem("p1_passed")
        n1t_turned = sem("p1_n1t_turned")
        n1t_ready = sem("p1_n1t_ready")
        n1t_split = sem("p1_n1t_split")
        proj_ready = sem("p1_proj_ready")
        rope_read = sem("p1_rope_read")
        roped_ready = sem("p1_roped_ready")
        v_ready = sem("p1_v_ready")
        qkt_turned = sem("p1_qkt_turned")
        qkt_ready = sem("p1_qkt_ready")
        qkt_split = sem("p1_qkt_split")
        qk_stored = [sem("p1_qk_stored0"), sem("p1_qk_stored1")]
        v_stored = [sem("p1_v_stored0"), sem("p1_v_stored1")]

        GROUPS = [(0, 512, 0, 8, 0, 0), (512, 512, 8, 8, 2, 1), (1024, 512, None, 0, 0, 2),
                  (1536, 512, 16, 8, 0, 3), (2048, 256, 24, 2, 2, 0)]
        BATCH = [(0, 4), (4, 4), (8, 4), (12, 1)]

        with nc.Block() as block:
            @block.sync
            def _(sp):
                sp.dma_start(ident[:, :], ident_d).then_inc(const_in, 16)
                sp.dma_start(g_bc[:, :], row_broadcast(norm1_g, D)).then_inc(const_in, 16)
                for b in range(2):
                    sp.sem_inc(qk_stored[b], 32)

                def load_rope(t, s):
                    sp.dma_start(rope_sb[:, s, :, :].rearrange("p k d -> p (k d)"), rope[bass.ts(t, P), :])\
                        .then_inc(rope_in[s], 16)

                for s in range(2):
                    sp.dma_start(x_sb[:, s, :], x[s * P:(s + 1) * P, :]).then_inc(x_in[s], 16)
                    load_rope(s, s)

                def store(t, s):
                    sp.wait_ge(v_ready, t * 2 + 2)
                    sp.dma_start(v_d[bass.ts(t, P), :], vrow[:, s, :]).then_inc(v_stored[s], 16)
                    for b, (first, n) in enumerate(BATCH):
                        sp.wait_ge(qkt_split, t * 4 + (b + 1))
                        sp.sem_inc(passed, 1)
                        for part in range(2):
                            sp.dma_start(qk_d[part, first:first + n, :, bass.ts(t, P)].rearrange("b p t -> p b t"),
                                         qkT[:, b % 2, part, 0:n, :].bitcast(F32)).then_inc(qk_stored[b % 2], 16)

                def tile(t, s):
                    if not (static(t) and t >= TILES - 2):
                        sp.wait_ge(n1t_turned, t + 1)
                        sp.dma_start(x_sb[:, s, :], x[bass.ts(t + 2, P), :]).then_inc(x_in[s], 16)
                    if not (static(t) and t == 0):
                        store(t - 1, 1 - s)
                    if not (static(t) and t >= TILES - 2):
                        sp.wait_ge(rope_read, t * 4 + 4)
                        load_rope(t + 2, s)

                over_pairs(sp, tile)
                store(TILES - 1, 1)
                for s in range(2):
                    sp.wait_ge(qk_stored[s], 64 * TILES + 32)
                    sp.wait_ge(v_stored[s], 8 * TILES)

            @block.scalar
            def _(act):
                def mean_square(t, s):
                    act.wait_ge(x_in[s], (t // 2 if static(t) else (t - s) // 2) * 16 + 16)
                    if not (static(t) and t < 2):
                        act.wait_ge(n1_ready, t - 1)
                    act.activation(sq[:, :], x_sb[:, s, :], ACT.Square, scale=1.0 / math.sqrt(D),
                                   accum_out=ss[:, s:s + 1]).then_inc(ss_ready, 1)

                def copy_n1t(t, s):
                    act.wait_ge(n1t_turned, t + 1)
                    act.copy(n1T_hi[:, s, :, :], n1t_ps[:, :, :]).then_inc(n1t_ready, 1)

                def copy_qkt(t, s):
                    for b, (first, n) in enumerate(BATCH):
                        act.wait_ge(qkt_turned, t * 4 + (b + 1))
                        act.wait_ge(qk_stored[b % 2], t * 64 + (32 * (b // 2) + 32))
                        act.copy(qkT[:, b % 2, 0, 0:n, :], qkt_ps[:, b % 2, 0:n, :]).then_inc(qkt_ready, 1)

                def tile(t, s):
                    if not (static(t) and t == TILES - 1):
                        mean_square(t + 1, 1 - s)
                        copy_n1t(t + 1, 1 - s)
                    if not (static(t) and t < 2):
                        act.wait_ge(v_stored[s], (t - s) * 8)
                    act.wait_ge(proj_ready, t * 5 + 3)
                    act.copy(vrow[:, s, 0:512], proj[:, 2, :]).then_inc(v_ready, 1)
                    act.wait_ge(proj_ready, t * 5 + 5)
                    act.wait_ge(rope_read, t * 4 + 4)
                    act.copy(vrow[:, s, 512:640], proj[:, 0, 128:256]).then_inc(v_ready, 1)
                    if not (static(t) and t == 0):
                        copy_qkt(t - 1, 1 - s)

                mean_square(0, 0)
                copy_n1t(0, 0)
                over_pairs(act, tile)
                copy_qkt(TILES - 1, 1)

            @block.vector
            def _(dve):
                def normalize(t, s):
                    dve.wait_ge(rstd_ready, t + 1)
                    dve.scalar_tensor_tensor(out=x_sb[:, s, :], in0=x_sb[:, s, :], scalar=rstd[:, s:s + 1],
                                             in1=g_bc[:, :], op0=ALU.mult, op1=ALU.mult).then_inc(n1_ready, 1)

                def split_n1t(t, s):
                    dve.wait_ge(n1t_ready, t + 1)
                    dve.tensor_tensor(n1T_lo[:, s, :, :], n1t_ps[:, :, :], n1T_hi[:, s, :, :], ALU.subtract)\
                        .then_inc(n1t_split, 1)

                def split_qkt(t, s):
                    for b, (first, n) in enumerate(BATCH):
                        dve.wait_ge(qkt_ready, t * 4 + (b + 1))
                        dve.tensor_tensor(qkT[:, b % 2, 1, 0:n, :], qkt_ps[:, b % 2, 0:n, :],
                                          qkT[:, b % 2, 0, 0:n, :], ALU.subtract).then_inc(qkt_split, 1)

                def tile(t, s):
                    if not (static(t) and t == TILES - 1):
                        normalize(t + 1, 1 - s)
                    dve.wait_ge(rope_in[s], (t - s) * 8 + 16)
                    if not (static(t) and t < 2):
                        dve.wait_ge(qkt_turned, t * 4 - 4)
                    for g, (_, _, head, heads, table, bank) in enumerate(GROUPS):
                        if head is None:
                            continue
                        dve.wait_ge(proj_ready, t * 5 + (g + 1))
                        part = g - (g > 2)
                        if not (static(t) and t * 4 + part < 2):
                            dve.wait_ge(roped_ready, t * 4 + (part - 1))
                        src = proj[:, bank, 0:heads * HD].rearrange("p (h d) -> p h d", d=HD)
                        cos = rope_sb[:, s:s + 1, table, :]
                        sin = rope_sb[:, s:s + 1, table + 1, :]
                        dve.tensor_tensor(cosx[:, part % 2, 0:heads, :], src,
                                          cos.to_broadcast([P, heads, HD]), ALU.mult)
                        dve.tensor_tensor(roped[:, s, head:head + heads, 0:32], src[:, :, 32:64],
                                          sin[:, :, 0:32].to_broadcast([P, heads, 32]), ALU.mult)
                        dve.tensor_tensor(roped[:, s, head:head + heads, 32:64], src[:, :, 0:32],
                                          sin[:, :, 32:64].to_broadcast([P, heads, 32]), ALU.mult)\
                            .then_inc(rope_read, 1)
                        if g == 1 and not (static(t) and t == TILES - 1):
                            split_n1t(t + 1, 1 - s)
                    if not (static(t) and t == 0):
                        split_qkt(t - 1, 1 - s)

                dve.wait_ge(const_in, 32)
                normalize(0, 0)
                split_n1t(0, 0)
                over_pairs(dve, tile)
                split_qkt(TILES - 1, 1)

            @block.gpsimd
            def _(pool):
                def inverse_root(t, s):
                    pool.wait_ge(ss_ready, t + 1)
                    pool.tensor_tensor(var[:, s:s + 1], ss[:, s:s + 1], power[:, 1:2], ALU.add).then_inc(var_ready, 1)
                    pool.wait_ge(var_ready, t + 1)
                    if not (static(t) and t < 2):
                        pool.wait_ge(n1_ready, t - 1)
                    pool.tensor_tensor(rstd[:, s:s + 1], var[:, s:s + 1], power[:, 0:1], ALU.pow)\
                        .then_inc(rstd_ready, 1)

                def tile(t, s):
                    if not (static(t) and t == TILES - 1):
                        inverse_root(t + 1, 1 - s)
                    for n, (head, heads) in enumerate([(0, 8), (8, 8), (16, 8), (24, 2)]):
                        pool.wait_ge(rope_read, t * 4 + (n + 1))
                        pool.tensor_tensor(roped[:, s, head:head + heads, :], roped[:, s, head:head + heads, :],
                                           cosx[:, n % 2, 0:heads, :], ALU.add).then_inc(roped_ready, 1)

                pool.memset(power[:, 0:1], -0.5).then_inc(power_ready, 1)
                pool.memset(power[:, 1:2], EPS).then_inc(power_ready, 1)
                pool.wait_ge(power_ready, 2)
                inverse_root(0, 0)
                over_pairs(pool, tile)

            @block.tensor
            def _(pe):
                def turn_n1(t, s):
                    pe.wait_ge(n1_ready, t + 1)
                    for k in range(KD):
                        mm = pe.transpose(n1t_ps[:, k, :], x_sb[:, s, k * P:(k + 1) * P], ident[:, :])
                    mm.then_inc(n1t_turned, 1)

                def group(t, s, g):
                    c0, w, _, _, _, bank = GROUPS[g]
                    if g == 0:
                        pe.wait_ge(n1t_split, t + 1)
                        if not (static(t) and t == 0):
                            pe.wait_ge(rope_read, t * 4)
                            pe.wait_ge(v_ready, t * 2)
                    if g == 4:
                        pe.wait_ge(rope_read, t * 4 + 1)
                    for k in range(KD):
                        mm = split_product(pe, proj[:, bank, 0:w], n1T_hi[:, s, k, :], n1T_lo[:, s, k, :],
                                           w_hi[:, k, c0:c0 + w], w_lo[:, k, c0:c0 + w], k == 0, k == KD - 1)
                    mm.then_inc(proj_ready, 1)

                def turn_qk(t, s):
                    pe.wait_ge(roped_ready, t * 4 + 4)
                    blocks = roped[:, s, :, :].rearrange("p (b h) d -> p b (h d)", h=2)
                    for b, (first, n) in enumerate(BATCH):
                        if not (static(t) and t * 4 + b < 2):
                            pe.wait_ge(qkt_split, t * 4 + (b - 1))
                        for j in range(n):
                            mm = pe.transpose(qkt_ps[:, b % 2, j, :], blocks[:, first + j, :], ident[:, :])
                        mm.then_inc(qkt_turned, 1)

                def tile(t, s):
                    group(t, s, 0)
                    group(t, s, 1)
                    if not (static(t) and t == TILES - 1):
                        turn_n1(t + 1, 1 - s)
                    for g in (2, 3, 4):
                        group(t, s, g)
                    if not (static(t) and t == 0):
                        turn_qk(t - 1, 1 - s)

                pe.wait_ge(const_in, 32)
                turn_n1(0, 0)
                over_pairs(pe, tile)
                turn_qk(TILES - 1, 1)
def diff_attention(nc, sem, qk_d, v_d, lambdas, subln_g, ident_d, causal_d, mix_d):
    LAG = 6
    CHUNK = 512
    DV = 2 * HD
    STEPS = []
    ORDER = [(0, i) for i in range(TILES)] + [(1, i) for i in range(1, TILES)] + [(1, 0)]
    for m, (hh, i) in enumerate(ORDER):
        keys = (i + 1) * P
        piece = CHUNK if keys > CHUNK else 2 * P if i > 1 else P
        for j in range(0, keys, piece):
            STEPS.append((hh, i, j, min(piece, keys - j), m))
    N = len(STEPS)
    RUN = len(ORDER)
    NEEDS = {min(n for n in range(N) if STEPS[n][0] == hh and STEPS[n][1] * P // CHUNK >= c): (hh, c)
             for hh in range(2) for c in range(SEQ // CHUNK)}
    HEAD_END = {max(n for n in range(N) if STEPS[n][0] == hh): hh for hh in range(2)}
    FIRST = {m: min(n for n in range(N) if STEPS[n][4] == m) for m in range(RUN)}
    LAST = {m: max(n for n in range(N) if STEPS[n][4] == m) for m in range(RUN)}
    ENDS = {n: m for m, n in LAST.items()}
    RING = 7
    assert RING > LAG and N % 2 == 0
    STATS = [6 if LAST[m] > FIRST[m] else 1 for m in range(RUN)]
    STAT_END = [sum(STATS[:m + 1]) for m in range(RUN)]
    STAT_ALL = STAT_END[-1]
    LONG = [m for m in range(RUN) if LAST[m] > FIRST[m]]
    ON_ACT = [u % 8 != 5 for u in range(N)]
    COPIES = {True: sum(ON_ACT), False: N - sum(ON_ACT)}
    LAMBDA_INIT = 0.8 - 0.6 * math.exp(-0.3 * 0)

    with ExitStack() as ctx:
        def sb(name, shape, dt=F32):
            return ctx.enter_context(nc.sbuf_tensor(name, shape, dt))

        def ps(name, shape):
            return ctx.enter_context(nc.psum_tensor(name, shape, F32))

        ident = sb("ident2", [P, P])
        causal_f = sb("causal_f", [P, 2, P])
        causal = sb("causal", [P, 2, P], BF16)
        lam_in = sb("lam_in", [P, 4, HD])
        lam_prod = sb("lam_prod", [P, 2, HD])
        lam = sb("lam", [P, 6])
        g_bc = sb("subln_bc", [P, DV])
        g_out = sb("subln_out", [P, DV])
        power = sb("power2", [P, 2])
        qT = sb("qT", [P, 2, 2, SEQ], F32R)
        kT_hi = sb("kT_hi", [P, 2, 2, SEQ], F32R)
        kT_lo = sb("kT_lo", [P, 2, 2, SEQ], F32R)
        v = sb("v_sb", [P, 2, TILES, DV])
        prob = sb("prob", [P, RING, 2, CHUNK])
        nmax = sb("nmax", [P, 2, N])
        nrow = sb("nrow", [P, 2, RUN])
        part = sb("part", [P, 2, N])
        under = sb("under", [P, 2, N])
        fac = sb("fac", [P, 2, N])
        part_row = sb("part_row", [P, 2, N])
        total = sb("total", [P, 2, RUN])
        inv = sb("inv", [P, 2, RUN])
        scale = sb("scale", [P, 2, N])
        aT = sb("aT", [P, 2, CHUNK])
        osq = sb("osq", [P, 2, DV])
        oss = sb("oss", [P, 2])
        ovar = sb("ovar", [P, 2])
        orstd = sb("orstd", [P, 2])
        onorm = sb("onorm", [P, 2, DV])
        oT = sb("oT", [P, 2, P])

        score = ps("score", [P, 2, 2, CHUNK])
        aT_ps = ps("aT_ps", [P, CHUNK])
        o_ps = ps("o_ps", [P, 2, CHUNK])
        oT_ps = ps("oT_ps", [P, CHUNK])

        const_in = sem("p2_const_in")
        lam_step = sem("p2_lam_step")
        mask_ready = sem("p2_mask_ready")
        power_ready = sem("p2_power_ready")
        passed = sem("p2_passed")
        head_in = [[sem(f"p2_head_in{hh}_{c}") for c in range(SEQ // CHUNK)] for hh in range(2)]
        LOAD = 7 * 16
        head_done = sem("p2_head_done")
        score_ready = sem("p2_score_ready")
        score_free = sem("p2_score_free")
        max_ready = sem("p2_max_ready")
        fac_ready = sem("p2_fac_ready")
        stat_step = sem("p2_stat_step")
        scaled = sem("p2_scaled")
        a_ready = sem("p2_a_ready")
        a_turned = sem("p2_a_turned")
        aT_ready = {True: sem("p2_aT_by_act"), False: sem("p2_aT_by_dve")}
        pv_done = sem("p2_pv_done")
        oss_ready = sem("p2_oss_ready")
        ovar_ready = sem("p2_ovar_ready")
        orstd_ready = sem("p2_orstd_ready")
        on_ready = sem("p2_on_ready")
        o_turned = sem("p2_o_turned")
        oT_ready = sem("p2_oT_ready")
        stored = [sem("p2_stored0"), sem("p2_stored1")]

        def copied(g, u):
            if u < 0:
                return aT_ready[ON_ACT[N - 1]], g * COPIES[ON_ACT[N - 1]] + 1
            on_act = ON_ACT[u]
            return aT_ready[on_act], g * COPIES[on_act] + (1 + sum(ON_ACT[k] == on_act for k in range(u + 1)))

        def over_pairs(eng, pair):
            with eng.Fori(0, DIFF_HEADS // 2) as g:
                pair(g)

        SLOTS = N + LAG + 4

        with nc.Block() as block:
            @block.sync
            def _(sp):
                def load(h, hh):
                    for n in range(SEQ // CHUNK):
                        at = slice(n * CHUNK, (n + 1) * CHUNK)
                        for half in range(2):
                            to = slice(half * HD, (half + 1) * HD)
                            for dest, part, block in ((qT, half, h), (kT_hi, 0, DIFF_HEADS + h),
                                                      (kT_lo, 1, DIFF_HEADS + h)):
                                sp.dma_start(dest[to, hh, :, at].bitcast(F32),
                                             qk_d[part, block, :, at].rearrange("(c d) t -> d c t", d=HD))\
                                    .then_inc(head_in[hh][n], 16)
                        sp.dma_start(v[:, hh, n * (CHUNK // P):(n + 1) * (CHUNK // P), :],
                                     v_d[at, h * DV:(h + 1) * DV].rearrange("(t p) d -> p t d", p=P))\
                            .then_inc(head_in[hh][n], 16)

                sp.dma_start(causal_f[:, :, :], causal_d.rearrange("k p n -> p k n")).then_inc(const_in, 16)
                sp.dma_start(ident[:, :], ident_d).then_inc(const_in, 16)
                sp.dma_start(g_bc[:, :], row_broadcast(subln_g, DV)).then_inc(const_in, 16)
                for n, a in enumerate(lambdas):
                    sp.dma_start(lam_in[:, n, :], row_broadcast(a, HD)).then_inc(const_in, 16)
                for s in range(2):
                    sp.sem_inc(stored[s], 16)
                load(0, 0)
                load(1, 1)
                for h in range(DIFF_HEADS):
                    for m in range(TILES):
                        t = ORDER[h % 2 * TILES + m][1]
                        sp.wait_ge(oT_ready, h * TILES + m + 2)
                        sp.dma_start(mix_d[h, :, t * P:(t + 1) * P], oT[:, m % 2, :]).then_inc(stored[m % 2], 16)
                    if h + 2 < DIFF_HEADS:
                        sp.wait_ge(head_done, h + 1)
                        load(h + 2, h % 2)
                for s in range(2):
                    sp.wait_ge(stored[s], 16 + 16 * DIFF_HEADS * TILES // 2)

            @block.scalar
            def _(act):
                act.wait_ge(lam_step, 2)
                act.activation(lam[:, 2:4], lam[:, 0:2], ACT.Exp).then_inc(lam_step, 1)
                act.sem_inc(score_free, 4)
                act.sem_inc(aT_ready[True], 1)
                act.sem_inc(oT_ready, 1)

                def pair(g):
                    for n in range(SLOTS):
                        if ENDS.get(n - 1) in LONG:
                            m = ENDS[n - 1]
                            a, b = FIRST[m], LAST[m] + 1
                            act.wait_ge(stat_step, g * STAT_ALL + (STAT_END[m] - 4))
                            act.activation(fac[:, :, a:b], under[:, :, a:b], ACT.Exp).then_inc(fac_ready, 1)
                        u = n - LAG
                        if 0 <= u < N and ON_ACT[u]:
                            w = STEPS[u][3]
                            act.wait_ge(a_turned, g * N + (u + 1 + RING))
                            act.wait_ge(pv_done, g * N + (u + 1))
                            act.copy(aT[:, u % 2, 0:w], aT_ps[:, 0:w]).then_inc(aT_ready[True], 1)
                        if n < N:
                            w = STEPS[n][3]
                            act.wait_ge(max_ready, g * N + (n + 1))
                            act.wait_ge(a_turned, g * N + max(n + 1, RING))
                            for c in range(2):
                                act.activation(prob[:, n % RING, c, 0:w], score[:, n % 2, c, 0:w], ACT.Exp,
                                               bias=nmax[:, c, n:n + 1], accum_out=part[:, c, n:n + 1])\
                                    .then_inc(score_free, 1)
                        if n - LAG - 2 in ENDS:
                            m = ENDS[n - LAG - 2]
                            act.wait_ge(pv_done, g * N + (LAST[m] + 3))
                            act.wait_ge(on_ready, g * RUN + (m + 1))
                            act.activation(osq[:, m % 2, :], o_ps[:, m % 2, 0:DV], ACT.Square, scale=1.0 / math.sqrt(DV),
                                           accum_out=oss[:, m % 2:m % 2 + 1]).then_inc(oss_ready, 1)
                        if n - LAG - 4 in ENDS:
                            m = ENDS[n - LAG - 4]
                            act.wait_ge(o_turned, g * RUN + (m + 3))
                            act.wait_ge(stored[m % 2], g * (8 * RUN) + 16 * (m // 2 + 1))
                            act.copy(oT[:, m % 2, :], oT_ps[:, 0:P]).then_inc(oT_ready, 1)

                over_pairs(act, pair)

            @block.gpsimd
            def _(pool):
                pool.memset(power[:, 0:1], -0.5).then_inc(power_ready, 1)
                pool.memset(power[:, 1:2], EPS).then_inc(power_ready, 1)
                pool.wait_ge(power_ready, 2)
                pool.wait_ge(lam_step, 5)

                def pair(g):
                    for n in range(SLOTS):
                        u = n - (LAG - 2)
                        if 0 <= u < N:
                            w, m = STEPS[u][3], STEPS[u][4]
                            pool.wait_ge(stat_step, g * STAT_ALL + STAT_END[m])
                            pool.sem_inc(passed, 1)
                            pool.tensor_scalar(prob[:, u % RING, 1, 0:w], prob[:, u % RING, 1, 0:w],
                                               scale[:, 1, u:u + 1], lam[:, 5:6], ALU.mult, ALU.mult)\
                                .then_inc(scaled, 1)
                        if n - LAG - 2 in ENDS:
                            m = ENDS[n - LAG - 2]
                            s = m % 2
                            pool.wait_ge(oss_ready, g * RUN + (m + 1))
                            pool.tensor_tensor(ovar[:, s:s + 1], oss[:, s:s + 1], power[:, 1:2], ALU.add)\
                                .then_inc(ovar_ready, 1)
                            pool.wait_ge(ovar_ready, g * RUN + (m + 1))
                            pool.tensor_tensor(orstd[:, s:s + 1], ovar[:, s:s + 1], power[:, 0:1], ALU.pow)\
                                .then_inc(orstd_ready, 1)

                over_pairs(pool, pair)

            @block.vector
            def _(dve):
                dve.wait_ge(const_in, 16 * 7)
                dve.tensor_copy(causal[:, :, :], causal_f[:, :, :]).then_inc(mask_ready, 1)
                dve.tensor_scalar(g_out[:, :], g_bc[:, :], 1.0 - LAMBDA_INIT, None, ALU.mult).then_inc(mask_ready, 1)
                pairs = lam_in[:, :, :].rearrange("p (a b) d -> p a b d", b=2)
                dve.tensor_tensor(lam_prod[:, :, :], pairs[:, :, 0, :], pairs[:, :, 1, :], ALU.mult)\
                    .then_inc(lam_step, 1)
                dve.wait_ge(lam_step, 1)
                dve.tensor_reduce(lam[:, 0:2], lam_prod[:, :, :], AX.X, ALU.add).then_inc(lam_step, 1)
                dve.wait_ge(lam_step, 3)
                dve.tensor_tensor(lam[:, 4:5], lam[:, 2:3], lam[:, 3:4], ALU.subtract).then_inc(lam_step, 1)
                dve.wait_ge(lam_step, 4)
                dve.tensor_scalar(lam[:, 5:6], lam[:, 4:5], -1.0, -LAMBDA_INIT, ALU.mult, ALU.add)\
                    .then_inc(lam_step, 1)
                dve.wait_ge(lam_step, 5)
                dve.wait_ge(mask_ready, 2)
                dve.sem_inc(aT_ready[False], 1)
                dve.sem_inc(on_ready, 2)

                def pair(g):
                    for n in range(SLOTS):
                        if ENDS.get(n - 1) in LONG:
                            m = ENDS[n - 1]
                            dve.wait_ge(max_ready, g * N + n)
                            dve.tensor_reduce(nrow[:, :, m:m + 1], nmax[:, :, FIRST[m]:n], AX.X, ALU.min)\
                                .then_inc(stat_step, 1)
                            dve.wait_ge(stat_step, g * STAT_ALL + (STAT_END[m] - 5))
                            dve.tensor_tensor(under[:, :, FIRST[m]:n],
                                              nrow[:, :, m:m + 1].to_broadcast([P, 2, n - FIRST[m]]),
                                              nmax[:, :, FIRST[m]:n], ALU.subtract).then_inc(stat_step, 1)
                        u = n - LAG
                        if 0 <= u < N and not ON_ACT[u]:
                            w = STEPS[u][3]
                            dve.wait_ge(a_turned, g * N + (u + 1 + RING))
                            dve.wait_ge(pv_done, g * N + (u + 1))
                            dve.tensor_copy(aT[:, u % 2, 0:w], aT_ps[:, 0:w]).then_inc(aT_ready[False], 1)
                        u = n - (LAG - 1)
                        if 0 <= u < N:
                            w = STEPS[u][3]
                            dve.wait_ge(scaled, g * N + (u + 1))
                            dve.scalar_tensor_tensor(out=prob[:, u % RING, 0, 0:w], in0=prob[:, u % RING, 0, 0:w],
                                                     scalar=scale[:, 0, u:u + 1],
                                                     in1=prob[:, u % RING, 1, 0:w],
                                                     op0=ALU.mult, op1=ALU.add).then_inc(a_ready, 1)
                        if n < N:
                            w = STEPS[n][3]
                            dve.wait_ge(score_ready, g * N + (n + 1))
                            dve.tensor_reduce(nmax[:, :, n:n + 1], score[:, n % 2, :, 0:w], AX.X, ALU.max,
                                              negate=True).then_inc(max_ready, 1)
                        if n - LAG - 3 in ENDS:
                            m = ENDS[n - LAG - 3]
                            dve.wait_ge(orstd_ready, g * RUN + (m + 1))
                            dve.wait_ge(o_turned, g * RUN + (m + 1))
                            dve.scalar_tensor_tensor(out=onorm[:, m % 2, :], in0=o_ps[:, m % 2, 0:DV],
                                                     scalar=orstd[:, m % 2:m % 2 + 1], in1=g_out[:, :],
                                                     op0=ALU.mult, op1=ALU.mult).then_inc(on_ready, 1)
                        if ENDS.get(n - 1) in LONG:
                            m = ENDS[n - 1]
                            a, b = FIRST[m], LAST[m] + 1
                            end = g * STAT_ALL + STAT_END[m]
                            dve.wait_ge(fac_ready, g * len(LONG) + (LONG.index(m) + 1))
                            dve.wait_ge(score_free, g * (2 * N) + (2 * n + 4))
                            dve.tensor_tensor(part_row[:, :, a:b], part[:, :, a:b], fac[:, :, a:b],
                                              ALU.mult).then_inc(stat_step, 1)
                            dve.wait_ge(stat_step, end - 3)
                            dve.tensor_reduce(total[:, :, m:m + 1], part_row[:, :, a:b], AX.X, ALU.add)\
                                .then_inc(stat_step, 1)
                            dve.wait_ge(stat_step, end - 2)
                            dve.reciprocal(inv[:, :, m:m + 1], total[:, :, m:m + 1]).then_inc(stat_step, 1)
                            dve.wait_ge(stat_step, end - 1)
                            dve.tensor_tensor(scale[:, :, a:b], fac[:, :, a:b],
                                              inv[:, :, m:m + 1].to_broadcast([P, 2, b - a]), ALU.mult)\
                                .then_inc(stat_step, 1)
                        elif n - 1 in ENDS:
                            dve.wait_ge(score_free, g * (2 * N) + (2 * n + 4))
                            dve.reciprocal(scale[:, :, n - 1:n], part[:, :, n - 1:n]).then_inc(stat_step, 1)

                over_pairs(dve, pair)

            @block.tensor
            def _(pe):
                pe.sem_inc(a_turned, RING)
                pe.sem_inc(pv_done, 2)
                pe.sem_inc(o_turned, 2)
                pe.wait_ge(const_in, 16 * 7)
                pe.wait_ge(mask_ready, 2)

                def pair(g):
                    for n in range(SLOTS):
                        if n < N:
                            hh, i, j, w, m = STEPS[n]
                            if n in NEEDS:
                                pe.wait_ge(head_in[hh][NEEDS[n][1]], g * LOAD + LOAD)
                            pe.wait_ge(score_free, g * (2 * N) + (2 * n + 2))
                            diagonal = j + w == (i + 1) * P
                            for c in range(2):
                                q = qT[:, hh, c, i * P:(i + 1) * P]
                                pe.matmul(score[:, n % 2, c, 0:w], q, kT_lo[:, hh, c, j:j + w],
                                          start=True, stop=False)
                                mm = pe.matmul(score[:, n % 2, c, 0:w], q, kT_hi[:, hh, c, j:j + w],
                                               start=False, stop=not diagonal)
                            if diagonal:
                                for c in range(2):
                                    mm = pe.matmul(score[:, n % 2, c, w - P:w], causal[:, 0, :], causal[:, 1, :],
                                                   start=False, stop=True)
                            mm.then_inc(score_ready, 1)
                        u = n - LAG
                        if 0 <= u < N:
                            pe.wait_ge(a_ready, g * N + (u + 1))
                            pe.wait_ge(*copied(g, u - 1))
                            for b in range(STEPS[u][3] // P):
                                mm = pe.transpose(aT_ps[:, b * P:(b + 1) * P],
                                                  prob[:, u % RING, 0, b * P:(b + 1) * P], ident[:, :])
                            mm.then_inc(a_turned, 1)
                        if n - LAG - 4 in ENDS:
                            m = ENDS[n - LAG - 4]
                            pe.wait_ge(on_ready, g * RUN + (m + 3))
                            pe.wait_ge(oT_ready, g * RUN + (m + 1))
                            pe.transpose(oT_ps[:, 0:P], onorm[:, m % 2, :], ident[:, :]).then_inc(o_turned, 1)
                        u = n - LAG - 1
                        if 0 <= u < N:
                            hh, i, j, w, m = STEPS[u]
                            if u == FIRST[m]:
                                pe.wait_ge(on_ready, g * RUN + (m + 1))
                            pe.wait_ge(*copied(g, u))
                            for b in range(w // P):
                                mm = pe.matmul(o_ps[:, m % 2, 0:DV], aT[:, u % 2, b * P:(b + 1) * P],
                                               v[:, hh, j // P + b, :], start=(u == FIRST[m] and b == 0),
                                               stop=(u == LAST[m] and b == w // P - 1))
                            mm.then_inc(pv_done, 1)
                            if u in HEAD_END:
                                pe.sem_inc(head_done, 1)

                over_pairs(pe, pair)
def window_attention(nc, sem, qk_d, v_d, sinks, ident_d, band_d, mix_d):
    GROUP = SWA_HEADS // KV_HEADS
    WIN = 2 * P
    Q0, K0, V0 = 2 * DIFF_HEADS, 2 * DIFF_HEADS + SWA_HEADS // 2, DIFF_HEADS * 2 * HD

    with ExitStack() as ctx:
        def sb(name, shape, dt=F32):
            return ctx.enter_context(nc.sbuf_tensor(name, shape, dt))

        def ps(name, shape):
            return ctx.enter_context(nc.psum_tensor(name, shape, F32))

        ident = sb("ident3", [P, P])
        band_f = sb("band_f", [P, 5, P])
        band = sb("band", [P, 5, P], BF16)
        sink = sb("sink", [P, SWA_HEADS])
        nsink = sb("nsink", [P, SWA_HEADS])
        k_hi = sb("k_hi", [P, KV_HEADS, P + SEQ], F32R)
        k_lo = sb("k_lo", [P, KV_HEADS, P + SEQ], F32R)
        v = sb("v_swa", [P, TILES + 1, KV_HEADS * HD])
        q = sb("q_swa", [P, 2, SWA_HEADS, P], F32R)
        prob = sb("prob_swa", [P, 2, GROUP, WIN])
        nmax = sb("nmax_swa", [P, 2, GROUP])
        nrow = sb("nrow_swa", [P, 2, GROUP])
        part = sb("part_swa", [P, 2, GROUP])
        over = sb("over_swa", [P, 2, GROUP])
        esink = sb("esink", [P, 2, GROUP])
        total = sb("total_swa", [P, 2, GROUP])
        inv = sb("inv_swa", [P, 2, GROUP])
        pT = sb("pT_swa", [P, 2, GROUP, WIN])
        o = sb("o_swa", [P, 2, SWA_HEADS * HD])
        oT = sb("oT_swa", [P, 2, SWA_HEADS // 2, P])

        score = ps("score_swa", [P, 2, GROUP, WIN])
        pT_ps = ps("pT_ps_swa", [P, GROUP, WIN])
        o_ps = ps("o_ps_swa", [P, 512])
        oT_ps = ps("oT_ps_swa", [P, SWA_HEADS // 2, P])

        const_in = sem("p3_const_in")
        mask_ready = sem("p3_mask_ready")
        kv_in = sem("p3_kv_in")
        q_in = [sem("p3_q_in0"), sem("p3_q_in1")]
        score_ready = sem("p3_score_ready")
        score_free = sem("p3_score_free")
        nmax_ready = sem("p3_nmax_ready")
        nrow_ready = sem("p3_nrow_ready")
        exp_ready = sem("p3_exp_ready")
        total_ready = sem("p3_total_ready")
        inv_ready = sem("p3_inv_ready")
        p_turned = sem("p3_p_turned")
        pT_ready = sem("p3_pT_ready")
        pv_done = sem("p3_pv_done")
        o_ready = sem("p3_o_ready")
        o_turned = sem("p3_o_turned")
        oT_ready = sem("p3_oT_ready")
        stored = [sem("p3_stored0"), sem("p3_stored1")]

        def tile_pairs(eng, tile):
            for s in range(2):
                tile(s, s)
            with eng.Fori(1, TILES // 2) as i:
                for s in range(2):
                    tile(i * 2 + s, s)

        with nc.Block() as block:
            @block.sync
            def _(sp):
                for s in range(2):
                    sp.sem_inc(stored[s], 16)
                sp.dma_start(band_f[:, :, :], band_d.rearrange("k p n -> p k n")).then_inc(const_in, 16)
                sp.dma_start(ident[:, :], ident_d).then_inc(const_in, 16)
                sp.dma_start(sink[:, :], row_broadcast(sinks, SWA_HEADS)).then_inc(const_in, 16)

                def load(t, s):
                    for half in range(2):
                        sp.dma_start(q[half * HD:(half + 1) * HD, s, :, :].bitcast(F32),
                                     qk_d[half, Q0:Q0 + SWA_HEADS // 2, :, bass.ts(t, P)]
                                     .rearrange("b (h d) t -> d (b h) t", d=HD)).then_inc(q_in[s], 16)

                load(0, 0)
                for half in range(2):
                    to = slice(half * HD, (half + 1) * HD)
                    for part, k in ((0, k_hi), (1, k_lo)):
                        sp.dma_start(k[to, :, P:].bitcast(F32),
                                     qk_d[part, K0, :, :].rearrange("(g d) t -> d g t", d=HD)).then_inc(kv_in, 16)
                sp.dma_start(v[:, 1:, :], v_d[:, V0:V0 + KV_HEADS * HD].rearrange("(t p) d -> p t d", p=P))\
                    .then_inc(kv_in, 16)
                load(1, 1)

                def store(t, s):
                    sp.wait_ge(oT_ready, t + 1)
                    sp.dma_start(mix_d[DIFF_HEADS:, :, bass.ts(t, P)].rearrange("b p t -> p b t"), oT[:, s, :, :])\
                        .then_inc(stored[s], 16)

                def tile(t, s):
                    if not (static(t) and t < 2):
                        sp.wait_ge(score_ready, t * 2 - 2)
                        load(t, s)
                        store(t - 2, s)

                tile_pairs(sp, tile)
                for s in range(2):
                    store(TILES - 2 + s, s)
                for s in range(2):
                    sp.wait_ge(stored[s], 16 + 16 * TILES // 2)

            @block.vector
            def _(dve):
                dve.memset(k_hi[:, :, 0:P].bitcast(F32), 0.0)
                dve.memset(k_lo[:, :, 0:P].bitcast(F32), 0.0)
                dve.memset(v[:, 0, :], 0.0).then_inc(mask_ready, 1)
                dve.wait_ge(const_in, 16 * 3)
                dve.tensor_copy(band[:, :, :], band_f[:, :, :]).then_inc(mask_ready, 1)
                dve.tensor_scalar(nsink[:, :], sink[:, :], -1.0, None, ALU.mult).then_inc(mask_ready, 1)
                dve.wait_ge(mask_ready, 3)
                dve.sem_inc(pT_ready, 1)
                dve.sem_inc(o_ready, 1)

                def finish(t, g):
                    step, b = t * 2 + g, g
                    dve.wait_ge(p_turned, step + 1)
                    dve.tensor_copy(pT[:, b, 0:2, :], pT_ps[:, 0:2, :]).then_inc(pT_ready, 1)
                    dve.wait_ge(exp_ready, step + 1)
                    dve.tensor_tensor(total[:, b, :], part[:, b, :], esink[:, b, :], ALU.add)\
                        .then_inc(total_ready, 1)
                    dve.wait_ge(total_ready, step + 1)
                    dve.reciprocal(inv[:, b, :], total[:, b, :]).then_inc(inv_ready, 1)
                    dve.wait_ge(inv_ready, step + 1)

                def output(t, g, s):
                    step = t * 2 + g
                    dve.wait_ge(pv_done, step + 1)
                    dve.wait_ge(o_turned, t + 1)
                    dve.tensor_tensor(
                        o[:, s, g * GROUP * HD:(g + 1) * GROUP * HD].rearrange("p (h d) -> p h d", d=HD),
                        o_ps[:, 0:GROUP * HD].rearrange("p (h d) -> p h d", d=HD),
                        inv[:, g, :].unsqueeze(2).to_broadcast([P, GROUP, HD]), ALU.mult).then_inc(o_ready, 1)

                def tile(t, s):
                    for g in range(KV_HEADS):
                        step = t * 2 + g
                        heads = slice(g * GROUP, (g + 1) * GROUP)
                        dve.wait_ge(score_ready, step + 1)
                        dve.tensor_reduce(nmax[:, g, :], score[:, g, :, :], AX.X, ALU.max, negate=True)\
                            .then_inc(nmax_ready, 1)
                        dve.wait_ge(nmax_ready, step + 1)
                        dve.tensor_tensor(nrow[:, g, :], nmax[:, g, :], nsink[:, heads], ALU.min)\
                            .then_inc(nrow_ready, 1)
                        dve.wait_ge(nrow_ready, step * 2 + 1)
                        dve.tensor_tensor(over[:, g, :], nrow[:, g, :], sink[:, heads], ALU.add)\
                            .then_inc(nrow_ready, 1)
                        if not (static(t) and t == 0 and g == 0):
                            finish(*((t, 0) if g else (t - 1, 1)))
                        if not (static(t) and t == 0):
                            output(t - 1, g, 1 - s)

                tile_pairs(dve, tile)
                finish(TILES - 1, 1)
                for g in range(KV_HEADS):
                    output(TILES - 1, g, 1)

            @block.scalar
            def _(act):
                act.sem_inc(score_free, 2 * GROUP)
                act.sem_inc(pT_ready, 1)

                def copy_pT(t, g):
                    step = t * 2 + g
                    act.wait_ge(p_turned, step + 1)
                    act.copy(pT[:, g, 2:4, :], pT_ps[:, 2:4, :]).then_inc(pT_ready, 1)

                def copy_oT(t, s):
                    act.wait_ge(o_turned, t + 3)
                    act.wait_ge(stored[s], (t - s) * 8 + 16)
                    act.copy(oT[:, s, :, :], oT_ps[:, :, :]).then_inc(oT_ready, 1)

                def tile(t, s):
                    for g in range(KV_HEADS):
                        step = t * 2 + g
                        if not (static(t) and t == 0 and g == 0):
                            pt, pg = (t, 0) if g else (t - 1, 1)
                            copy_pT(pt, pg)
                        act.wait_ge(nrow_ready, step * 2 + 2)
                        if not (static(t) and t == 0):
                            act.wait_ge(p_turned, step - 1)
                            act.wait_ge(total_ready, step - 1)
                        for hd in range(GROUP):
                            act.activation(prob[:, g, hd, :], score[:, g, hd, :], ACT.Exp,
                                               bias=nrow[:, g, hd:hd + 1], accum_out=part[:, g, hd:hd + 1])\
                                .then_inc(score_free, 1)
                        act.activation(esink[:, g, :], over[:, g, :], ACT.Exp).then_inc(exp_ready, 1)
                        if g == 0 and not (static(t) and t < 2):
                            copy_oT(t - 2, s)

                tile_pairs(act, tile)
                copy_pT(TILES - 1, 1)
                copy_oT(TILES - 2, 0)
                copy_oT(TILES - 1, 1)

            @block.tensor
            def _(pe):
                pe.sem_inc(o_turned, 2)
                pe.wait_ge(const_in, 16 * 3)
                pe.wait_ge(mask_ready, 3)
                pe.wait_ge(kv_in, 16 * 5)

                def turn_p(t, g):
                    step = t * 2 + g
                    pe.wait_ge(score_free, (step + 3) * GROUP)
                    pe.wait_ge(pT_ready, step * 2 + 2)
                    for hd in range(GROUP):
                        for b in range(2):
                            mm = pe.transpose(pT_ps[:, hd, b * P:(b + 1) * P], prob[:, g, hd, b * P:(b + 1) * P],
                                              ident[:, :])
                    mm.then_inc(p_turned, 1)

                def times_v(t, g):
                    step = t * 2 + g
                    pe.wait_ge(pT_ready, step * 2 + 4)
                    pe.wait_ge(o_ready, step + 1)
                    for hd in range(GROUP):
                        for b in range(2):
                            vv = v[:, bass.ds(t + b, 1), g * HD:(g + 1) * HD]
                            mm = pe.matmul(o_ps[:, hd * HD:(hd + 1) * HD], pT[:, g, hd, b * P:(b + 1) * P], vv,
                                           start=(b == 0), stop=(b == 1))
                    mm.then_inc(pv_done, 1)

                def turn_o(t, s):
                    pe.wait_ge(o_ready, t * 2 + 3)
                    if not (static(t) and t == 0):
                        pe.wait_ge(oT_ready, t)
                    for b in range(SWA_HEADS // 2):
                        mm = pe.transpose(oT_ps[:, b, :], o[:, s, b * P:(b + 1) * P], ident[:, :])
                    mm.then_inc(o_turned, 1)

                def tile(t, s):
                    for g in range(KV_HEADS):
                        step = t * 2 + g
                        if g == 0:
                            pe.wait_ge(q_in[s], (t - s) * 16 + 32)
                            if not (static(t) and t < 2):
                                turn_o(t - 2, s)
                        pe.wait_ge(score_free, (step + 1) * GROUP)
                        for hd in range(GROUP):
                            for k in (k_lo, k_hi):
                                pe.matmul(score[:, g, hd, :], q[:, s, g * GROUP + hd, :], k[:, g, bass.ds(t * P, WIN)],
                                          start=(k is k_lo), stop=False)
                            mask = band[:, 1:3, :] if static(t) and t == 0 else band[:, 3:5, :]
                            mm = pe.matmul(score[:, g, hd, :], band[:, 0, :], mask, start=False, stop=True)
                        mm.then_inc(score_ready, 1)
                        if not (static(t) and t == 0 and g == 0):
                            turn_p(*((t, 0) if g else (t - 1, 1)))
                        if not (static(t) and t == 0):
                            times_v(t - 1, g)

                tile_pairs(pe, tile)
                turn_p(TILES - 1, 1)
                times_v(TILES - 1, 0)
                times_v(TILES - 1, 1)
                turn_o(TILES - 2, 0)
                turn_o(TILES - 1, 1)
N_GROUPS = 4
N_EXPERTS = 32
PER_GROUP = N_EXPERTS // N_GROUPS
LOGITS = N_GROUPS + N_EXPERTS


def output_projection(nc, sem, x, mix_d, w_out, norm2_g, w_rg, b_rg, w_re, b_re, ident_d, h_sb, logits, n2_d):
    with ExitStack() as ctx:
        def sb(name, shape, dt=F32):
            return ctx.enter_context(nc.sbuf_tensor(name, shape, dt))

        def ps(name, shape):
            return ctx.enter_context(nc.psum_tensor(name, shape, F32))

        ident = sb("ident4", [P, P])
        w_sb = sb("w_out_sb", [P, KD, D])
        wr_sb = sb("w_router_sb", [P, KD, LOGITS])
        br_sb = sb("b_router_sb", [P, LOGITS])
        g_bc = sb("g2_bc", [P, D])
        power = sb("power4", [P, 2])
        mixT = sb("mixT", [P, 2, KD, P])
        x_sb = sb("x4_sb", [P, 2, D])
        sq = sb("sq4", [P, 2, D])
        ss = sb("ss4", [P, 2])
        var = sb("var4", [P, 2])
        rstd = sb("rstd4", [P, 2])
        n2 = sb("n2", [P, 2, D])
        n2T = sb("n2T", [P, 2, KD, P])

        proj = ps("proj4", [P, 2, 2, 512])
        n2t_ps = ps("n2t_ps", [P, KD, P])
        lg_ps = ps("lg_ps", [P, LOGITS])

        const_in = sem("p4_const_in")
        power_ready = sem("p4_power_ready")
        w_in_s = [sem(f"p4_w_in{k}") for k in range(2)]
        tile_in = [sem("p4_tile_in0"), sem("p4_tile_in1")]
        proj_ready = sem("p4_proj_ready")
        h_ready = sem("p4_h_ready")
        ss_ready = sem("p4_ss_ready")
        var_ready = sem("p4_var_ready")
        rstd_ready = sem("p4_rstd_ready")
        n2_ready = sem("p4_n2_ready")
        n2_turned = sem("p4_n2_turned")
        n2T_ready = sem("p4_n2T_ready")
        lg_ready = sem("p4_lg_ready")
        lg_done = sem("p4_lg_done")
        stored = [sem("p4_stored0"), sem("p4_stored1")]

        with nc.Block() as block:
            @block.sync
            def _(sp):
                def load(t, s):
                    sp.dma_start(mixT[:, s, :, :], mix_d[:, :, bass.ts(t, P)].rearrange("b p t -> p b t"))\
                        .then_inc(tile_in[s], 16)
                    sp.dma_start(x_sb[:, s, :], x[bass.ts(t, P), :]).then_inc(tile_in[s], 16)

                load(0, 0)
                wv = w_out.rearrange("(k p) n -> p k n", p=P)
                for k in range(2):
                    sp.dma_start(w_sb[:, k * 4:k * 4 + 4, :], wv[:, k * 4:k * 4 + 4, :]).then_inc(w_in_s[k], 16)
                load(1, 1)
                sp.dma_start(ident[:, :], ident_d).then_inc(const_in, 16)
                sp.dma_start(g_bc[:, :], row_broadcast(norm2_g, D)).then_inc(const_in, 16)
                sp.dma_start(wr_sb[:, :, 0:N_GROUPS], w_rg.rearrange("(k p) n -> p k n", p=P)).then_inc(const_in, 16)
                sp.dma_start(wr_sb[:, :, N_GROUPS:], w_re.rearrange("(k p) n -> p k n", p=P)).then_inc(const_in, 16)
                sp.dma_start(br_sb[:, 0:N_GROUPS], row_broadcast(b_rg, N_GROUPS)).then_inc(const_in, 16)
                sp.dma_start(br_sb[:, N_GROUPS:], row_broadcast(b_re, N_EXPERTS)).then_inc(const_in, 16)

                def store(t, s):
                    sp.wait_ge(n2_ready, t + 1)
                    sp.dma_start(n2_d[bass.ts(t, P), :], n2[:, s, :]).then_inc(stored[s], 16)

                def tile(t, s):
                    if not (static(t) and t >= TILES - 2):
                        sp.wait_ge(h_ready, t + 1)
                        load(t + 2, s)
                    store(t, s)

                over_pairs(sp, tile)
                for s in range(2):
                    sp.wait_ge(stored[s], 8 * TILES)

            @block.vector
            def _(dve):
                def residual(t, s):
                    dve.wait_ge(proj_ready, t + 1)
                    h = h_sb[:, t:t + 1, :] if static(t) else h_sb[:, bass.ds(t, 1), :]
                    dve.tensor_tensor(h, proj[:, s, :, :].rearrange("p (o a) b -> p o (a b)", o=1),
                                      x_sb[:, s:s + 1, :], ALU.add).then_inc(h_ready, 1)

                def normalize(t, s):
                    dve.wait_ge(rstd_ready, t + 1)
                    if not (static(t) and t < 2):
                        dve.wait_ge(n2_turned, t - 1)
                        dve.wait_ge(stored[s], (t - s) * 8)
                    h = h_sb[:, t:t + 1, :] if static(t) else h_sb[:, bass.ds(t, 1), :]
                    dve.scalar_tensor_tensor(out=n2[:, s:s + 1, :], in0=h, scalar=rstd[:, s:s + 1],
                                             in1=g_bc[:, :].rearrange("p (o a) -> p o a", o=1),
                                             op0=ALU.mult, op1=ALU.mult).then_inc(n2_ready, 1)

                def take_logits(t, s):
                    dve.wait_ge(lg_ready, t + 1)
                    out = logits[:, t:t + 1, :] if static(t) else logits[:, bass.ds(t, 1), :]
                    dve.tensor_tensor(out, lg_ps[:, :].rearrange("p (o a) -> p o a", o=1),
                                      br_sb[:, :].rearrange("p (o a) -> p o a", o=1), ALU.add).then_inc(lg_done, 1)

                def tile(t, s):
                    residual(t, s)
                    if static(t) and t == 0:
                        dve.wait_ge(const_in, 96)
                    dve.wait_ge(h_ready, t + 1)
                    normalize(t, s)
                    if not (static(t) and t == 0):
                        take_logits(t - 1, 1 - s)

                over_pairs(dve, tile)
                take_logits(TILES - 1, 1)

            @block.scalar
            def _(act):
                def tile(t, s):
                    act.wait_ge(h_ready, t + 1)
                    if not (static(t) and t < 2):
                        act.wait_ge(n2_ready, t - 1)
                    h = h_sb[:, t:t + 1, :] if static(t) else h_sb[:, bass.ds(t, 1), :]
                    act.activation(sq[:, s:s + 1, :], h, ACT.Square, scale=1.0 / math.sqrt(D),
                                   accum_out=ss[:, s:s + 1]).then_inc(ss_ready, 1)
                    act.wait_ge(n2_turned, t + 1)
                    act.copy(n2T[:, s, :, :], n2t_ps[:, :, :]).then_inc(n2T_ready, 1)

                over_pairs(act, tile)

            @block.gpsimd
            def _(pool):
                pool.memset(power[:, 0:1], -0.5).then_inc(power_ready, 1)
                pool.memset(power[:, 1:2], EPS).then_inc(power_ready, 1)
                pool.wait_ge(power_ready, 2)

                def tile(t, s):
                    pool.wait_ge(ss_ready, t + 1)
                    pool.tensor_tensor(var[:, s:s + 1], ss[:, s:s + 1], power[:, 1:2], ALU.add).then_inc(var_ready, 1)
                    pool.wait_ge(var_ready, t + 1)
                    pool.tensor_tensor(rstd[:, s:s + 1], var[:, s:s + 1], power[:, 0:1], ALU.pow)\
                        .then_inc(rstd_ready, 1)

                over_pairs(pool, tile)

            @block.tensor
            def _(pe):
                def project(t, s):
                    pe.wait_ge(tile_in[s], (t - s) * 16 + 32)
                    if not (static(t) and t < 2):
                        pe.wait_ge(h_ready, t - 1)
                    for k in range(KD):
                        if static(t) and t == 0 and k % 4 == 0:
                            pe.wait_ge(w_in_s[k // 4], 16)
                        for half in range(2):
                            mm = pe.matmul(proj[:, s, half, :], mixT[:, s, k, :],
                                           w_sb[:, k, half * 512:(half + 1) * 512], start=(k == 0), stop=(k == KD - 1))
                    mm.then_inc(proj_ready, 1)

                def turn(t, s):
                    pe.wait_ge(n2_ready, t + 1)
                    if not (static(t) and t == 0):
                        pe.wait_ge(n2T_ready, t)
                    for k in range(KD):
                        mm = pe.transpose(n2t_ps[:, k, :], n2[:, s, k * P:(k + 1) * P], ident[:, :])
                    mm.then_inc(n2_turned, 1)

                def route(t, s):
                    pe.wait_ge(n2T_ready, t + 1)
                    if not (static(t) and t == 0):
                        pe.wait_ge(lg_done, t)
                    for k in range(KD):
                        mm = pe.matmul(lg_ps[:, :], n2T[:, s, k, :], wr_sb[:, k, :], start=(k == 0), stop=(k == KD - 1))
                    mm.then_inc(lg_ready, 1)

                def tile(t, s):
                    project(t, s)
                    if static(t) and t == 0:
                        pe.wait_ge(const_in, 96)
                    else:
                        turn(t - 1, 1 - s)
                    if not (static(t) and t <= 1):
                        route(t - 2, s)

                over_pairs(pe, tile)
                turn(TILES - 1, 1)
                route(TILES - 2, 0)
                route(TILES - 1, 1)
BLOCKS = 64
MAX_TOK = 1e30


def routing(nc, sem, logits, tables_d, gates, dest, slots, starts, ends):
    G, E, PG = N_GROUPS, N_EXPERTS, PER_GROUP
    T = TILES
    VDIFF = 23
    BEFORE = VDIFF + 2 + T
    NBLK = BEFORE + 3
    with ExitStack() as ctx:
        def sb(name, shape, dt=F32):
            return ctx.enter_context(nc.sbuf_tensor(name, shape, dt))

        def ps(name, shape):
            return ctx.enter_context(nc.psum_tensor(name, shape, F32))

        tri = sb("tri", [P, P])
        ones = sb("ones5", [P, P])
        iota = sb("iota5", [P, P])
        tok = sb("tok5", [P, P])
        gmax = sb("gmax", [P, T])
        gdiff = sb("gdiff", [P, T, G])
        gexp = sb("gexp", [P, T, G])
        gsum = sb("gsum", [P, T])
        ptop = sb("ptop", [P, T])
        geq = sb("geq", [P, T, G])
        gidx = sb("gidx", [P, T])
        ghot = sb("ghot", [P, T, G])
        el = sb("el", [P, T, E])
        eq = sb("eq", [P, T, E])
        top = sb("top", [P, 2, T])
        eidx = sb("eidx", [P, 2, T])
        hot = sb("hot", [P, 2, T, E])
        both = sb("both", [P, T, E])
        before = sb("before", [P, T + 1, E])
        vdiff = sb("vdiff", [P, T])
        vexp = sb("vexp", [P, T])
        vsum = sb("vsum", [P, T])
        vinv = sb("vinv", [P, T])
        rank_i = sb("rank_i", [P, T, E], I32)
        pos_i = sb("pos_i", [P, T, E], I32)
        blk_i = sb("blk_i", [P, T, E], I32)
        posf = sb("posf", [P, T, E])
        blkf = sb("blkf", [P, T, E])
        count_i = sb("count_i", [P, 1], I32)
        nb_i = sb("nb_i", [P, 1], I32)
        nb = sb("nb", [P, 1])
        start_row = sb("start_row", [P, E + 1])
        end_row = sb("end_row", [P, E])
        prod = sb("prod5", [P, 2, T, E])
        pos_k = sb("pos_k", [P, 2, T])
        blk_k = sb("blk_k", [P, 2, T])
        destf = sb("destf", [P, 2, T])
        at_pos = sb("at_pos", [P, 2, P])
        at_blk = sb("at_blk", [P, 2, BLOCKS + 1])

        rank_ps = ps("rank_ps", [P, T * E])
        count_ps = ps("count_ps", [P, 1])
        start_ps = ps("start_ps", [P, E + 1])
        slot_ps = ps("slot_ps", [P, BLOCKS + 1])

        const_in = sem("p5_const_in")
        step = sem("p5_step")
        act_step = sem("p5_act_step")
        pe_step = sem("p5_pe_step")
        pair_ready = sem("p5_pair_ready")
        pair_used = sem("p5_pair_used")

        with nc.Block() as block:
            @block.sync
            def _(sp):
                for n, a in enumerate((tri, ones, iota, tok)):
                    sp.dma_start(a[:, :], tables_d[n, :, :]).then_inc(const_in, 16)

            @block.scalar
            def _(act):
                act.wait_ge(step, 2)
                act.activation(gexp[:, :, :], gdiff[:, :, :], ACT.Exp).then_inc(act_step, 1)
                act.wait_ge(step, VDIFF)
                act.activation(vexp[:, :], vdiff[:, :], ACT.Exp).then_inc(act_step, 1)

            @block.tensor
            def _(pe):
                pe.wait_ge(const_in, 64)
                pe.wait_ge(step, BEFORE)
                pe.matmul(rank_ps[:, :], tri[:, :], both[:, :, :], start=True, stop=False)
                pe.matmul(rank_ps[:, :], ones[:, :], before[:, 0:T, :], start=False, stop=True).then_inc(pe_step, 1)
                pe.matmul(count_ps[0:E, :], before[:, T, :], ones[:, 0:1], start=True, stop=True).then_inc(pe_step, 1)
                pe.wait_ge(step, NBLK)
                pe.matmul(start_ps[:, :], nb[0:E, :].to_broadcast([E, P]), tri[0:E, 0:E + 1], start=True, stop=True)\
                    .then_inc(pe_step, 1)
                for n in range(2 * T):
                    pe.wait_ge(pair_ready, n + 1)
                    pe.matmul(slot_ps[:, :], at_pos[:, n % 2, :], at_blk[:, n % 2, :], start=(n == 0),
                              stop=(n == 2 * T - 1)).then_inc(pair_used, 1)

            @block.vector
            def _(dve):
                done = [0]

                def then(ins):
                    done[0] += 1
                    ins.then_inc(step, 1)
                    dve.wait_ge(step, done[0])

                gl = logits[:, :, 0:G]

                def bc(a, n):
                    return a.unsqueeze(2).to_broadcast([P, T, n])

                def iota_bc(n):
                    return iota[:, 0:n].unsqueeze(1).to_broadcast([P, T, n])

                dve.wait_ge(const_in, 64)
                then(dve.tensor_reduce(gmax[:, :], gl, AX.X, ALU.max))
                then(dve.tensor_tensor(gdiff[:, :, :], gl, bc(gmax[:, :], G), ALU.subtract))
                then(dve.tensor_tensor(geq[:, :, :], gl, bc(gmax[:, :], G), ALU.is_equal))
                then(dve.scalar_tensor_tensor(out=geq[:, :, :], in0=geq[:, :, :], scalar=-float(P),
                                              in1=iota_bc(G), op0=ALU.mult, op1=ALU.add))
                then(dve.tensor_reduce(gidx[:, :], geq[:, :, :], AX.X, ALU.min))
                then(dve.tensor_scalar(gidx[:, :], gidx[:, :], float(P), None, ALU.add))
                then(dve.tensor_tensor(ghot[:, :, :], iota_bc(G), bc(gidx[:, :], G), ALU.is_equal))
                then(dve.tensor_scalar(ghot[:, :, :], ghot[:, :, :], MAX_TOK, -MAX_TOK, ALU.mult, ALU.add))
                then(dve.tensor_tensor(el[:, :, :].rearrange("p t (g e) -> p t g e", g=G),
                                       logits[:, :, G:].rearrange("p t (g e) -> p t g e", g=G),
                                       ghot[:, :, :].unsqueeze(3).to_broadcast([P, T, G, PG]), ALU.add))
                for k in range(2):
                    then(dve.tensor_reduce(top[:, k, :], el[:, :, :], AX.X, ALU.max))
                    then(dve.tensor_tensor(eq[:, :, :], el[:, :, :], bc(top[:, k, :], E), ALU.is_equal))
                    then(dve.scalar_tensor_tensor(out=eq[:, :, :], in0=eq[:, :, :], scalar=-float(P),
                                                  in1=iota_bc(E), op0=ALU.mult, op1=ALU.add))
                    then(dve.tensor_reduce(eidx[:, k, :], eq[:, :, :], AX.X, ALU.min))
                    then(dve.tensor_scalar(eidx[:, k, :], eidx[:, k, :], float(P), None, ALU.add))
                    then(dve.tensor_tensor(hot[:, k, :, :], iota_bc(E), bc(eidx[:, k, :], E), ALU.is_equal))
                    if k == 0:
                        then(dve.scalar_tensor_tensor(out=el[:, :, :], in0=hot[:, 0, :, :], scalar=-2 * MAX_TOK,
                                                      in1=el[:, :, :], op0=ALU.mult, op1=ALU.add))
                then(dve.tensor_tensor(vdiff[:, :], top[:, 1, :], top[:, 0, :], ALU.subtract))
                assert done[0] == VDIFF
                then(dve.tensor_tensor(both[:, :, :], hot[:, 0, :, :], hot[:, 1, :, :], ALU.add))
                then(dve.memset(before[:, 0, :], 0.0))
                for t in range(T):
                    then(dve.tensor_tensor(before[:, t + 1, :], before[:, t, :], both[:, t, :], ALU.add))
                assert done[0] == BEFORE
                dve.wait_ge(pe_step, 2)
                then(dve.tensor_scalar(count_i[0:E, :], count_ps[0:E, :], float(P - 1), None, ALU.add))
                then(dve.tensor_scalar(nb_i[0:E, :], count_i[0:E, :], 7, None, ALU.arith_shift_right))
                then(dve.tensor_scalar(nb[0:E, :], nb_i[0:E, :], 1.0, None, ALU.max))
                assert done[0] == NBLK
                then(dve.tensor_copy(rank_i[:, :, :], rank_ps[:, :].rearrange("p (t e) -> p t e", t=T)))
                then(dve.tensor_scalar(pos_i[:, :, :], rank_i[:, :, :], P - 1, None, ALU.bitwise_and))
                then(dve.tensor_scalar(blk_i[:, :, :], rank_i[:, :, :], 7, None, ALU.arith_shift_right))
                then(dve.tensor_copy(posf[:, :, :], pos_i[:, :, :]))
                dve.wait_ge(pe_step, 3)
                then(dve.tensor_copy(start_row[:, :], start_ps[:, :]))
                then(dve.tensor_copy(starts[:, :], start_row[:, :]))
                then(dve.tensor_scalar(end_row[:, :], start_row[:, 1:], -1.0, None, ALU.add))
                then(dve.tensor_copy(ends[:, :], end_row[:, :]))
                then(dve.tensor_tensor(blkf[:, :, :], blk_i[:, :, :],
                                       start_row[:, 0:E].unsqueeze(1).to_broadcast([P, T, E]), ALU.add))
                for a, out in ((posf, pos_k), (blkf, blk_k)):
                    then(dve.tensor_tensor(prod[:, :, :, :], hot[:, :, :, :],
                                           a[:, :, :].unsqueeze(1).to_broadcast([P, 2, T, E]), ALU.mult))
                    then(dve.tensor_reduce(out[:, :, :], prod[:, :, :, :], AX.X, ALU.add))
                then(dve.scalar_tensor_tensor(out=destf[:, :, :], in0=blk_k[:, :, :], scalar=float(P),
                                              in1=pos_k[:, :, :], op0=ALU.mult, op1=ALU.add))
                then(dve.tensor_copy(dest[:, :, :], destf[:, :, :]))
                for n in range(2 * T):
                    k, t = n % 2, n // 2
                    if n >= 2:
                        dve.wait_ge(pair_used, n - 1)
                    dve.tensor_scalar(at_pos[:, n % 2, :], iota[:, :], pos_k[:, k, t:t + 1], None, ALU.is_equal)
                    dve.tensor_scalar(at_blk[:, n % 2, :], iota[:, 0:BLOCKS + 1], blk_k[:, k, t:t + 1],
                                      tok[:, t:t + 1], ALU.is_equal, ALU.mult).then_inc(pair_ready, 1)
                dve.wait_ge(act_step, 2)
                then(dve.tensor_reduce(gsum[:, :], gexp[:, :, :], AX.X, ALU.add))
                then(dve.reciprocal(ptop[:, :], gsum[:, :]))
                then(dve.tensor_scalar(vsum[:, :], vexp[:, :], 1.0, None, ALU.add))
                then(dve.reciprocal(vinv[:, :], vsum[:, :]))
                then(dve.tensor_tensor(gates[:, 0, :], ptop[:, :], vinv[:, :], ALU.mult))
                then(dve.tensor_tensor(gates[:, 1, :], gates[:, 0, :], vexp[:, :], ALU.mult))
                dve.wait_ge(pair_used, 2 * T)
                then(dve.tensor_copy(slots[:, :], slot_ps[:, :]))
FF = 512
KF = FF // P


def experts(nc, sem, n2_d, w_gate, w_up, w_down, ident_d, slots, starts, ends, y_d):
    PIECES = 12
    PW = 1024
    RAW = 6
    SIGNALLED = [0, 1, 2, 4, 6, 8, 9, 10]
    HALF = FF // 2
    HI_BY = {k: "dve" if k < 3 else "act" for k in range(PIECES)}
    LO_BY = {k: "pool" if k in (1, 4, 7, 9) else "dve" for k in range(PIECES)}
    assert PIECES % RAW == 0

    with ExitStack() as ctx:
        def sb(name, shape, dt=F32):
            return ctx.enter_context(nc.sbuf_tensor(name, shape, dt))

        def ps(name, shape):
            return ctx.enter_context(nc.psum_tensor(name, shape, F32))

        ident = sb("ident6", [P, P])
        wg = [sb(f"wg_{part}", [P, KD, FF], F32R) for part in ("hi", "lo")]
        wu = [sb(f"wu_{part}", [P, KD, FF], F32R) for part in ("hi", "lo")]
        wd = [sb(f"wd_{part}", [P, KF, D], F32R) for part in ("hi", "lo")]
        raw = sb("raw6", [P, RAW, PW])
        idx = sb("idx6", [P, 1], I32)
        x = sb("x6", [P, D])
        xT_hi = sb("xT_hi", [P, KD, P], F32R)
        xT_lo = sb("xT_lo", [P, KD, P], F32R)
        hid = sb("hid", [P, FF])
        hT_hi = sb("hT_hi", [P, KF, P], F32R)
        hT_lo = sb("hT_lo", [P, KF, P], F32R)
        y = sb("y6", [P, D])
        zero = sb("zero6", [P, 64])

        xT_ps = ps("xT_ps", [P, KD, P])
        g_ps = ps("g_ps", [P, FF])
        u_ps = ps("u_ps", [P, 2, FF])
        y_ps = ps("y_ps", [P, 2, 512])

        ident_in = sem("p6_ident_in")
        raw_in = [sem(f"p6_raw_in{r}") for r in range(RAW)]
        piece_used = sem("p6_piece_used")
        hi_ready = {by: sem(f"p6_hi_by_{by}") for by in ("act", "dve")}
        lo_ready = {by: sem(f"p6_lo_by_{by}") for by in ("dve", "pool")}
        idx_ready = sem("p6_idx_ready")
        gathering = sem("p6_gathering")
        x_in = sem("p6_x_in")
        x_turned = sem("p6_x_turned")
        xT_ready = sem("p6_xT_ready")
        xT_split = sem("p6_xT_split")
        g_done = sem("p6_g_done")
        u_done = sem("p6_u_done")
        silu_ready = sem("p6_silu_ready")
        hid_ready = sem("p6_hid_ready")
        h_turned = sem("p6_h_turned")
        hT_ready = sem("p6_hT_ready")
        hT_split = sem("p6_hT_split")
        y_done = sem("p6_y_done")
        y_ready = sem("p6_y_ready")
        zero_ready = sem("p6_zero_ready")
        cleared = sem("p6_cleared")
        all_stored = sem("p6_all_stored")
        y_stored = sem("p6_y_stored")

        def block_count(eng):
            return eng.value_load(starts[0:1, N_EXPERTS:N_EXPERTS + 1], min_val=1, max_val=BLOCKS)

        def over_experts(eng, one_block):
            def expert(e, replaced):
                first = eng.value_load(starts[0:1, bass.ds(e, 1)], min_val=0, max_val=BLOCKS - 1)
                last = eng.value_load(ends[0:1, bass.ds(e, 1)], min_val=0, max_val=BLOCKS - 1)
                with eng.If(first < last):
                    with eng.Fori(first, last) as b:
                        one_block(b, e, False)
                one_block(last, e, replaced)

            with eng.Fori(0, N_EXPERTS - 1) as e:
                expert(e, True)
            expert(N_EXPERTS - 1, False)

        def piece(w, k):
            if k < 4:
                return w[0][:, 2 * k:2 * k + 2, :]
            if k < 8:
                half, rows = (k - 4) // 2, (k - 4) % 2
                return w[1][:, 4 * rows:4 * rows + 4, half * HALF:(half + 1) * HALF]
            return w[2][:, k - 8:k - 7, :]

        def part_ready(by, ready, e, k):
            own = [n for n in range(PIECES) if by[n] == by[k]]
            return ready[by[k]], e * len(own) + (own.index(k) + 1)

        def hi_there(e, k):
            return part_ready(HI_BY, hi_ready, e, k)

        def lo_there(e, k):
            return part_ready(LO_BY, lo_ready, e, k)

        def wait_used(eng, b, e, k):
            if k in SIGNALLED:
                eng.wait_ge(piece_used, e * len(SIGNALLED) + (SIGNALLED.index(k) + 1))
            elif k == 3:
                eng.wait_ge(g_done, b + 1)
            elif k == PIECES - 1:
                eng.wait_ge(y_done, b + 1)
            else:
                eng.wait_ge(u_done, b * 2 + (k - 3) // 2)

        HI = (wg[0], wu[0], wd[0])
        LO = (wg[1], wu[1], wd[1])

        def raw_piece(k):
            return raw[:, k % RAW, :].rearrange("p (a b) -> p a b", a=(2, 4, 1)[k // 4])

        with nc.Block() as block:
            @block.sync
            def _(sp):
                sp.dma_start(ident[:, :], ident_d).then_inc(ident_in, 16)

                def load(e, k, before):
                    if before is not None or k >= RAW:
                        sp.wait_ge(*(lo_there(e, k - RAW) if k >= RAW else lo_there(before, k - RAW + PIECES)))
                    one = bass.ds(e, 1)
                    src = [w[one, :, :].rearrange("o (k p) n -> p (o k) n", p=P) for w in (w_gate, w_up, w_down)]
                    sp.dma_start(raw_piece(k), piece(src, k)).then_inc(raw_in[k % RAW], 16)

                for k in range(PIECES):
                    load(0, k, None)
                with sp.Fori(0, N_EXPERTS - 1) as e:
                    for k in range(PIECES):
                        load(e + 1, k, e)

            @block.gpsimd
            def _(pool):
                nb = block_count(pool)

                def gather(b):
                    pool.wait_ge(x_turned, b + 1)
                    pool.tensor_copy(idx[:, :], slots[:, bass.ds(b, 1)]).then_inc(idx_ready, 1)
                    pool.wait_ge(idx_ready, b + 1)
                    pool.sem_inc(gathering, 1)
                    pool.indirect_dma_start(x[:, :], None, n2_d, bass.IndirectOffsetOnAxis(ap=idx[:, 0:1], axis=0))\
                        .then_inc(x_in, 16)

                def lows(e):
                    for k in range(PIECES):
                        if LO_BY[k] == "pool":
                            pool.wait_ge(*hi_there(e, k))
                            pool.tensor_tensor(piece(LO, k), raw_piece(k), piece(HI, k), ALU.subtract)\
                                .then_inc(lo_ready["pool"], 1)

                def one_block(b, e, replaced):
                    gather(b + 1)
                    if replaced:
                        lows(e + 1)

                gather(0)
                lows(0)
                over_experts(pool, one_block)
                pool.wait_ge(x_in, (nb + 1) * 16)
                pool.sem_inc(gathering, 1)

            @block.scalar
            def _(act):
                nb = block_count(act)
                act.sem_inc(y_ready, 1)
                act.sem_inc(y_stored, 16)

                def copy_xT(b):
                    act.wait_ge(x_turned, b + 2)
                    act.copy(xT_hi[:, :, :], xT_ps[:, :, :]).then_inc(xT_ready, 1)

                def copy_hT(b, half):
                    act.wait_ge(h_turned, b * 2 + (half + 2))
                    src = g_ps if half == 0 else u_ps[:, 0, :]
                    act.copy(hT_hi[:, 2 * half:2 * half + 2, :], src[:, 0:HALF].rearrange("p (k n) -> p k n", k=2))\
                        .then_inc(hT_ready, 1)

                def one_block(b, e, replaced):
                    def pieces(first, last):
                        if replaced:
                            for k in range(first, last):
                                if HI_BY[k] != "act":
                                    continue
                                wait_used(act, b, e, k)
                                act.wait_ge(raw_in[k % RAW], e * 32 + (32 + 16 * (k // RAW) + 16))
                                act.copy(piece(HI, k), raw_piece(k)).then_inc(hi_ready["act"], 1)

                    act.sem_inc(cleared, 16)
                    act.wait_ge(g_done, b + 1)
                    act.wait_ge(h_turned, b * 2 + 1)
                    act.activation(hid[:, :], g_ps[:, :], ACT.Silu).then_inc(silu_ready, 1)
                    pieces(3, 6)
                    copy_hT(b, 0)
                    pieces(6, 7)
                    copy_hT(b, 1)
                    copy_xT(b + 1)
                    pieces(7, 11)
                    act.wait_ge(y_done, b + 1)
                    act.wait_ge(y_stored, b * 16 + 16)
                    act.copy(y[:, 512:], y_ps[:, 1, :]).then_inc(y_ready, 1)
                    pieces(11, 12)
                    act.wait_ge(y_ready, b * 2 + 4)
                    act.dma_start(y_d[bass.ds(b * P, P), :], y[:, :]).then_inc(y_stored, 16)

                for k in range(3, PIECES):
                    act.wait_ge(raw_in[k % RAW], 16 * (k // RAW) + 16)
                    act.copy(piece(HI, k), raw_piece(k)).then_inc(hi_ready["act"], 1)
                act.wait_ge(zero_ready, 1)
                with act.Fori(nb, BLOCKS + 1) as b:
                    act.dma_start(y_d[bass.ds(b * P, P), :].rearrange("p (a b) -> p a b", b=64),
                                  zero[:, :].unsqueeze(1).to_broadcast([P, D // 64, 64])).then_inc(cleared, 16)
                copy_xT(0)
                over_experts(act, one_block)
                act.wait_ge(y_stored, nb * 16 + 16)
                act.sem_inc(all_stored, 1)
                act.wait_ge(cleared, 16 * (BLOCKS + 1))

            @block.vector
            def _(dve):
                dve.memset(zero[:, :], 0.0).then_inc(zero_ready, 1)
                dve.sem_inc(y_ready, 1)

                def high(e, k):
                    dve.wait_ge(raw_in[k % RAW], e * 32 + (16 * (k // RAW) + 16))
                    dve.tensor_copy(piece(HI, k), raw_piece(k)).then_inc(hi_ready["dve"], 1)

                def low(e, k):
                    if LO_BY[k] == "dve":
                        dve.wait_ge(*hi_there(e, k))
                        dve.tensor_tensor(piece(LO, k), raw_piece(k), piece(HI, k), ALU.subtract)\
                            .then_inc(lo_ready["dve"], 1)

                def split_xT(b):
                    dve.wait_ge(xT_ready, b + 1)
                    dve.tensor_tensor(xT_lo[:, :, :], xT_ps[:, :, :], xT_hi[:, :, :], ALU.subtract)\
                        .then_inc(xT_split, 1)

                def split_hT(b, half):
                    dve.wait_ge(hT_ready, b * 2 + (half + 1))
                    src = g_ps if half == 0 else u_ps[:, 0, :]
                    dve.tensor_tensor(hT_lo[:, 2 * half:2 * half + 2, :],
                                      src[:, 0:HALF].rearrange("p (k n) -> p k n", k=2),
                                      hT_hi[:, 2 * half:2 * half + 2, :], ALU.subtract).then_inc(hT_split, 1)

                def hidden(b, half):
                    dve.wait_ge(u_done, b * 2 + (half + 1))
                    cols = slice(half * HALF, (half + 1) * HALF)
                    dve.tensor_tensor(hid[:, cols], hid[:, cols], u_ps[:, half, 0:HALF], ALU.mult)\
                        .then_inc(hid_ready, 1)

                def one_block(b, e, replaced):
                    def lows(*ks):
                        if replaced:
                            for k in ks:
                                low(e + 1, k)

                    if replaced:
                        for k in range(3):
                            wait_used(dve, b, e, k)
                            high(e + 1, k)
                            low(e + 1, k)
                    lows(3)
                    dve.wait_ge(silu_ready, b + 1)
                    hidden(b, 0)
                    hidden(b, 1)
                    split_hT(b, 0)
                    lows(5)
                    split_hT(b, 1)
                    split_xT(b + 1)
                    lows(6)
                    lows(8, 10)
                    dve.wait_ge(y_done, b + 1)
                    dve.wait_ge(y_stored, b * 16 + 16)
                    dve.tensor_copy(y[:, 0:512], y_ps[:, 0, :]).then_inc(y_ready, 1)
                    lows(11)

                for k in range(3):
                    high(0, k)
                for k in range(PIECES):
                    low(0, k)
                split_xT(0)
                over_experts(dve, one_block)

            @block.tensor
            def _(pe):
                def turn_x(b):
                    pe.wait_ge(x_in, b * 16 + 16)
                    for k in range(KD):
                        mm = pe.transpose(xT_ps[:, k, :], x[:, k * P:(k + 1) * P], ident[:, :])
                    mm.then_inc(x_turned, 1)

                def turn_h(b, half):
                    pe.wait_ge(hid_ready, b * 2 + (half + 1))
                    out = g_ps if half == 0 else u_ps[:, 0, :]
                    for k in range(2):
                        at = (2 * half + k) * P
                        mm = pe.transpose(out[:, k * P:(k + 1) * P], hid[:, at:at + P], ident[:, :])
                    mm.then_inc(h_turned, 1)

                def one_block(b, e, replaced):
                    def used(mm, k):
                        if replaced and k in SIGNALLED:
                            mm.then_inc(piece_used, 1)

                    pe.wait_ge(xT_split, b + 1)
                    for k in range(KD):
                        if k % 2 == 0:
                            pe.wait_ge(*lo_there(e, k // 2))
                        mm = split_product(pe, g_ps[:, :], xT_hi[:, k, :], xT_lo[:, k, :], wg[0][:, k, :],
                                           wg[1][:, k, :], k == 0, k == KD - 1)
                        if k == KD - 1:
                            mm.then_inc(g_done, 1)
                        if k % 2 == 1:
                            used(mm, k // 2)
                    for half in range(2):
                        cols = slice(half * HALF, (half + 1) * HALF)
                        for k in range(KD):
                            if k % 4 == 0:
                                pe.wait_ge(*lo_there(e, 4 + 2 * half + k // 4))
                            mm = split_product(pe, u_ps[:, half, 0:HALF], xT_hi[:, k, :], xT_lo[:, k, :],
                                               wu[0][:, k, cols], wu[1][:, k, cols], k == 0, k == KD - 1)
                            if k == KD - 1:
                                mm.then_inc(u_done, 1)
                            if k % 4 == 3:
                                used(mm, 4 + 2 * half + k // 4)
                    turn_h(b, 0)
                    turn_x(b + 1)
                    turn_h(b, 1)
                    pe.wait_ge(y_ready, b * 2 + 2)
                    for k in range(KF):
                        if k % 2 == 0:
                            pe.wait_ge(hT_split, b * 2 + (k // 2 + 1))
                        pe.wait_ge(*lo_there(e, 8 + k))
                        for half in range(2):
                            cols = slice(half * 512, (half + 1) * 512)
                            mm = split_product(pe, y_ps[:, half, :], hT_hi[:, k, :], hT_lo[:, k, :], wd[0][:, k, cols],
                                               wd[1][:, k, cols], k == 0, k == KF - 1)
                        if k == KF - 1:
                            mm.then_inc(y_done, 1)
                        used(mm, 8 + k)

                pe.sem_inc(x_turned, 1)
                pe.sem_inc(h_turned, 1)
                pe.wait_ge(ident_in, 16)
                turn_x(0)
                over_experts(pe, one_block)


def combine(nc, sem, y_d, final_g, h_sb, gates, dest, out):
    with ExitStack() as ctx:
        def sb(name, shape, dt=F32):
            return ctx.enter_context(nc.sbuf_tensor(name, shape, dt))

        g_bc = sb("gf_bc", [P, D])
        power = sb("power7", [P, 2])
        idx = sb("idx7", [P, 2, 2, 1], I32)
        gate = sb("gate7", [P, 2, 2, 1])
        y = sb("y7", [P, 2, 2, D])
        acc = sb("acc7", [P, 2, D])
        sq = sb("sq7", [P, 2, D])
        ss = sb("ss7", [P, 2])
        var = sb("var7", [P, 2])
        rstd = sb("rstd7", [P, 2])
        o = sb("o7", [P, 2, D])

        const_in = sem("p7_const_in")
        power_ready = sem("p7_power_ready")
        idx_ready = sem("p7_idx_ready")
        gathering = sem("p7_gathering")
        y_in = [sem("p7_y_in0"), sem("p7_y_in1")]
        acc_step = sem("p7_acc_step")
        ss_ready = sem("p7_ss_ready")
        var_ready = sem("p7_var_ready")
        rstd_ready = sem("p7_rstd_ready")
        o_ready = sem("p7_o_ready")
        stored = [sem("p7_stored0"), sem("p7_stored1")]

        with nc.Block() as block:
            @block.sync
            def _(sp):
                sp.dma_start(g_bc[:, :], row_broadcast(final_g, D)).then_inc(const_in, 16)

                def tile(t, s):
                    sp.wait_ge(o_ready, t + 1)
                    sp.dma_start(out[bass.ts(t, P), :], o[:, s, :]).then_inc(stored[s], 16)

                over_pairs(sp, tile)
                for s in range(2):
                    sp.wait_ge(stored[s], 8 * TILES)

            @block.gpsimd
            def _(pool):
                pool.memset(power[:, 0:1], -0.5).then_inc(power_ready, 1)
                pool.memset(power[:, 1:2], EPS).then_inc(power_ready, 1)
                pool.wait_ge(power_ready, 2)

                def gather(t, s):
                    if not (static(t) and t < 2):
                        pool.wait_ge(acc_step, t * 2 - 2)
                    one = bass.ds(t, 1)
                    pool.tensor_copy(idx[:, s, :, :], dest[:, :, one]).then_inc(idx_ready, 1)
                    pool.tensor_copy(gate[:, s, :, :], gates[:, :, one]).then_inc(idx_ready, 1)
                    pool.wait_ge(idx_ready, t * 2 + 2)
                    pool.sem_inc(gathering, 1)
                    for k in range(2):
                        pool.indirect_dma_start(y[:, s, k, :], None, y_d,
                                                bass.IndirectOffsetOnAxis(ap=idx[:, s, k, :], axis=0))\
                            .then_inc(y_in[s], 16)

                def tile(t, s):
                    if not (static(t) and t == TILES - 1):
                        gather(t + 1, 1 - s)
                    pool.wait_ge(ss_ready, t + 1)
                    pool.tensor_tensor(var[:, s:s + 1], ss[:, s:s + 1], power[:, 1:2], ALU.add).then_inc(var_ready, 1)
                    pool.wait_ge(var_ready, t + 1)
                    pool.tensor_tensor(rstd[:, s:s + 1], var[:, s:s + 1], power[:, 0:1], ALU.pow)\
                        .then_inc(rstd_ready, 1)

                gather(0, 0)
                over_pairs(pool, tile)

            @block.scalar
            def _(act):
                def tile(t, s):
                    act.wait_ge(acc_step, t * 2 + 2)
                    if not (static(t) and t < 2):
                        act.wait_ge(o_ready, t - 1)
                    act.activation(sq[:, s, :], acc[:, s, :], ACT.Square, scale=1.0 / math.sqrt(D),
                                   accum_out=ss[:, s:s + 1]).then_inc(ss_ready, 1)

                over_pairs(act, tile)

            @block.vector
            def _(dve):
                def normalize(t, s):
                    dve.wait_ge(rstd_ready, t + 1)
                    if not (static(t) and t < 2):
                        dve.wait_ge(stored[s], (t - s) * 8)
                    dve.scalar_tensor_tensor(out=o[:, s, :], in0=acc[:, s, :], scalar=rstd[:, s:s + 1],
                                             in1=g_bc[:, :], op0=ALU.mult, op1=ALU.mult).then_inc(o_ready, 1)

                def tile(t, s):
                    dve.wait_ge(y_in[s], (t - s) * 16 + 32)
                    if not (static(t) and t < 2):
                        dve.wait_ge(o_ready, t - 1)
                    h = h_sb[:, t:t + 1, :] if static(t) else h_sb[:, bass.ds(t, 1), :]
                    dve.scalar_tensor_tensor(out=acc[:, s:s + 1, :], in0=y[:, s, 0:1, :], scalar=gate[:, s, 0, :],
                                             in1=h, op0=ALU.mult, op1=ALU.add).then_inc(acc_step, 1)
                    dve.wait_ge(acc_step, t * 2 + 1)
                    dve.scalar_tensor_tensor(out=acc[:, s, :], in0=y[:, s, 1, :], scalar=gate[:, s, 1, :],
                                             in1=acc[:, s, :], op0=ALU.mult, op1=ALU.add).then_inc(acc_step, 1)
                    if not (static(t) and t == 0):
                        normalize(t - 1, 1 - s)

                dve.wait_ge(const_in, 16)
                over_pairs(dve, tile)
                normalize(TILES - 1, 1)
def build(nc, x, norm1_g, w_in, lambda_q1, lambda_k1, lambda_q2, lambda_k2, subln_g, sinks, w_out, norm2_g,
          w_router_group, b_router_group, w_router_expert, b_router_expert, w_gate, w_up, w_down, final_g,
          rope, ident, causal, band, tables, out):
    qk_d = nc.dram_tensor("qk_scratch", [2, QK_BLOCKS, P, SEQ], F32).ap()
    v_d = nc.dram_tensor("v_scratch", [SEQ, V_COLS], F32).ap()
    mix_d = nc.dram_tensor("mix_scratch", [KD, P, SEQ], F32).ap()
    n2_d = nc.dram_tensor("n2_scratch", [SEQ, D], F32).ap()
    y_d = nc.dram_tensor("y_scratch", [(BLOCKS + 1) * P, D], F32).ap()
    with ExitStack() as ctx:
        def sb(name, shape, dt=F32):
            return ctx.enter_context(nc.sbuf_tensor(name, shape, dt))

        def sem(name):
            return ctx.enter_context(nc.semaphore(name))

        projection(nc, sem, x, norm1_g, w_in, rope, ident, qk_d, v_d)
        diff_attention(nc, sem, qk_d, v_d, (lambda_q1, lambda_k1, lambda_q2, lambda_k2), subln_g, ident, causal, mix_d)
        window_attention(nc, sem, qk_d, v_d, sinks, ident, band, mix_d)
        h_sb = sb("h_sb", [P, TILES, D])
        gates = sb("gates", [P, 2, TILES])
        dest = sb("dest", [P, 2, TILES], I32)
        slots = sb("slots", [P, BLOCKS + 1], I32)
        starts = sb("starts", [P, N_EXPERTS + 1], I32)
        ends = sb("ends", [P, N_EXPERTS], I32)
        with nc.sbuf_tensor("logits", [P, TILES, LOGITS], F32) as logits:
            output_projection(nc, sem, x, mix_d, w_out, norm2_g, w_router_group, b_router_group, w_router_expert,
                              b_router_expert, ident, h_sb, logits, n2_d)
            routing(nc, sem, logits, tables, gates, dest, slots, starts, ends)
        experts(nc, sem, n2_d, w_gate, w_up, w_down, ident, slots, starts, ends, y_d)
        combine(nc, sem, y_d, final_g, h_sb, gates, dest, out)


def constants():
    inv = (1.0 / (10000.0 ** (np.arange(0, HD, 2, dtype=np.float32) / np.float32(HD)))).astype(np.float32)
    ang = np.arange(SEQ, dtype=np.float32)[:, None] * inv[None, :]
    c, s, q = np.cos(ang), np.sin(ang), np.float32(HD ** -0.5)
    rope = np.concatenate([c * q, c * q, -s * q, s * q, c, c, -s, s], axis=1).astype(np.float32)
    r = np.arange(P)
    eye = np.eye(P, dtype=np.float32)
    own = np.where(r[None, :] > r[:, None], NEG, 0.0)
    ahead = np.where(r[None, :] <= r[:, None], NEG, 0.0)
    none = np.full((P, P), NEG)
    tables = [r[:, None] < r[None, :], np.ones((P, P)), np.broadcast_to(r[None, :], (P, P)),
              r[:, None] + P * r[None, :]]
    return {
        "rope": rope,
        "ident": eye,
        "causal": np.stack([eye, own]).astype(np.float32),
        "band": np.stack([eye, none, own, ahead, own]).astype(np.float32),
        "tables": np.stack(tables).astype(np.float32),
    }


_INS = ["x", "norm1_g", "w_in", "lambda_q1", "lambda_k1", "lambda_q2", "lambda_k2", "subln_g", "sinks", "w_out",
        "norm2_g", "w_router_group", "b_router_group", "w_router_expert", "b_router_expert", "w_gate", "w_up",
        "w_down", "final_g"]


def kernel(**inputs):
    import concourse.bacc as _bacc
    from concourse.bass_utils import run_bass_kernel_spmd as _run

    nc = _bacc.Bacc("TRN2", target_bir_lowering=False, num_devices=1)
    arrays, args = {}, {}

    def declare(name, a):
        arrays[f"in_{name}"] = a
        args[name] = nc.dram_tensor(f"in_{name}", a.shape, mybir.dt.from_np(a.dtype), kind="ExternalInput").ap()

    for name in _INS:
        a = np.ascontiguousarray(inputs[name])
        declare(name, a if name == "final_g" else a[0])
    for name, a in constants().items():
        declare(name, a)
    out = nc.dram_tensor("out_0", [SEQ, D], F32, kind="ExternalOutput").ap()
    build(nc, out=out, **args)
    r = _run(nc, [arrays], core_ids=[0])
    return r.results[0]["out_0"].reshape(1, SEQ, D)
```

```python
import math
from contextlib import ExitStack

import numpy as np
import concourse.bass as bass
from concourse import mybir

F32 = mybir.dt.float32
F32R = mybir.dt.float32r
BF16 = mybir.dt.bfloat16
I32 = mybir.dt.int32
ALU = mybir.AluOpType
ACT = mybir.ActivationFunctionType
AX = mybir.AxisListType

P = 128
D = 1024
KD = D // P
SEQ = 2048
TILES = SEQ // P
HD = 64
DIFF_HEADS = 4
SWA_HEADS = 8
KV_HEADS = 2
IN_COLS = 2304
ROPE_HEADS = 26
QK_BLOCKS = ROPE_HEADS // 2
V_COLS = 640
EPS = 1e-6
NEG = -1e30


def row_broadcast(ap, width):
    return bass.AP(ap.tensor, ap.offset, [[0, P], [1, width]])


def over_pairs(eng, tile, last=TILES // 2):
    for s in range(2):
        tile(s, s)
    with eng.Fori(1, last - 1) as i:
        for s in range(2):
            tile(i * 2 + s, s)
    for s in range(2):
        tile(2 * last - 2 + s, s)


def static(t):
    return isinstance(t, int)


def split_product(pe, out, hi, lo, w_hi, w_lo, first, last):
    pe.matmul(out, hi, w_lo, start=first, stop=False)
    pe.matmul(out, lo, w_hi, start=False, stop=False)
    return pe.matmul(out, hi, w_hi, start=False, stop=last)


def split_weights(nc, sem, name, src, hi, lo, width, load_next):
    RING = 3
    K, N = hi.shape[1], hi.shape[2]
    pieces = N // width
    with ExitStack() as ctx:
        raw = ctx.enter_context(nc.sbuf_tensor(f"{name}_raw", [P, RING, K, width], F32))
        raw_in = [sem(f"{name}_raw_in{r}") for r in range(RING)]
        hi_ready = sem(f"{name}_hi_ready")
        lo_ready = sem(f"{name}_lo_ready")

        with nc.Block() as block:
            @block.sync
            def _(sp):
                for n in range(pieces):
                    if n >= RING:
                        sp.wait_ge(lo_ready, n - RING + 1)
                    sp.dma_start(raw[:, n % RING, :, :], src[:, :, n * width:(n + 1) * width])\
                        .then_inc(raw_in[n % RING], 16)
                load_next(sp)

            @block.scalar
            def _(act):
                for n in range(pieces):
                    act.wait_ge(raw_in[n % RING], 16 * (n // RING + 1))
                    act.copy(hi[:, :, n * width:(n + 1) * width], raw[:, n % RING, :, :]).then_inc(hi_ready, 1)

            @block.vector
            def _(dve):
                for n in range(pieces):
                    dve.wait_ge(hi_ready, n + 1)
                    dve.tensor_tensor(lo[:, :, n * width:(n + 1) * width], raw[:, n % RING, :, :],
                                      hi[:, :, n * width:(n + 1) * width], ALU.subtract).then_inc(lo_ready, 1)


def projection(nc, sem, x, norm1_g, w_in, rope, ident_d, qk_d, v_d):
    with ExitStack() as ctx:
        def sb(name, shape, dt=F32):
            return ctx.enter_context(nc.sbuf_tensor(name, shape, dt))

        def ps(name, shape):
            return ctx.enter_context(nc.psum_tensor(name, shape, F32))

        w_hi = sb("w_in_hi", [P, KD, IN_COLS], F32R)
        w_lo = sb("w_in_lo", [P, KD, IN_COLS], F32R)
        ident = sb("ident1", [P, P])
        g_bc = sb("g1_bc", [P, D])
        rope_sb = sb("rope_sb", [P, 2, 4, HD])
        x_sb = sb("x_sb", [P, 2, D])
        const_in = sem("p1_const_in")
        rope_in = [sem("p1_rope_in0"), sem("p1_rope_in1")]
        x_in = [sem("p1_x_in0"), sem("p1_x_in1")]

        def load_rope(sp, t, s):
            sp.dma_start(rope_sb[:, s, :, :].rearrange("p k d -> p (k d)"), rope[bass.ts(t, P), :])\
                .then_inc(rope_in[s], 16)

        def load_first(sp):
            sp.dma_start(ident[:, :], ident_d).then_inc(const_in, 16)
            sp.dma_start(g_bc[:, :], row_broadcast(norm1_g, D)).then_inc(const_in, 16)
            for s in range(2):
                sp.dma_start(x_sb[:, s, :], x[s * P:(s + 1) * P, :]).then_inc(x_in[s], 16)
                load_rope(sp, s, s)

        split_weights(nc, sem, "w_in", w_in.rearrange("(k p) n -> p k n", p=P), w_hi, w_lo, 256, load_first)
        sq = sb("sq1", [P, D], BF16)
        ss = sb("ss1", [P, 2])
        power = sb("power1", [P, 2])
        var = sb("var1", [P, 2])
        rstd = sb("rstd1", [P, 2])
        n1T_hi = sb("n1T_hi", [P, 2, KD, P], F32R)
        n1T_lo = sb("n1T_lo", [P, 2, KD, P], F32R)
        cosx = sb("cosx", [P, 2, 8, HD])
        roped = sb("roped", [P, 2, ROPE_HEADS, HD])
        vrow = sb("vrow", [P, 2, V_COLS])
        qkT = sb("qkT", [P, 2, 2, 4, P], F32R)

        proj = ps("proj", [P, 4, 512])
        n1t_ps = ps("n1t_ps", [P, KD, P])
        qkt_ps = ps("qkt_ps", [P, 2, 4, P])

        ss_ready = sem("p1_ss_ready")
        var_ready = sem("p1_var_ready")
        rstd_ready = sem("p1_rstd_ready")
        power_ready = sem("p1_power_ready")
        n1_ready = sem("p1_n1_ready")
        passed = sem("p1_passed")
        n1t_turned = sem("p1_n1t_turned")
        n1t_ready = sem("p1_n1t_ready")
        n1t_split = sem("p1_n1t_split")
        proj_ready = sem("p1_proj_ready")
        rope_read = sem("p1_rope_read")
        roped_ready = sem("p1_roped_ready")
        v_ready = sem("p1_v_ready")
        qkt_turned = sem("p1_qkt_turned")
        qkt_ready = sem("p1_qkt_ready")
        qkt_split = sem("p1_qkt_split")
        qk_stored = [sem("p1_qk_stored0"), sem("p1_qk_stored1")]
        v_stored = [sem("p1_v_stored0"), sem("p1_v_stored1")]

        GROUPS = [(0, 512, 0, 8, 0, 0), (512, 512, 8, 8, 2, 1), (1024, 512, None, 0, 0, 2),
                  (1536, 512, 16, 8, 0, 3), (2048, 256, 24, 2, 2, 1)]
        BATCH = [(0, 4), (4, 4), (8, 4), (12, 1)]

        with nc.Block() as block:
            @block.sync
            def _(sp):
                for b in range(2):
                    sp.sem_inc(qk_stored[b], 32)

                def store(t, s):
                    sp.wait_ge(v_ready, t * 2 + 2)
                    sp.dma_start(v_d[bass.ts(t, P), :], vrow[:, s, :]).then_inc(v_stored[s], 16)
                    for b, (first, n) in enumerate(BATCH):
                        sp.wait_ge(qkt_split, t * 4 + (b + 1))
                        sp.sem_inc(passed, 1)
                        for part in range(2):
                            sp.dma_start(qk_d[part, first:first + n, :, bass.ts(t, P)].rearrange("b p t -> p b t"),
                                         qkT[:, b % 2, part, 0:n, :].bitcast(F32)).then_inc(qk_stored[b % 2], 16)

                def tile(t, s):
                    if not (static(t) and t >= TILES - 2):
                        sp.wait_ge(n1t_turned, t + 1)
                        sp.dma_start(x_sb[:, s, :], x[bass.ts(t + 2, P), :]).then_inc(x_in[s], 16)
                    if not (static(t) and t == 0):
                        store(t - 1, 1 - s)
                    if not (static(t) and t >= TILES - 2):
                        sp.wait_ge(rope_read, t * 4 + 4)
                        load_rope(sp, t + 2, s)

                over_pairs(sp, tile)
                store(TILES - 1, 1)
                for s in range(2):
                    sp.wait_ge(qk_stored[s], 64 * TILES + 32)
                    sp.wait_ge(v_stored[s], 8 * TILES)

            @block.scalar
            def _(act):
                def mean_square(t, s):
                    act.wait_ge(x_in[s], (t // 2 if static(t) else (t - s) // 2) * 16 + 16)
                    if not (static(t) and t < 2):
                        act.wait_ge(n1_ready, t - 1)
                    act.activation(sq[:, :], x_sb[:, s, :], ACT.Square, scale=1.0 / math.sqrt(D),
                                   accum_out=ss[:, s:s + 1]).then_inc(ss_ready, 1)

                def copy_n1t(t, s):
                    act.wait_ge(n1t_turned, t + 1)
                    act.copy(n1T_hi[:, s, :, :], n1t_ps[:, :, :]).then_inc(n1t_ready, 1)

                def copy_qkt(t, b):
                    n = BATCH[b][1]
                    act.wait_ge(qkt_turned, t * 4 + (b + 1))
                    act.wait_ge(qk_stored[b % 2], t * 64 + (32 * (b // 2) + 32))
                    act.copy(qkT[:, b % 2, 0, 0:n, :], qkt_ps[:, b % 2, 0:n, :]).then_inc(qkt_ready, 1)

                def tile(t, s):
                    before = not (static(t) and t == 0)
                    after = not (static(t) and t == TILES - 1)
                    if before:
                        copy_qkt(t - 1, 0)
                    if after:
                        mean_square(t + 1, 1 - s)
                    if before:
                        copy_qkt(t - 1, 1)
                    if after:
                        copy_n1t(t + 1, 1 - s)
                    if not (static(t) and t < 2):
                        act.wait_ge(v_stored[s], (t - s) * 8)
                    act.wait_ge(proj_ready, t * 5 + 3)
                    act.copy(vrow[:, s, 0:512], proj[:, 2, :]).then_inc(v_ready, 1)
                    if before:
                        copy_qkt(t - 1, 2)
                        copy_qkt(t - 1, 3)
                    act.wait_ge(proj_ready, t * 5 + 5)
                    act.wait_ge(rope_read, t * 4 + 4)
                    act.copy(vrow[:, s, 512:640], proj[:, 1, 128:256]).then_inc(v_ready, 1)

                mean_square(0, 0)
                copy_n1t(0, 0)
                over_pairs(act, tile)
                for b in range(4):
                    copy_qkt(TILES - 1, b)

            @block.vector
            def _(dve):
                def normalize(t, s):
                    dve.wait_ge(rstd_ready, t + 1)
                    dve.scalar_tensor_tensor(out=x_sb[:, s, :], in0=x_sb[:, s, :], scalar=rstd[:, s:s + 1],
                                             in1=g_bc[:, :], op0=ALU.mult, op1=ALU.mult).then_inc(n1_ready, 1)

                def split_n1t(t, s):
                    dve.wait_ge(n1t_ready, t + 1)
                    dve.tensor_tensor(n1T_lo[:, s, :, :], n1t_ps[:, :, :], n1T_hi[:, s, :, :], ALU.subtract)\
                        .then_inc(n1t_split, 1)

                def split_qkt(t, b):
                    n = BATCH[b][1]
                    dve.wait_ge(qkt_ready, t * 4 + (b + 1))
                    dve.tensor_tensor(qkT[:, b % 2, 1, 0:n, :], qkt_ps[:, b % 2, 0:n, :],
                                      qkT[:, b % 2, 0, 0:n, :], ALU.subtract).then_inc(qkt_split, 1)

                def tile(t, s):
                    if not (static(t) and t == TILES - 1):
                        normalize(t + 1, 1 - s)
                    dve.wait_ge(rope_in[s], (t - s) * 8 + 16)
                    if not (static(t) and t < 2):
                        dve.wait_ge(qkt_turned, t * 4 - 4)
                    for g, (_, _, head, heads, table, bank) in enumerate(GROUPS):
                        if head is None:
                            if not (static(t) and t == 0):
                                split_qkt(t - 1, g)
                            continue
                        dve.wait_ge(proj_ready, t * 5 + (g + 1))
                        part = g - (g > 2)
                        if not (static(t) and t * 4 + part < 2):
                            dve.wait_ge(roped_ready, t * 4 + (part - 1))
                        src = proj[:, bank, 0:heads * HD].rearrange("p (h d) -> p h d", d=HD)
                        cos = rope_sb[:, s:s + 1, table, :]
                        sin = rope_sb[:, s:s + 1, table + 1, :]
                        dve.tensor_tensor(cosx[:, part % 2, 0:heads, :], src,
                                          cos.to_broadcast([P, heads, HD]), ALU.mult)
                        dve.tensor_tensor(roped[:, s, head:head + heads, 0:32], src[:, :, 32:64],
                                          sin[:, :, 0:32].to_broadcast([P, heads, 32]), ALU.mult)
                        dve.tensor_tensor(roped[:, s, head:head + heads, 32:64], src[:, :, 0:32],
                                          sin[:, :, 32:64].to_broadcast([P, heads, 32]), ALU.mult)\
                            .then_inc(rope_read, 1)
                        if g < 4 and not (static(t) and t == 0):
                            split_qkt(t - 1, g)
                        if g == 1 and not (static(t) and t == TILES - 1):
                            split_n1t(t + 1, 1 - s)

                dve.wait_ge(const_in, 32)
                normalize(0, 0)
                split_n1t(0, 0)
                over_pairs(dve, tile)
                for b in range(4):
                    split_qkt(TILES - 1, b)

            @block.gpsimd
            def _(pool):
                def inverse_root(t, s):
                    pool.wait_ge(ss_ready, t + 1)
                    pool.tensor_tensor(var[:, s:s + 1], ss[:, s:s + 1], power[:, 1:2], ALU.add).then_inc(var_ready, 1)
                    pool.wait_ge(var_ready, t + 1)
                    if not (static(t) and t < 2):
                        pool.wait_ge(n1_ready, t - 1)
                    pool.tensor_tensor(rstd[:, s:s + 1], var[:, s:s + 1], power[:, 0:1], ALU.pow)\
                        .then_inc(rstd_ready, 1)

                def tile(t, s):
                    if not (static(t) and t == TILES - 1):
                        inverse_root(t + 1, 1 - s)
                    for n, (head, heads) in enumerate([(0, 8), (8, 8), (16, 8), (24, 2)]):
                        pool.wait_ge(rope_read, t * 4 + (n + 1))
                        pool.tensor_tensor(roped[:, s, head:head + heads, :], roped[:, s, head:head + heads, :],
                                           cosx[:, n % 2, 0:heads, :], ALU.add).then_inc(roped_ready, 1)

                pool.memset(power[:, 0:1], -0.5).then_inc(power_ready, 1)
                pool.memset(power[:, 1:2], EPS).then_inc(power_ready, 1)
                pool.wait_ge(power_ready, 2)
                inverse_root(0, 0)
                over_pairs(pool, tile)

            @block.tensor
            def _(pe):
                def turn_n1(t, s):
                    pe.wait_ge(n1_ready, t + 1)
                    for k in range(KD):
                        mm = pe.transpose(n1t_ps[:, k, :], x_sb[:, s, k * P:(k + 1) * P], ident[:, :])
                    mm.then_inc(n1t_turned, 1)

                def group(t, s, g):
                    c0, w, _, _, _, bank = GROUPS[g]
                    if g == 0:
                        pe.wait_ge(n1t_split, t + 1)
                    if not (static(t) and t == 0):
                        if g == 0:
                            pe.wait_ge(rope_read, t * 4 - 3)
                        elif g == 1:
                            pe.wait_ge(rope_read, t * 4)
                            pe.wait_ge(v_ready, t * 2)
                    if g == 4:
                        pe.wait_ge(rope_read, t * 4 + 2)
                    for k in range(KD):
                        mm = split_product(pe, proj[:, bank, 0:w], n1T_hi[:, s, k, :], n1T_lo[:, s, k, :],
                                           w_hi[:, k, c0:c0 + w], w_lo[:, k, c0:c0 + w], k == 0, k == KD - 1)
                    mm.then_inc(proj_ready, 1)

                def turn_qk(t, s, b):
                    first, n = BATCH[b]
                    if b == 0:
                        pe.wait_ge(roped_ready, t * 4 + 4)
                    blocks = roped[:, s, :, :].rearrange("p (b h) d -> p b (h d)", h=2)
                    if not (static(t) and t * 4 + b < 2):
                        pe.wait_ge(qkt_split, t * 4 + (b - 1))
                    for j in range(n):
                        mm = pe.transpose(qkt_ps[:, b % 2, j, :], blocks[:, first + j, :], ident[:, :])
                    mm.then_inc(qkt_turned, 1)

                def tile(t, s):
                    for g in range(len(GROUPS)):
                        group(t, s, g)
                        if g < len(BATCH) and not (static(t) and t == 0):
                            turn_qk(t - 1, 1 - s, g)
                        if g == 1 and not (static(t) and t == TILES - 1):
                            turn_n1(t + 1, 1 - s)

                pe.wait_ge(const_in, 32)
                turn_n1(0, 0)
                over_pairs(pe, tile)
                for b in range(len(BATCH)):
                    turn_qk(TILES - 1, 1, b)
def diff_attention(nc, sem, qk_d, v_d, lambdas, subln_g, ident_d, causal_d, mix_d, y_d):
    LAG = 6
    CHUNK = 512
    DV = 2 * HD
    STEPS = []
    ORDER = [(0, i) for i in range(TILES)] + [(1, i) for i in range(1, TILES)] + [(1, 0)]
    for m, (hh, i) in enumerate(ORDER):
        keys = (i + 1) * P
        piece = CHUNK if keys > CHUNK else 2 * P if i > 1 else P
        for j in range(0, keys, piece):
            STEPS.append((hh, i, j, min(piece, keys - j), m))
    N = len(STEPS)
    RUN = len(ORDER)
    NEEDS = {min(n for n in range(N) if STEPS[n][0] == hh and STEPS[n][1] * P // CHUNK >= c): (hh, c)
             for hh in range(2) for c in range(SEQ // CHUNK)}
    HEAD_END = {max(n for n in range(N) if STEPS[n][0] == hh): hh for hh in range(2)}
    FIRST = {m: min(n for n in range(N) if STEPS[n][4] == m) for m in range(RUN)}
    LAST = {m: max(n for n in range(N) if STEPS[n][4] == m) for m in range(RUN)}
    ENDS = {n: m for m, n in LAST.items()}
    RING = 7
    assert RING > LAG and N % 2 == 0
    STATS = [6 if LAST[m] > FIRST[m] else 1 for m in range(RUN)]
    STAT_END = [sum(STATS[:m + 1]) for m in range(RUN)]
    STAT_ALL = STAT_END[-1]
    LONG = [m for m in range(RUN) if LAST[m] > FIRST[m]]
    LAMBDA_INIT = 0.8 - 0.6 * math.exp(-0.3 * 0)

    with ExitStack() as ctx:
        def sb(name, shape, dt=F32):
            return ctx.enter_context(nc.sbuf_tensor(name, shape, dt))

        def ps(name, shape):
            return ctx.enter_context(nc.psum_tensor(name, shape, F32))

        ident = sb("ident2", [P, P])
        causal_f = sb("causal_f", [P, 2, P])
        causal = sb("causal", [P, 2, P], BF16)
        lam_in = sb("lam_in", [P, 4, HD])
        lam_prod = sb("lam_prod", [P, 2, HD])
        lam = sb("lam", [P, 6])
        g_bc = sb("subln_bc", [P, DV])
        g_out = sb("subln_out", [P, DV])
        power = sb("power2", [P, 2])
        zero = sb("zero2", [P, y_d.shape[1]])
        qT = sb("qT", [P, 2, 2, SEQ], F32R)
        kT_hi = sb("kT_hi", [P, 2, 2, SEQ], F32R)
        kT_lo = sb("kT_lo", [P, 2, 2, SEQ], F32R)
        v = sb("v_sb", [P, 2, TILES, DV])
        prob = sb("prob", [P, RING, 2, CHUNK])
        nmax = sb("nmax", [P, 2, N])
        nrow = sb("nrow", [P, 2, RUN])
        part = sb("part", [P, 2, N])
        under = sb("under", [P, 2, N])
        fac = sb("fac", [P, 2, N])
        part_row = sb("part_row", [P, 2, N])
        total = sb("total", [P, 2, RUN])
        inv = sb("inv", [P, 2, RUN])
        scale = sb("scale", [P, 2, N])
        aT = sb("aT", [P, 2, CHUNK])
        osq = sb("osq", [P, 2, DV])
        oss = sb("oss", [P, 2])
        ovar = sb("ovar", [P, 2])
        orstd = sb("orstd", [P, 2])
        onorm = sb("onorm", [P, 2, DV])
        oT = sb("oT", [P, 2, P])

        score = ps("score", [P, 2, 2, CHUNK])
        aT_ps = ps("aT_ps", [P, CHUNK])
        o_ps = ps("o_ps", [P, 2, CHUNK])
        oT_ps = ps("oT_ps", [P, CHUNK])

        const_in = sem("p2_const_in")
        lam_step = sem("p2_lam_step")
        mask_ready = sem("p2_mask_ready")
        power_ready = sem("p2_power_ready")
        passed = sem("p2_passed")
        cleared = sem("p2_cleared")
        head_in = [[sem(f"p2_head_in{hh}_{c}") for c in range(SEQ // CHUNK)] for hh in range(2)]
        LOAD = 7 * 16
        head_done = sem("p2_head_done")
        score_ready = sem("p2_score_ready")
        score_free = sem("p2_score_free")
        max_ready = sem("p2_max_ready")
        fac_ready = sem("p2_fac_ready")
        stat_step = sem("p2_stat_step")
        scaled = sem("p2_scaled")
        a_ready = sem("p2_a_ready")
        a_turned = sem("p2_a_turned")
        aT_ready = sem("p2_aT_ready")
        pv_done = sem("p2_pv_done")
        oss_ready = sem("p2_oss_ready")
        ovar_ready = sem("p2_ovar_ready")
        orstd_ready = sem("p2_orstd_ready")
        on_ready = sem("p2_on_ready")
        o_turned = sem("p2_o_turned")
        oT_ready = sem("p2_oT_ready")
        stored = [sem("p2_stored0"), sem("p2_stored1")]

        def over_pairs(eng, pair):
            with eng.Fori(0, DIFF_HEADS // 2) as g:
                pair(g)

        SLOTS = N + LAG + 4

        with nc.Block() as block:
            @block.sync
            def _(sp):
                def load(h, hh):
                    for n in range(SEQ // CHUNK):
                        at = slice(n * CHUNK, (n + 1) * CHUNK)
                        for half in range(2):
                            to = slice(half * HD, (half + 1) * HD)
                            for dest, part, block in ((qT, half, h), (kT_hi, 0, DIFF_HEADS + h),
                                                      (kT_lo, 1, DIFF_HEADS + h)):
                                sp.dma_start(dest[to, hh, :, at].bitcast(F32),
                                             qk_d[part, block, :, at].rearrange("(c d) t -> d c t", d=HD))\
                                    .then_inc(head_in[hh][n], 16)
                        sp.dma_start(v[:, hh, n * (CHUNK // P):(n + 1) * (CHUNK // P), :],
                                     v_d[at, h * DV:(h + 1) * DV].rearrange("(t p) d -> p t d", p=P))\
                            .then_inc(head_in[hh][n], 16)

                def clear(b):
                    sp.dma_start(y_d[b * P:(b + 1) * P, :], zero[:, :]).then_inc(cleared, 16)

                for s in range(2):
                    sp.sem_inc(stored[s], 16)
                load(0, 0)
                load(1, 1)
                sp.wait_ge(power_ready, 3)
                for h in range(DIFF_HEADS):
                    for m in range(TILES):
                        t = ORDER[h % 2 * TILES + m][1]
                        sp.wait_ge(oT_ready, h * TILES + m + 2)
                        sp.dma_start(mix_d[h, :, t * P:(t + 1) * P], oT[:, m % 2, :]).then_inc(stored[m % 2], 16)
                        clear(h * TILES + m)
                    if h + 2 < DIFF_HEADS:
                        sp.wait_ge(head_done, h + 1)
                        load(h + 2, h % 2)
                for b in range(DIFF_HEADS * TILES, y_d.shape[0] // P):
                    clear(b)
                for s in range(2):
                    sp.wait_ge(stored[s], 16 + 16 * DIFF_HEADS * TILES // 2)
                sp.wait_ge(cleared, 16 * (y_d.shape[0] // P))

            @block.scalar
            def _(act):
                act.dma_start(causal_f[:, :, :], causal_d.rearrange("k p n -> p k n")).then_inc(const_in, 16)
                act.dma_start(ident[:, :], ident_d).then_inc(const_in, 16)
                act.dma_start(g_bc[:, :], row_broadcast(subln_g, DV)).then_inc(const_in, 16)
                for n, a in enumerate(lambdas):
                    act.dma_start(lam_in[:, n, :], row_broadcast(a, HD)).then_inc(const_in, 16)
                act.wait_ge(lam_step, 2)
                act.activation(lam[:, 2:4], lam[:, 0:2], ACT.Exp).then_inc(lam_step, 1)
                act.sem_inc(score_free, 4)
                act.sem_inc(aT_ready, 1)
                act.sem_inc(oT_ready, 1)

                def pair(g):
                    for n in range(SLOTS):
                        if ENDS.get(n - 1) in LONG:
                            m = ENDS[n - 1]
                            a, b = FIRST[m], LAST[m] + 1
                            act.wait_ge(stat_step, g * STAT_ALL + (STAT_END[m] - 4))
                            act.activation(fac[:, :, a:b], under[:, :, a:b], ACT.Exp).then_inc(fac_ready, 1)
                        u = n - LAG
                        if 0 <= u < N:
                            w = STEPS[u][3]
                            act.wait_ge(a_turned, g * N + (u + 1 + RING))
                            act.wait_ge(pv_done, g * N + (u + 1))
                            act.copy(aT[:, u % 2, 0:w], aT_ps[:, 0:w]).then_inc(aT_ready, 1)
                        if n < N:
                            w = STEPS[n][3]
                            act.wait_ge(max_ready, g * N + (n + 1))
                            act.wait_ge(a_turned, g * N + max(n + 1, RING))
                            for c in range(2):
                                act.activation(prob[:, n % RING, c, 0:w], score[:, n % 2, c, 0:w], ACT.Exp,
                                               bias=nmax[:, c, n:n + 1], accum_out=part[:, c, n:n + 1])\
                                    .then_inc(score_free, 1)
                        if n - LAG - 2 in ENDS:
                            m = ENDS[n - LAG - 2]
                            act.wait_ge(pv_done, g * N + (LAST[m] + 3))
                            act.wait_ge(on_ready, g * RUN + (m + 1))
                            act.activation(osq[:, m % 2, :], o_ps[:, m % 2, 0:DV], ACT.Square, scale=1.0 / math.sqrt(DV),
                                           accum_out=oss[:, m % 2:m % 2 + 1]).then_inc(oss_ready, 1)
                        if n - LAG - 4 in ENDS:
                            m = ENDS[n - LAG - 4]
                            act.wait_ge(o_turned, g * RUN + (m + 3))
                            act.wait_ge(stored[m % 2], g * (8 * RUN) + 16 * (m // 2 + 1))
                            act.copy(oT[:, m % 2, :], oT_ps[:, 0:P]).then_inc(oT_ready, 1)

                over_pairs(act, pair)

            @block.gpsimd
            def _(pool):
                pool.memset(power[:, 0:1], -0.5).then_inc(power_ready, 1)
                pool.memset(power[:, 1:2], EPS).then_inc(power_ready, 1)
                pool.memset(zero[:, :], 0.0).then_inc(power_ready, 1)
                pool.wait_ge(power_ready, 3)
                pool.wait_ge(lam_step, 5)

                def pair(g):
                    for n in range(SLOTS):
                        u = n - (LAG - 2)
                        if 0 <= u < N:
                            w, m = STEPS[u][3], STEPS[u][4]
                            pool.wait_ge(stat_step, g * STAT_ALL + STAT_END[m])
                            pool.sem_inc(passed, 1)
                            pool.tensor_scalar(prob[:, u % RING, 1, 0:w], prob[:, u % RING, 1, 0:w],
                                               scale[:, 1, u:u + 1], lam[:, 5:6], ALU.mult, ALU.mult)\
                                .then_inc(scaled, 1)
                        if n - LAG - 2 in ENDS:
                            m = ENDS[n - LAG - 2]
                            s = m % 2
                            pool.wait_ge(oss_ready, g * RUN + (m + 1))
                            pool.tensor_tensor(ovar[:, s:s + 1], oss[:, s:s + 1], power[:, 1:2], ALU.add)\
                                .then_inc(ovar_ready, 1)
                            pool.wait_ge(ovar_ready, g * RUN + (m + 1))
                            pool.tensor_tensor(orstd[:, s:s + 1], ovar[:, s:s + 1], power[:, 0:1], ALU.pow)\
                                .then_inc(orstd_ready, 1)

                over_pairs(pool, pair)

            @block.vector
            def _(dve):
                dve.wait_ge(const_in, 16 * 7)
                dve.tensor_copy(causal[:, :, :], causal_f[:, :, :]).then_inc(mask_ready, 1)
                dve.tensor_scalar(g_out[:, :], g_bc[:, :], 1.0 - LAMBDA_INIT, None, ALU.mult).then_inc(mask_ready, 1)
                pairs = lam_in[:, :, :].rearrange("p (a b) d -> p a b d", b=2)
                dve.tensor_tensor(lam_prod[:, :, :], pairs[:, :, 0, :], pairs[:, :, 1, :], ALU.mult)\
                    .then_inc(lam_step, 1)
                dve.wait_ge(lam_step, 1)
                dve.tensor_reduce(lam[:, 0:2], lam_prod[:, :, :], AX.X, ALU.add).then_inc(lam_step, 1)
                dve.wait_ge(lam_step, 3)
                dve.tensor_tensor(lam[:, 4:5], lam[:, 2:3], lam[:, 3:4], ALU.subtract).then_inc(lam_step, 1)
                dve.wait_ge(lam_step, 4)
                dve.tensor_scalar(lam[:, 5:6], lam[:, 4:5], -1.0, -LAMBDA_INIT, ALU.mult, ALU.add)\
                    .then_inc(lam_step, 1)
                dve.wait_ge(lam_step, 5)
                dve.wait_ge(mask_ready, 2)
                dve.sem_inc(on_ready, 2)

                def pair(g):
                    for n in range(SLOTS):
                        if ENDS.get(n - 1) in LONG:
                            m = ENDS[n - 1]
                            dve.wait_ge(max_ready, g * N + n)
                            dve.tensor_reduce(nrow[:, :, m:m + 1], nmax[:, :, FIRST[m]:n], AX.X, ALU.min)\
                                .then_inc(stat_step, 1)
                            dve.wait_ge(stat_step, g * STAT_ALL + (STAT_END[m] - 5))
                            dve.tensor_tensor(under[:, :, FIRST[m]:n],
                                              nrow[:, :, m:m + 1].to_broadcast([P, 2, n - FIRST[m]]),
                                              nmax[:, :, FIRST[m]:n], ALU.subtract).then_inc(stat_step, 1)
                        u = n - (LAG - 1)
                        if 0 <= u < N:
                            w = STEPS[u][3]
                            dve.wait_ge(scaled, g * N + (u + 1))
                            dve.scalar_tensor_tensor(out=prob[:, u % RING, 0, 0:w], in0=prob[:, u % RING, 0, 0:w],
                                                     scalar=scale[:, 0, u:u + 1],
                                                     in1=prob[:, u % RING, 1, 0:w],
                                                     op0=ALU.mult, op1=ALU.add).then_inc(a_ready, 1)
                        if n < N:
                            w = STEPS[n][3]
                            dve.wait_ge(score_ready, g * N + (n + 1))
                            dve.tensor_reduce(nmax[:, :, n:n + 1], score[:, n % 2, :, 0:w], AX.X, ALU.max,
                                              negate=True).then_inc(max_ready, 1)
                        if n - LAG - 3 in ENDS:
                            m = ENDS[n - LAG - 3]
                            dve.wait_ge(orstd_ready, g * RUN + (m + 1))
                            dve.wait_ge(o_turned, g * RUN + (m + 1))
                            dve.scalar_tensor_tensor(out=onorm[:, m % 2, :], in0=o_ps[:, m % 2, 0:DV],
                                                     scalar=orstd[:, m % 2:m % 2 + 1], in1=g_out[:, :],
                                                     op0=ALU.mult, op1=ALU.mult).then_inc(on_ready, 1)
                        if ENDS.get(n - 1) in LONG:
                            m = ENDS[n - 1]
                            a, b = FIRST[m], LAST[m] + 1
                            end = g * STAT_ALL + STAT_END[m]
                            dve.wait_ge(fac_ready, g * len(LONG) + (LONG.index(m) + 1))
                            dve.wait_ge(score_free, g * (2 * N) + (2 * n + 4))
                            dve.tensor_tensor(part_row[:, :, a:b], part[:, :, a:b], fac[:, :, a:b],
                                              ALU.mult).then_inc(stat_step, 1)
                            dve.wait_ge(stat_step, end - 3)
                            dve.tensor_reduce(total[:, :, m:m + 1], part_row[:, :, a:b], AX.X, ALU.add)\
                                .then_inc(stat_step, 1)
                            dve.wait_ge(stat_step, end - 2)
                            dve.reciprocal(inv[:, :, m:m + 1], total[:, :, m:m + 1]).then_inc(stat_step, 1)
                            dve.wait_ge(stat_step, end - 1)
                            dve.tensor_tensor(scale[:, :, a:b], fac[:, :, a:b],
                                              inv[:, :, m:m + 1].to_broadcast([P, 2, b - a]), ALU.mult)\
                                .then_inc(stat_step, 1)
                        elif n - 1 in ENDS:
                            dve.wait_ge(score_free, g * (2 * N) + (2 * n + 4))
                            dve.reciprocal(scale[:, :, n - 1:n], part[:, :, n - 1:n]).then_inc(stat_step, 1)

                over_pairs(dve, pair)

            @block.tensor
            def _(pe):
                pe.sem_inc(a_turned, RING)
                pe.sem_inc(pv_done, 2)
                pe.sem_inc(o_turned, 2)
                pe.wait_ge(const_in, 16 * 7)
                pe.wait_ge(mask_ready, 2)

                def pair(g):
                    for n in range(SLOTS):
                        if n < N:
                            hh, i, j, w, m = STEPS[n]
                            if n in NEEDS:
                                pe.wait_ge(head_in[hh][NEEDS[n][1]], g * LOAD + LOAD)
                            pe.wait_ge(score_free, g * (2 * N) + (2 * n + 2))
                            diagonal = j + w == (i + 1) * P
                            for c in range(2):
                                q = qT[:, hh, c, i * P:(i + 1) * P]
                                pe.matmul(score[:, n % 2, c, 0:w], q, kT_lo[:, hh, c, j:j + w],
                                          start=True, stop=False)
                                mm = pe.matmul(score[:, n % 2, c, 0:w], q, kT_hi[:, hh, c, j:j + w],
                                               start=False, stop=not diagonal)
                            if diagonal:
                                for c in range(2):
                                    mm = pe.matmul(score[:, n % 2, c, w - P:w], causal[:, 0, :], causal[:, 1, :],
                                                   start=False, stop=True)
                            mm.then_inc(score_ready, 1)
                        u = n - LAG
                        if 0 <= u < N:
                            pe.wait_ge(a_ready, g * N + (u + 1))
                            pe.wait_ge(aT_ready, g * N + (u + 1))
                            for b in range(STEPS[u][3] // P):
                                mm = pe.transpose(aT_ps[:, b * P:(b + 1) * P],
                                                  prob[:, u % RING, 0, b * P:(b + 1) * P], ident[:, :])
                            mm.then_inc(a_turned, 1)
                        if n - LAG - 4 in ENDS:
                            m = ENDS[n - LAG - 4]
                            pe.wait_ge(on_ready, g * RUN + (m + 3))
                            pe.wait_ge(oT_ready, g * RUN + (m + 1))
                            pe.transpose(oT_ps[:, 0:P], onorm[:, m % 2, :], ident[:, :]).then_inc(o_turned, 1)
                        u = n - LAG - 1
                        if 0 <= u < N:
                            hh, i, j, w, m = STEPS[u]
                            if u == FIRST[m]:
                                pe.wait_ge(on_ready, g * RUN + (m + 1))
                            pe.wait_ge(aT_ready, g * N + (u + 2))
                            for b in range(w // P):
                                mm = pe.matmul(o_ps[:, m % 2, 0:DV], aT[:, u % 2, b * P:(b + 1) * P],
                                               v[:, hh, j // P + b, :], start=(u == FIRST[m] and b == 0),
                                               stop=(u == LAST[m] and b == w // P - 1))
                            mm.then_inc(pv_done, 1)
                            if u in HEAD_END:
                                pe.sem_inc(head_done, 1)

                over_pairs(pe, pair)
def window_attention(nc, sem, qk_d, v_d, sinks, ident_d, band_d, mix_d, w_out, wo_hi, wo_lo, wo_raw, wo_split):
    GROUP = SWA_HEADS // KV_HEADS
    WIN = 2 * P
    Q0, K0, V0 = 2 * DIFF_HEADS, 2 * DIFF_HEADS + SWA_HEADS // 2, DIFF_HEADS * 2 * HD

    with ExitStack() as ctx:
        def sb(name, shape, dt=F32):
            return ctx.enter_context(nc.sbuf_tensor(name, shape, dt))

        def ps(name, shape):
            return ctx.enter_context(nc.psum_tensor(name, shape, F32))

        ident = sb("ident3", [P, P])
        band_f = sb("band_f", [P, 5, P])
        band = sb("band", [P, 5, P], BF16)
        sink = sb("sink", [P, SWA_HEADS])
        nsink = sb("nsink", [P, SWA_HEADS])
        k_hi = sb("k_hi", [P, KV_HEADS, P + SEQ], F32R)
        k_lo = sb("k_lo", [P, KV_HEADS, P + SEQ], F32R)
        v = sb("v_swa", [P, TILES + 1, KV_HEADS * HD])
        q = sb("q_swa", [P, 2, SWA_HEADS, P], F32R)
        prob = sb("prob_swa", [P, 2, GROUP, WIN])
        nmax = sb("nmax_swa", [P, 2, GROUP])
        nrow = sb("nrow_swa", [P, 2, GROUP])
        part = sb("part_swa", [P, 2, GROUP])
        over = sb("over_swa", [P, 2, GROUP])
        esink = sb("esink", [P, 2, GROUP])
        total = sb("total_swa", [P, 2, GROUP])
        inv = sb("inv_swa", [P, 2, GROUP])
        pT = sb("pT_swa", [P, 2, GROUP, WIN])
        o = sb("o_swa", [P, 2, SWA_HEADS * HD])
        oT = sb("oT_swa", [P, 2, SWA_HEADS // 2, P])

        score = ps("score_swa", [P, 2, GROUP, WIN])
        pT_ps = ps("pT_ps_swa", [P, GROUP, WIN])
        o_ps = ps("o_ps_swa", [P, 512])
        oT_ps = ps("oT_ps_swa", [P, SWA_HEADS // 2, P])

        const_in = sem("p3_const_in")
        mask_ready = sem("p3_mask_ready")
        kv_in = [sem("p3_kv_in0"), sem("p3_kv_in1")]
        wo_in = [sem("p3_wo_in0"), sem("p3_wo_in1")]
        wo_high = sem("p3_wo_high")
        q_in = [sem("p3_q_in0"), sem("p3_q_in1")]
        score_ready = sem("p3_score_ready")
        score_free = sem("p3_score_free")
        nmax_ready = sem("p3_nmax_ready")
        nrow_ready = sem("p3_nrow_ready")
        exp_ready = sem("p3_exp_ready")
        total_ready = sem("p3_total_ready")
        inv_ready = sem("p3_inv_ready")
        p_turned = sem("p3_p_turned")
        pT_ready = sem("p3_pT_ready")
        pv_done = sem("p3_pv_done")
        o_ready = sem("p3_o_ready")
        o_turned = sem("p3_o_turned")
        oT_ready = sem("p3_oT_ready")
        stored = [sem("p3_stored0"), sem("p3_stored1")]

        def tile_pairs(eng, tile, between=None):
            for s in range(2):
                tile(s, s)
            if between:
                between()
            with eng.Fori(1, TILES // 2) as i:
                for s in range(2):
                    tile(i * 2 + s, s)

        with nc.Block() as block:
            @block.sync
            def _(sp):
                for s in range(2):
                    sp.sem_inc(stored[s], 16)
                sp.dma_start(band_f[:, :, :], band_d.rearrange("k p n -> p k n")).then_inc(const_in, 16)
                sp.dma_start(ident[:, :], ident_d).then_inc(const_in, 16)
                sp.dma_start(sink[:, :], row_broadcast(sinks, SWA_HEADS)).then_inc(const_in, 16)

                def load(t, s):
                    for half in range(2):
                        sp.dma_start(q[half * HD:(half + 1) * HD, s, :, :].bitcast(F32),
                                     qk_d[half, Q0:Q0 + SWA_HEADS // 2, :, bass.ts(t, P)]
                                     .rearrange("b (h d) t -> d (b h) t", d=HD)).then_inc(q_in[s], 16)

                load(0, 0)
                for n, (t0, t1) in enumerate([(0, 2), (2, TILES)]):
                    at, keys = slice(t0 * P, t1 * P), slice((t0 + 1) * P, (t1 + 1) * P)
                    for half in range(2):
                        to = slice(half * HD, (half + 1) * HD)
                        for part, k in ((0, k_hi), (1, k_lo)):
                            sp.dma_start(k[to, :, keys].bitcast(F32),
                                         qk_d[part, K0, :, at].rearrange("(g d) t -> d g t", d=HD)).then_inc(kv_in[n], 16)
                    sp.dma_start(v[:, t0 + 1:t1 + 1, :],
                                 v_d[at, V0:V0 + KV_HEADS * HD].rearrange("(t p) d -> p t d", p=P))\
                        .then_inc(kv_in[n], 16)
                load(1, 1)

                def store(t, s):
                    sp.wait_ge(oT_ready, t + 1)
                    sp.dma_start(mix_d[DIFF_HEADS:, :, bass.ts(t, P)].rearrange("b p t -> p b t"), oT[:, s, :, :])\
                        .then_inc(stored[s], 16)

                def tile(t, s):
                    sp.wait_ge(score_ready, t * 2 - 2)
                    load(t, s)
                    if not (static(t) and t < 3):
                        store(t - 3, 1 - s)

                for t in (2, 3):
                    tile(t, t % 2)
                with sp.Fori(2, TILES // 2) as i:
                    for s in range(2):
                        tile(i * 2 + s, s)
                for t in range(TILES - 3, TILES):
                    store(t, t % 2)
                for s in range(2):
                    sp.wait_ge(stored[s], 16 + 16 * TILES // 2)

            @block.gpsimd
            def _(pool):
                wv = w_out.rearrange("(k p) n -> p k n", p=P)

                def load_w(k):
                    pool.dma_start(wo_raw[:, k % 2, :], wv[:, k, :]).then_inc(wo_in[k % 2], 16)

                load_w(0)
                load_w(1)
                for k in range(KD):
                    pool.wait_ge(wo_in[k % 2], 16 * (k // 2) + 16)
                    pool.tensor_copy(wo_hi[:, k, :], wo_raw[:, k % 2, :]).then_inc(wo_high, 1)
                    pool.wait_ge(wo_high, k + 1)
                    pool.tensor_tensor(wo_lo[:, k, :], wo_raw[:, k % 2, :], wo_hi[:, k, :], ALU.subtract)\
                        .then_inc(wo_split, 1)
                    if k + 2 < KD:
                        pool.wait_ge(wo_split, k + 1)
                        load_w(k + 2)

            @block.vector
            def _(dve):
                dve.memset(k_hi[:, :, 0:P].bitcast(F32), 0.0)
                dve.memset(k_lo[:, :, 0:P].bitcast(F32), 0.0)
                dve.memset(v[:, 0, :], 0.0).then_inc(mask_ready, 1)
                dve.wait_ge(const_in, 16 * 3)
                dve.tensor_copy(band[:, :, :], band_f[:, :, :]).then_inc(mask_ready, 1)
                dve.tensor_scalar(nsink[:, :], sink[:, :], -1.0, None, ALU.mult).then_inc(mask_ready, 1)
                dve.wait_ge(mask_ready, 3)
                dve.sem_inc(pT_ready, 1)
                dve.sem_inc(o_ready, 1)

                def finish(t, g):
                    step, b = t * 2 + g, g
                    dve.wait_ge(p_turned, step + 1)
                    dve.tensor_copy(pT[:, b, 0:2, :], pT_ps[:, 0:2, :]).then_inc(pT_ready, 1)
                    dve.wait_ge(exp_ready, step + 1)
                    dve.tensor_tensor(total[:, b, :], part[:, b, :], esink[:, b, :], ALU.add)\
                        .then_inc(total_ready, 1)
                    dve.wait_ge(total_ready, step + 1)
                    dve.reciprocal(inv[:, b, :], total[:, b, :]).then_inc(inv_ready, 1)
                    dve.wait_ge(inv_ready, step + 1)

                def output(t, g, s):
                    step = t * 2 + g
                    dve.wait_ge(pv_done, step + 1)
                    dve.wait_ge(o_turned, t + 1)
                    dve.tensor_tensor(
                        o[:, s, g * GROUP * HD:(g + 1) * GROUP * HD].rearrange("p (h d) -> p h d", d=HD),
                        o_ps[:, 0:GROUP * HD].rearrange("p (h d) -> p h d", d=HD),
                        inv[:, g, :].unsqueeze(2).to_broadcast([P, GROUP, HD]), ALU.mult).then_inc(o_ready, 1)

                def tile(t, s):
                    for g in range(KV_HEADS):
                        step = t * 2 + g
                        heads = slice(g * GROUP, (g + 1) * GROUP)
                        dve.wait_ge(score_ready, step + 1)
                        dve.tensor_reduce(nmax[:, g, :], score[:, g, :, :], AX.X, ALU.max, negate=True)\
                            .then_inc(nmax_ready, 1)
                        dve.wait_ge(nmax_ready, step + 1)
                        dve.tensor_tensor(nrow[:, g, :], nmax[:, g, :], nsink[:, heads], ALU.min)\
                            .then_inc(nrow_ready, 1)
                        dve.wait_ge(nrow_ready, step * 2 + 1)
                        dve.tensor_tensor(over[:, g, :], nrow[:, g, :], sink[:, heads], ALU.add)\
                            .then_inc(nrow_ready, 1)
                        if not (static(t) and t == 0 and g == 0):
                            finish(*((t, 0) if g else (t - 1, 1)))
                        if not (static(t) and t == 0):
                            output(t - 1, g, 1 - s)

                tile_pairs(dve, tile)
                finish(TILES - 1, 1)
                for g in range(KV_HEADS):
                    output(TILES - 1, g, 1)

            @block.scalar
            def _(act):
                act.sem_inc(score_free, 2 * GROUP)
                act.sem_inc(pT_ready, 1)

                def copy_pT(t, g):
                    step = t * 2 + g
                    act.wait_ge(p_turned, step + 1)
                    act.copy(pT[:, g, 2:4, :], pT_ps[:, 2:4, :]).then_inc(pT_ready, 1)

                def copy_oT(t, s):
                    act.wait_ge(o_turned, t + 3)
                    act.wait_ge(stored[s], (t - s) * 8 + 16)
                    act.copy(oT[:, s, :, :], oT_ps[:, :, :]).then_inc(oT_ready, 1)

                def tile(t, s):
                    for g in range(KV_HEADS):
                        step = t * 2 + g
                        if not (static(t) and t == 0 and g == 0):
                            pt, pg = (t, 0) if g else (t - 1, 1)
                            copy_pT(pt, pg)
                        act.wait_ge(nrow_ready, step * 2 + 2)
                        if not (static(t) and t == 0):
                            act.wait_ge(p_turned, step - 1)
                            act.wait_ge(total_ready, step - 1)
                        for hd in range(GROUP):
                            act.activation(prob[:, g, hd, :], score[:, g, hd, :], ACT.Exp,
                                               bias=nrow[:, g, hd:hd + 1], accum_out=part[:, g, hd:hd + 1])\
                                .then_inc(score_free, 1)
                        act.activation(esink[:, g, :], over[:, g, :], ACT.Exp).then_inc(exp_ready, 1)
                        if g == 0 and not (static(t) and t < 2):
                            copy_oT(t - 2, s)

                tile_pairs(act, tile)
                copy_pT(TILES - 1, 1)
                copy_oT(TILES - 2, 0)
                copy_oT(TILES - 1, 1)

            @block.tensor
            def _(pe):
                pe.sem_inc(o_turned, 2)
                pe.wait_ge(const_in, 16 * 3)
                pe.wait_ge(mask_ready, 3)
                pe.wait_ge(kv_in[0], 16 * 5)

                def turn_p(t, g):
                    step = t * 2 + g
                    pe.wait_ge(score_free, (step + 3) * GROUP)
                    pe.wait_ge(pT_ready, step * 2 + 2)
                    for hd in range(GROUP):
                        for b in range(2):
                            mm = pe.transpose(pT_ps[:, hd, b * P:(b + 1) * P], prob[:, g, hd, b * P:(b + 1) * P],
                                              ident[:, :])
                    mm.then_inc(p_turned, 1)

                def times_v(t, g):
                    step = t * 2 + g
                    pe.wait_ge(pT_ready, step * 2 + 4)
                    pe.wait_ge(o_ready, step + 1)
                    for hd in range(GROUP):
                        for b in range(2):
                            vv = v[:, bass.ds(t + b, 1), g * HD:(g + 1) * HD]
                            mm = pe.matmul(o_ps[:, hd * HD:(hd + 1) * HD], pT[:, g, hd, b * P:(b + 1) * P], vv,
                                           start=(b == 0), stop=(b == 1))
                    mm.then_inc(pv_done, 1)

                def turn_o(t, s):
                    pe.wait_ge(o_ready, t * 2 + 3)
                    if not (static(t) and t == 0):
                        pe.wait_ge(oT_ready, t)
                    for b in range(SWA_HEADS // 2):
                        mm = pe.transpose(oT_ps[:, b, :], o[:, s, b * P:(b + 1) * P], ident[:, :])
                    mm.then_inc(o_turned, 1)

                def tile(t, s):
                    for g in range(KV_HEADS):
                        step = t * 2 + g
                        if g == 0:
                            pe.wait_ge(q_in[s], (t - s) * 16 + 32)
                        pe.wait_ge(score_free, (step + 1) * GROUP)
                        for hd in range(GROUP):
                            for k in (k_lo, k_hi):
                                pe.matmul(score[:, g, hd, :], q[:, s, g * GROUP + hd, :], k[:, g, bass.ds(t * P, WIN)],
                                          start=(k is k_lo), stop=False)
                            mask = band[:, 1:3, :] if static(t) and t == 0 else band[:, 3:5, :]
                            mm = pe.matmul(score[:, g, hd, :], band[:, 0, :], mask, start=False, stop=True)
                        mm.then_inc(score_ready, 1)
                        if g == 0 and not (static(t) and t < 2):
                            turn_o(t - 2, s)
                        if not (static(t) and t == 0 and g == 0):
                            turn_p(*((t, 0) if g else (t - 1, 1)))
                        if not (static(t) and t == 0):
                            times_v(t - 1, g)

                tile_pairs(pe, tile, lambda: pe.wait_ge(kv_in[1], 16 * 5))
                turn_p(TILES - 1, 1)
                times_v(TILES - 1, 0)
                times_v(TILES - 1, 1)
                turn_o(TILES - 2, 0)
                turn_o(TILES - 1, 1)
N_GROUPS = 4
N_EXPERTS = 32
PER_GROUP = N_EXPERTS // N_GROUPS
LOGITS = N_GROUPS + N_EXPERTS


def output_projection(nc, sem, x, mix_d, wo_hi, wo_lo, wo_split, norm2_g, w_rg, b_rg, w_re, b_re, ident_d, h_sb, logits, n2_d):
    with ExitStack() as ctx:
        def sb(name, shape, dt=F32):
            return ctx.enter_context(nc.sbuf_tensor(name, shape, dt))

        def ps(name, shape):
            return ctx.enter_context(nc.psum_tensor(name, shape, F32))

        ident = sb("ident4", [P, P])
        wr_sb = sb("w_router_sb", [P, KD, LOGITS])
        br_sb = sb("b_router_sb", [P, LOGITS])
        g_bc = sb("g2_bc", [P, D])
        power = sb("power4", [P, 2])
        mixT = sb("mixT", [P, 2, KD, P])
        mixT_hi = sb("mixT_hi", [P, 2, KD, P], F32R)
        mixT_lo = sb("mixT_lo", [P, 2, KD, P], F32R)
        x_sb = sb("x4_sb", [P, 2, D])
        sq = sb("sq4", [P, 1, D], BF16)
        ss = sb("ss4", [P, 2])
        var = sb("var4", [P, 2])
        rstd = sb("rstd4", [P, 2])
        n2 = sb("n2", [P, 2, D])
        n2T = sb("n2T", [P, 2, KD, P])

        proj = ps("proj4", [P, 2, 2, 512])
        n2t_ps = ps("n2t_ps", [P, KD, P])
        lg_ps = ps("lg_ps", [P, LOGITS])

        const_in = sem("p4_const_in")
        power_ready = sem("p4_power_ready")
        tile_in = [sem("p4_tile_in0"), sem("p4_tile_in1")]
        mix_high = sem("p4_mix_high")
        mix_split = sem("p4_mix_split")
        proj_ready = sem("p4_proj_ready")
        h_ready = sem("p4_h_ready")
        ss_ready = sem("p4_ss_ready")
        var_ready = sem("p4_var_ready")
        rstd_ready = sem("p4_rstd_ready")
        n2_ready = sem("p4_n2_ready")
        n2_turned = sem("p4_n2_turned")
        n2T_ready = sem("p4_n2T_ready")
        lg_ready = sem("p4_lg_ready")
        lg_done = sem("p4_lg_done")
        stored = [sem("p4_stored0"), sem("p4_stored1")]

        with nc.Block() as block:
            @block.sync
            def _(sp):
                def load(t, s):
                    sp.dma_start(mixT[:, s, :, :], mix_d[:, :, bass.ts(t, P)].rearrange("b p t -> p b t"))\
                        .then_inc(tile_in[s], 16)
                    sp.dma_start(x_sb[:, s, :], x[bass.ts(t, P), :]).then_inc(tile_in[s], 16)

                load(0, 0)
                load(1, 1)
                sp.dma_start(ident[:, :], ident_d).then_inc(const_in, 16)
                sp.dma_start(g_bc[:, :], row_broadcast(norm2_g, D)).then_inc(const_in, 16)
                sp.dma_start(wr_sb[:, :, 0:N_GROUPS], w_rg.rearrange("(k p) n -> p k n", p=P)).then_inc(const_in, 16)
                sp.dma_start(wr_sb[:, :, N_GROUPS:], w_re.rearrange("(k p) n -> p k n", p=P)).then_inc(const_in, 16)
                sp.dma_start(br_sb[:, 0:N_GROUPS], row_broadcast(b_rg, N_GROUPS)).then_inc(const_in, 16)
                sp.dma_start(br_sb[:, N_GROUPS:], row_broadcast(b_re, N_EXPERTS)).then_inc(const_in, 16)

                def store(t, s):
                    sp.wait_ge(n2_ready, t + 1)
                    sp.dma_start(n2_d[bass.ts(t, P), :], n2[:, s, :]).then_inc(stored[s], 16)

                def tile(t, s):
                    if not (static(t) and t >= TILES - 2):
                        sp.wait_ge(h_ready, t + 1)
                        load(t + 2, s)
                    store(t, s)

                over_pairs(sp, tile)
                for s in range(2):
                    sp.wait_ge(stored[s], 8 * TILES)

            @block.vector
            def _(dve):
                def residual(t, s):
                    dve.wait_ge(proj_ready, t + 1)
                    h = h_sb[:, t:t + 1, :] if static(t) else h_sb[:, bass.ds(t, 1), :]
                    dve.tensor_tensor(h, proj[:, s, :, :].rearrange("p (o a) b -> p o (a b)", o=1),
                                      x_sb[:, s:s + 1, :], ALU.add).then_inc(h_ready, 1)

                def normalize(t, s):
                    dve.wait_ge(rstd_ready, t + 1)
                    if not (static(t) and t < 2):
                        dve.wait_ge(n2_turned, t - 1)
                        dve.wait_ge(stored[s], (t - s) * 8)
                    h = h_sb[:, t:t + 1, :] if static(t) else h_sb[:, bass.ds(t, 1), :]
                    dve.scalar_tensor_tensor(out=n2[:, s:s + 1, :], in0=h, scalar=rstd[:, s:s + 1],
                                             in1=g_bc[:, :].rearrange("p (o a) -> p o a", o=1),
                                             op0=ALU.mult, op1=ALU.mult).then_inc(n2_ready, 1)

                def take_logits(t, s):
                    dve.wait_ge(lg_ready, t + 1)
                    out = logits[:, t:t + 1, :] if static(t) else logits[:, bass.ds(t, 1), :]
                    dve.tensor_tensor(out, lg_ps[:, :].rearrange("p (o a) -> p o a", o=1),
                                      br_sb[:, :].rearrange("p (o a) -> p o a", o=1), ALU.add).then_inc(lg_done, 1)

                def low_mix(t, s):
                    dve.wait_ge(mix_high, t + 1)
                    dve.tensor_tensor(mixT_lo[:, s, :, :], mixT[:, s, :, :], mixT_hi[:, s, :, :], ALU.subtract)\
                        .then_inc(mix_split, 1)

                def tile(t, s):
                    residual(t, s)
                    if static(t) and t == 0:
                        dve.wait_ge(const_in, 96)
                    dve.wait_ge(h_ready, t + 1)
                    normalize(t, s)
                    if not (static(t) and t >= TILES - 2):
                        low_mix(t + 2, s)
                    if not (static(t) and t == 0):
                        take_logits(t - 1, 1 - s)

                low_mix(0, 0)
                low_mix(1, 1)
                over_pairs(dve, tile)
                take_logits(TILES - 1, 1)

            @block.scalar
            def _(act):
                def high_mix(t, s):
                    act.wait_ge(tile_in[s], (t - s) * 16 + 32)
                    if not (static(t) and t < 2):
                        act.wait_ge(proj_ready, t - 1)
                    act.copy(mixT_hi[:, s, :, :], mixT[:, s, :, :]).then_inc(mix_high, 1)

                def tile(t, s):
                    act.wait_ge(h_ready, t + 1)
                    if not (static(t) and t < 2):
                        act.wait_ge(n2_ready, t - 1)
                    h = h_sb[:, t:t + 1, :] if static(t) else h_sb[:, bass.ds(t, 1), :]
                    act.activation(sq[:, :, :], h, ACT.Square, scale=1.0 / math.sqrt(D),
                                   accum_out=ss[:, s:s + 1]).then_inc(ss_ready, 1)
                    if not (static(t) and t >= TILES - 2):
                        high_mix(t + 2, s)
                    act.wait_ge(n2_turned, t + 1)
                    act.copy(n2T[:, s, :, :], n2t_ps[:, :, :]).then_inc(n2T_ready, 1)

                high_mix(0, 0)
                high_mix(1, 1)
                over_pairs(act, tile)

            @block.gpsimd
            def _(pool):
                pool.memset(power[:, 0:1], -0.5).then_inc(power_ready, 1)
                pool.memset(power[:, 1:2], EPS).then_inc(power_ready, 1)
                pool.wait_ge(power_ready, 2)

                def tile(t, s):
                    pool.wait_ge(ss_ready, t + 1)
                    pool.tensor_tensor(var[:, s:s + 1], ss[:, s:s + 1], power[:, 1:2], ALU.add).then_inc(var_ready, 1)
                    pool.wait_ge(var_ready, t + 1)
                    pool.tensor_tensor(rstd[:, s:s + 1], var[:, s:s + 1], power[:, 0:1], ALU.pow)\
                        .then_inc(rstd_ready, 1)

                over_pairs(pool, tile)

            @block.tensor
            def _(pe):
                def project(t, s):
                    pe.wait_ge(mix_split, t + 1)
                    if static(t) and t == 0:
                        pe.wait_ge(wo_split, KD)
                    if not (static(t) and t < 2):
                        pe.wait_ge(h_ready, t - 1)
                    for k in range(KD):
                        for half in range(2):
                            cols = slice(half * 512, (half + 1) * 512)
                            mm = split_product(pe, proj[:, s, half, :], mixT_hi[:, s, k, :], mixT_lo[:, s, k, :],
                                               wo_hi[:, k, cols], wo_lo[:, k, cols], k == 0, k == KD - 1)
                    mm.then_inc(proj_ready, 1)

                def turn(t, s):
                    pe.wait_ge(n2_ready, t + 1)
                    if not (static(t) and t == 0):
                        pe.wait_ge(n2T_ready, t)
                    for k in range(KD):
                        mm = pe.transpose(n2t_ps[:, k, :], n2[:, s, k * P:(k + 1) * P], ident[:, :])
                    mm.then_inc(n2_turned, 1)

                def route(t, s):
                    pe.wait_ge(n2T_ready, t + 1)
                    if not (static(t) and t == 0):
                        pe.wait_ge(lg_done, t)
                    for k in range(KD):
                        mm = pe.matmul(lg_ps[:, :], n2T[:, s, k, :], wr_sb[:, k, :], start=(k == 0), stop=(k == KD - 1))
                    mm.then_inc(lg_ready, 1)

                def tile(t, s):
                    project(t, s)
                    if static(t) and t == 0:
                        pe.wait_ge(const_in, 96)
                    else:
                        turn(t - 1, 1 - s)
                    if not (static(t) and t <= 1):
                        route(t - 2, s)

                over_pairs(pe, tile)
                turn(TILES - 1, 1)
                route(TILES - 2, 0)
                route(TILES - 1, 1)
BLOCKS = 64
MAX_TOK = 1e30
FF = 512
KF = FF // P

PIECES = 12
PW = 1024
RAW = 6
HALF = FF // 2
HI_BY = {k: "dve" if k < 3 else "act" for k in range(PIECES)}
LO_BY = {k: "pool" if k in (1, 4, 7, 9) else "dve" for k in range(PIECES)}
assert PIECES % RAW == 0


def piece(w, k):
    if k < 4:
        return w[0][:, 2 * k:2 * k + 2, :]
    if k < 8:
        half, rows = (k - 4) // 2, (k - 4) % 2
        return w[1][:, 4 * rows:4 * rows + 4, half * HALF:(half + 1) * HALF]
    return w[2][:, k - 8:k - 7, :]


def raw_piece(raw, k):
    return raw[:, k % RAW, :].rearrange("p (a b) -> p a b", a=(2, 4, 1)[k // 4])


def load_piece(eng, w_d, raw, raw_in, e, k):
    src = [w[bass.ds(e, 1), :, :].rearrange("o (k p) n -> p (o k) n", p=P) for w in w_d]
    eng.dma_start(raw_piece(raw, k), piece(src, k)).then_inc(raw_in[k % RAW], 16)


def part_ready(by, ready, e, k):
    own = [n for n in range(PIECES) if by[n] == by[k]]
    return ready[by[k]], e * len(own) + (own.index(k) + 1)


def routing(nc, sem, logits, tables_d, gates, dest, slots, starts, ends, w_d, wg, wu, raw, raw_in,
            hi_ready, lo_ready):
    G, E, PG = N_GROUPS, N_EXPERTS, PER_GROUP
    T = TILES
    RING = 8
    VDIFF = 23
    BEFORE = VDIFF + 2 + T
    NBLK = BEFORE + 3
    with ExitStack() as ctx:
        def sb(name, shape, dt=F32):
            return ctx.enter_context(nc.sbuf_tensor(name, shape, dt))

        def ps(name, shape):
            return ctx.enter_context(nc.psum_tensor(name, shape, F32))

        tri = sb("tri", [P, P])
        ones = sb("ones5", [P, P])
        iota = sb("iota5", [P, P])
        tok = sb("tok5", [P, P])
        gmax = sb("gmax", [P, T])
        gdiff = sb("gdiff", [P, T, G])
        gexp = sb("gexp", [P, T, G])
        gsum = sb("gsum", [P, T])
        ptop = sb("ptop", [P, T])
        geq = sb("geq", [P, T, G])
        gidx = sb("gidx", [P, T])
        ghot = sb("ghot", [P, T, G])
        el = sb("el", [P, T, E])
        eq = sb("eq", [P, T, E])
        top = sb("top", [P, 2, T])
        eidx = sb("eidx", [P, 2, T])
        hot = sb("hot", [P, 2, T, E])
        both = sb("both", [P, T, E])
        before = sb("before", [P, T + 1, E])
        vdiff = sb("vdiff", [P, T])
        vexp = sb("vexp", [P, T])
        vsum = sb("vsum", [P, T])
        vinv = sb("vinv", [P, T])
        rank_i = sb("rank_i", [P, T, E], I32)
        pos_i = sb("pos_i", [P, T, E], I32)
        blk_i = sb("blk_i", [P, T, E], I32)
        posf = sb("posf", [P, T, E])
        blkf = sb("blkf", [P, T, E])
        count_i = sb("count_i", [P, 1], I32)
        nb_i = sb("nb_i", [P, 1], I32)
        nb = sb("nb", [P, 1])
        start_row = sb("start_row", [P, E + 1])
        end_row = sb("end_row", [P, E])
        prod = sb("prod5", [P, 2, T, E])
        pos_k = sb("pos_k", [P, 2, T])
        blk_k = sb("blk_k", [P, 2, T])
        destf = sb("destf", [P, 2, T])
        at_pos = sb("at_pos", [P, RING, P])
        at_blk = sb("at_blk", [P, RING, BLOCKS + 1])

        rank_ps = ps("rank_ps", [P, T * E])
        count_ps = ps("count_ps", [P, 1])
        start_ps = ps("start_ps", [P, E + 1])
        slot_ps = ps("slot_ps", [P, BLOCKS + 1])

        const_in = sem("p5_const_in")
        step = sem("p5_step")
        act_step = sem("p5_act_step")
        pe_step = sem("p5_pe_step")
        pair_ready = sem("p5_pair_ready")
        pair_used = sem("p5_pair_used")

        with nc.Block() as block:
            @block.sync
            def _(sp):
                for n, a in enumerate((tri, ones, iota, tok)):
                    sp.dma_start(a[:, :], tables_d[n, :, :]).then_inc(const_in, 16)
                for k in range(PIECES):
                    if k >= RAW:
                        sp.wait_ge(*part_ready(LO_BY, lo_ready, 0, k - RAW))
                    load_piece(sp, w_d, raw, raw_in, 0, k)

            @block.gpsimd
            def _(pool):
                for k in range(8):
                    pool.wait_ge(*part_ready(HI_BY, hi_ready, 0, k))
                    pool.tensor_tensor(piece((wg[1], wu[1]), k), raw_piece(raw, k), piece((wg[0], wu[0]), k),
                                       ALU.subtract).then_inc(lo_ready[LO_BY[k]], 1)

            @block.scalar
            def _(act):
                def high(first, last):
                    for k in range(first, last):
                        act.wait_ge(raw_in[k % RAW], 16 * (k // RAW) + 16)
                        act.copy(piece((wg[0], wu[0]), k), raw_piece(raw, k)).then_inc(hi_ready[HI_BY[k]], 1)

                act.wait_ge(step, 2)
                act.activation(gexp[:, :, :], gdiff[:, :, :], ACT.Exp).then_inc(act_step, 1)
                high(0, 8)
                act.wait_ge(step, VDIFF)
                act.activation(vexp[:, :], vdiff[:, :], ACT.Exp).then_inc(act_step, 1)

            @block.tensor
            def _(pe):
                pe.wait_ge(const_in, 64)
                pe.wait_ge(step, BEFORE)
                pe.matmul(rank_ps[:, :], tri[:, :], both[:, :, :], start=True, stop=False)
                pe.matmul(rank_ps[:, :], ones[:, :], before[:, 0:T, :], start=False, stop=True).then_inc(pe_step, 1)
                pe.matmul(count_ps[0:E, :], before[:, T, :], ones[:, 0:1], start=True, stop=True).then_inc(pe_step, 1)
                pe.wait_ge(step, NBLK)
                pe.matmul(start_ps[:, :], nb[0:E, :].to_broadcast([E, P]), tri[0:E, 0:E + 1], start=True, stop=True)\
                    .then_inc(pe_step, 1)
                for n in range(2 * T):
                    pe.wait_ge(pair_ready, n + 1)
                    pe.matmul(slot_ps[:, :], at_pos[:, n % RING, :], at_blk[:, n % RING, :], start=(n == 0),
                              stop=(n == 2 * T - 1)).then_inc(pair_used, 1)

            @block.vector
            def _(dve):
                done = [0]

                def then(ins):
                    done[0] += 1
                    ins.then_inc(step, 1)
                    dve.wait_ge(step, done[0])

                gl = logits[:, :, 0:G]

                def bc(a, n):
                    return a.unsqueeze(2).to_broadcast([P, T, n])

                def iota_bc(n):
                    return iota[:, 0:n].unsqueeze(1).to_broadcast([P, T, n])

                dve.wait_ge(const_in, 64)
                then(dve.tensor_reduce(gmax[:, :], gl, AX.X, ALU.max))
                then(dve.tensor_tensor(gdiff[:, :, :], gl, bc(gmax[:, :], G), ALU.subtract))
                then(dve.tensor_tensor(geq[:, :, :], gl, bc(gmax[:, :], G), ALU.is_equal))
                then(dve.scalar_tensor_tensor(out=geq[:, :, :], in0=geq[:, :, :], scalar=-float(P),
                                              in1=iota_bc(G), op0=ALU.mult, op1=ALU.add))
                then(dve.tensor_reduce(gidx[:, :], geq[:, :, :], AX.X, ALU.min))
                then(dve.tensor_scalar(gidx[:, :], gidx[:, :], float(P), None, ALU.add))
                then(dve.tensor_tensor(ghot[:, :, :], iota_bc(G), bc(gidx[:, :], G), ALU.is_equal))
                then(dve.tensor_scalar(ghot[:, :, :], ghot[:, :, :], MAX_TOK, -MAX_TOK, ALU.mult, ALU.add))
                then(dve.tensor_tensor(el[:, :, :].rearrange("p t (g e) -> p t g e", g=G),
                                       logits[:, :, G:].rearrange("p t (g e) -> p t g e", g=G),
                                       ghot[:, :, :].unsqueeze(3).to_broadcast([P, T, G, PG]), ALU.add))
                for k in range(2):
                    then(dve.tensor_reduce(top[:, k, :], el[:, :, :], AX.X, ALU.max))
                    then(dve.tensor_tensor(eq[:, :, :], el[:, :, :], bc(top[:, k, :], E), ALU.is_equal))
                    then(dve.scalar_tensor_tensor(out=eq[:, :, :], in0=eq[:, :, :], scalar=-float(P),
                                                  in1=iota_bc(E), op0=ALU.mult, op1=ALU.add))
                    then(dve.tensor_reduce(eidx[:, k, :], eq[:, :, :], AX.X, ALU.min))
                    then(dve.tensor_scalar(eidx[:, k, :], eidx[:, k, :], float(P), None, ALU.add))
                    then(dve.tensor_tensor(hot[:, k, :, :], iota_bc(E), bc(eidx[:, k, :], E), ALU.is_equal))
                    if k == 0:
                        then(dve.scalar_tensor_tensor(out=el[:, :, :], in0=hot[:, 0, :, :], scalar=-2 * MAX_TOK,
                                                      in1=el[:, :, :], op0=ALU.mult, op1=ALU.add))
                then(dve.tensor_tensor(vdiff[:, :], top[:, 1, :], top[:, 0, :], ALU.subtract))
                assert done[0] == VDIFF
                then(dve.tensor_tensor(both[:, :, :], hot[:, 0, :, :], hot[:, 1, :, :], ALU.add))
                then(dve.memset(before[:, 0, :], 0.0))
                for t in range(T):
                    then(dve.tensor_tensor(before[:, t + 1, :], before[:, t, :], both[:, t, :], ALU.add))
                assert done[0] == BEFORE
                dve.wait_ge(pe_step, 2)
                then(dve.tensor_scalar(count_i[0:E, :], count_ps[0:E, :], float(P - 1), None, ALU.add))
                then(dve.tensor_scalar(nb_i[0:E, :], count_i[0:E, :], 7, None, ALU.arith_shift_right))
                then(dve.tensor_scalar(nb[0:E, :], nb_i[0:E, :], 1.0, None, ALU.max))
                assert done[0] == NBLK
                then(dve.tensor_copy(rank_i[:, :, :], rank_ps[:, :].rearrange("p (t e) -> p t e", t=T)))
                then(dve.tensor_scalar(pos_i[:, :, :], rank_i[:, :, :], P - 1, None, ALU.bitwise_and))
                then(dve.tensor_scalar(blk_i[:, :, :], rank_i[:, :, :], 7, None, ALU.arith_shift_right))
                then(dve.tensor_copy(posf[:, :, :], pos_i[:, :, :]))
                dve.wait_ge(pe_step, 3)
                then(dve.tensor_copy(start_row[:, :], start_ps[:, :]))
                then(dve.tensor_copy(starts[:, :], start_row[:, :]))
                then(dve.tensor_scalar(end_row[:, :], start_row[:, 1:], -1.0, None, ALU.add))
                then(dve.tensor_copy(ends[:, :], end_row[:, :]))
                then(dve.tensor_tensor(blkf[:, :, :], blk_i[:, :, :],
                                       start_row[:, 0:E].unsqueeze(1).to_broadcast([P, T, E]), ALU.add))
                for a, out in ((posf, pos_k), (blkf, blk_k)):
                    then(dve.tensor_tensor(prod[:, :, :, :], hot[:, :, :, :],
                                           a[:, :, :].unsqueeze(1).to_broadcast([P, 2, T, E]), ALU.mult))
                    then(dve.tensor_reduce(out[:, :, :], prod[:, :, :, :], AX.X, ALU.add))
                then(dve.scalar_tensor_tensor(out=destf[:, :, :], in0=blk_k[:, :, :], scalar=float(P),
                                              in1=pos_k[:, :, :], op0=ALU.mult, op1=ALU.add))
                then(dve.tensor_copy(dest[:, :, :], destf[:, :, :]))
                for n in range(2 * T):
                    k, t = n % 2, n // 2
                    if n >= RING:
                        dve.wait_ge(pair_used, n - RING + 1)
                    dve.tensor_scalar(at_pos[:, n % RING, :], iota[:, :], pos_k[:, k, t:t + 1], None, ALU.is_equal)
                    dve.tensor_scalar(at_blk[:, n % RING, :], iota[:, 0:BLOCKS + 1], blk_k[:, k, t:t + 1],
                                      tok[:, t:t + 1], ALU.is_equal, ALU.mult).then_inc(pair_ready, 1)
                dve.wait_ge(act_step, 2)
                then(dve.tensor_reduce(gsum[:, :], gexp[:, :, :], AX.X, ALU.add))
                then(dve.reciprocal(ptop[:, :], gsum[:, :]))
                then(dve.tensor_scalar(vsum[:, :], vexp[:, :], 1.0, None, ALU.add))
                then(dve.reciprocal(vinv[:, :], vsum[:, :]))
                then(dve.tensor_tensor(gates[:, 0, :], ptop[:, :], vinv[:, :], ALU.mult))
                then(dve.tensor_tensor(gates[:, 1, :], gates[:, 0, :], vexp[:, :], ALU.mult))
                dve.wait_ge(pair_used, 2 * T)
                then(dve.tensor_copy(slots[:, :], slot_ps[:, :]))
def experts(nc, sem, n2_d, w_gate, w_up, w_down, ident_d, wg, wu, raw, raw_in, hi_ready, lo_ready, slots, starts,
            ends, y_d):
    SIGNALLED = [0, 1, 2, 4, 6, 8, 9, 10]

    with ExitStack() as ctx:
        def sb(name, shape, dt=F32):
            return ctx.enter_context(nc.sbuf_tensor(name, shape, dt))

        def ps(name, shape):
            return ctx.enter_context(nc.psum_tensor(name, shape, F32))

        ident = sb("ident6", [P, P])
        wd = [sb(f"wd_{part}", [P, KF, D], F32R) for part in ("hi", "lo")]
        idx = sb("idx6", [P, 1], I32)
        x = sb("x6", [P, D])
        xT_hi = sb("xT_hi", [P, KD, P], F32R)
        xT_lo = sb("xT_lo", [P, KD, P], F32R)
        hid = sb("hid", [P, FF])
        hT_hi = sb("hT_hi", [P, KF, P], F32R)
        hT_lo = sb("hT_lo", [P, KF, P], F32R)
        y = sb("y6", [P, D])

        xT_ps = ps("xT_ps", [P, KD, P])
        g_ps = ps("g_ps", [P, FF])
        u_ps = ps("u_ps", [P, 2, FF])
        y_ps = ps("y_ps", [P, 2, 512])

        ident_in = sem("p6_ident_in")
        piece_used = sem("p6_piece_used")
        idx_ready = sem("p6_idx_ready")
        gathering = sem("p6_gathering")
        x_in = sem("p6_x_in")
        x_turned = sem("p6_x_turned")
        xT_ready = sem("p6_xT_ready")
        xT_split = sem("p6_xT_split")
        g_done = sem("p6_g_done")
        u_done = sem("p6_u_done")
        silu_ready = sem("p6_silu_ready")
        hid_ready = sem("p6_hid_ready")
        h_turned = sem("p6_h_turned")
        hT_ready = sem("p6_hT_ready")
        hT_split = sem("p6_hT_split")
        y_done = sem("p6_y_done")
        y_ready = sem("p6_y_ready")
        all_stored = sem("p6_all_stored")
        y_stored = sem("p6_y_stored")

        def block_count(eng):
            return eng.value_load(starts[0:1, N_EXPERTS:N_EXPERTS + 1], min_val=1, max_val=BLOCKS)

        def over_experts(eng, one_block):
            def expert(e, replaced):
                first = eng.value_load(starts[0:1, bass.ds(e, 1)], min_val=0, max_val=BLOCKS - 1)
                last = eng.value_load(ends[0:1, bass.ds(e, 1)], min_val=0, max_val=BLOCKS - 1)
                with eng.If(first < last):
                    with eng.Fori(first, last) as b:
                        one_block(b, e, False)
                one_block(last, e, replaced)

            with eng.Fori(0, N_EXPERTS - 1) as e:
                expert(e, True)
            expert(N_EXPERTS - 1, False)

        def hi_there(e, k):
            return part_ready(HI_BY, hi_ready, e, k)

        def lo_there(e, k):
            return part_ready(LO_BY, lo_ready, e, k)

        def wait_used(eng, b, e, k):
            if k in SIGNALLED:
                eng.wait_ge(piece_used, e * len(SIGNALLED) + (SIGNALLED.index(k) + 1))
            elif k == 3:
                eng.wait_ge(g_done, b + 1)
            elif k == PIECES - 1:
                eng.wait_ge(y_done, b + 1)
            else:
                eng.wait_ge(u_done, b * 2 + (k - 3) // 2)

        HI = (wg[0], wu[0], wd[0])
        LO = (wg[1], wu[1], wd[1])

        with nc.Block() as block:
            @block.sync
            def _(sp):
                sp.dma_start(ident[:, :], ident_d).then_inc(ident_in, 16)

                with sp.Fori(0, N_EXPERTS - 1) as e:
                    for k in range(PIECES):
                        sp.wait_ge(*(lo_there(e + 1, k - RAW) if k >= RAW else lo_there(e, k - RAW + PIECES)))
                        load_piece(sp, (w_gate, w_up, w_down), raw, raw_in, e + 1, k)

            @block.gpsimd
            def _(pool):
                nb = block_count(pool)

                def gather(b):
                    pool.wait_ge(x_turned, b + 1)
                    pool.tensor_copy(idx[:, :], slots[:, bass.ds(b, 1)]).then_inc(idx_ready, 1)
                    pool.wait_ge(idx_ready, b + 1)
                    pool.sem_inc(gathering, 1)
                    pool.indirect_dma_start(x[:, :], None, n2_d, bass.IndirectOffsetOnAxis(ap=idx[:, 0:1], axis=0))\
                        .then_inc(x_in, 16)

                def lows(e, first=0):
                    for k in range(first, PIECES):
                        if LO_BY[k] == "pool":
                            pool.wait_ge(*hi_there(e, k))
                            pool.tensor_tensor(piece(LO, k), raw_piece(raw, k), piece(HI, k), ALU.subtract)\
                                .then_inc(lo_ready["pool"], 1)

                def one_block(b, e, replaced):
                    gather(b + 1)
                    if replaced:
                        lows(e + 1)

                gather(0)
                lows(0, 8)
                over_experts(pool, one_block)
                pool.wait_ge(x_in, (nb + 1) * 16)
                pool.sem_inc(gathering, 1)

            @block.scalar
            def _(act):
                nb = block_count(act)
                act.sem_inc(y_ready, 1)
                act.sem_inc(y_stored, 16)

                def copy_xT(b):
                    act.wait_ge(x_turned, b + 2)
                    act.copy(xT_hi[:, :, :], xT_ps[:, :, :]).then_inc(xT_ready, 1)

                def copy_hT(b, half):
                    act.wait_ge(h_turned, b * 2 + (half + 2))
                    src = g_ps if half == 0 else u_ps[:, 0, :]
                    act.copy(hT_hi[:, 2 * half:2 * half + 2, :], src[:, 0:HALF].rearrange("p (k n) -> p k n", k=2))\
                        .then_inc(hT_ready, 1)

                def one_block(b, e, replaced):
                    def pieces(first, last):
                        if replaced:
                            for k in range(first, last):
                                if HI_BY[k] != "act":
                                    continue
                                wait_used(act, b, e, k)
                                act.wait_ge(raw_in[k % RAW], e * 32 + (32 + 16 * (k // RAW) + 16))
                                act.copy(piece(HI, k), raw_piece(raw, k)).then_inc(hi_ready["act"], 1)

                    act.wait_ge(g_done, b + 1)
                    act.wait_ge(h_turned, b * 2 + 1)
                    act.activation(hid[:, :], g_ps[:, :], ACT.Silu).then_inc(silu_ready, 1)
                    pieces(3, 5)
                    copy_hT(b, 0)
                    copy_hT(b, 1)
                    copy_xT(b + 1)
                    pieces(5, 11)
                    act.wait_ge(y_done, b + 1)
                    act.wait_ge(y_stored, b * 16 + 16)
                    act.copy(y[:, 512:], y_ps[:, 1, :]).then_inc(y_ready, 1)
                    pieces(11, 12)
                    act.wait_ge(y_ready, b * 2 + 4)
                    act.dma_start(y_d[bass.ds(b * P, P), :], y[:, :]).then_inc(y_stored, 16)

                copy_xT(0)
                for k in range(8, PIECES):
                    act.wait_ge(raw_in[k % RAW], 16 * (k // RAW) + 16)
                    act.copy(piece(HI, k), raw_piece(raw, k)).then_inc(hi_ready["act"], 1)
                over_experts(act, one_block)
                act.wait_ge(y_stored, nb * 16 + 16)
                act.sem_inc(all_stored, 1)

            @block.vector
            def _(dve):
                dve.sem_inc(y_ready, 1)

                def high(e, k):
                    dve.wait_ge(raw_in[k % RAW], e * 32 + (16 * (k // RAW) + 16))
                    dve.tensor_copy(piece(HI, k), raw_piece(raw, k)).then_inc(hi_ready["dve"], 1)

                def low(e, k):
                    if LO_BY[k] == "dve":
                        dve.wait_ge(*hi_there(e, k))
                        dve.tensor_tensor(piece(LO, k), raw_piece(raw, k), piece(HI, k), ALU.subtract)\
                            .then_inc(lo_ready["dve"], 1)

                def split_xT(b):
                    dve.wait_ge(xT_ready, b + 1)
                    dve.tensor_tensor(xT_lo[:, :, :], xT_ps[:, :, :], xT_hi[:, :, :], ALU.subtract)\
                        .then_inc(xT_split, 1)

                def split_hT(b, half):
                    dve.wait_ge(hT_ready, b * 2 + (half + 1))
                    src = g_ps if half == 0 else u_ps[:, 0, :]
                    dve.tensor_tensor(hT_lo[:, 2 * half:2 * half + 2, :],
                                      src[:, 0:HALF].rearrange("p (k n) -> p k n", k=2),
                                      hT_hi[:, 2 * half:2 * half + 2, :], ALU.subtract).then_inc(hT_split, 1)

                def hidden(b, half):
                    dve.wait_ge(u_done, b * 2 + (half + 1))
                    cols = slice(half * HALF, (half + 1) * HALF)
                    dve.tensor_tensor(hid[:, cols], hid[:, cols], u_ps[:, half, 0:HALF], ALU.mult)\
                        .then_inc(hid_ready, 1)

                def one_block(b, e, replaced):
                    def lows(*ks):
                        if replaced:
                            for k in ks:
                                low(e + 1, k)

                    if replaced:
                        for k in range(3):
                            wait_used(dve, b, e, k)
                            high(e + 1, k)
                            low(e + 1, k)
                    lows(3)
                    dve.wait_ge(silu_ready, b + 1)
                    hidden(b, 0)
                    hidden(b, 1)
                    split_hT(b, 0)
                    split_hT(b, 1)
                    split_xT(b + 1)
                    lows(5, 6)
                    lows(8, 10)
                    dve.wait_ge(y_done, b + 1)
                    dve.wait_ge(y_stored, b * 16 + 16)
                    dve.tensor_copy(y[:, 0:512], y_ps[:, 0, :]).then_inc(y_ready, 1)
                    lows(11)

                split_xT(0)
                for k in range(8, PIECES):
                    low(0, k)
                over_experts(dve, one_block)

            @block.tensor
            def _(pe):
                def turn_x(b):
                    pe.wait_ge(x_in, b * 16 + 16)
                    for k in range(KD):
                        mm = pe.transpose(xT_ps[:, k, :], x[:, k * P:(k + 1) * P], ident[:, :])
                    mm.then_inc(x_turned, 1)

                def turn_h(b, half):
                    pe.wait_ge(hid_ready, b * 2 + (half + 1))
                    out = g_ps if half == 0 else u_ps[:, 0, :]
                    for k in range(2):
                        at = (2 * half + k) * P
                        mm = pe.transpose(out[:, k * P:(k + 1) * P], hid[:, at:at + P], ident[:, :])
                    mm.then_inc(h_turned, 1)

                def one_block(b, e, replaced):
                    def used(mm, k):
                        if replaced and k in SIGNALLED:
                            mm.then_inc(piece_used, 1)

                    pe.wait_ge(xT_split, b + 1)
                    for k in range(KD):
                        if k % 2 == 0:
                            pe.wait_ge(*lo_there(e, k // 2))
                        mm = split_product(pe, g_ps[:, :], xT_hi[:, k, :], xT_lo[:, k, :], wg[0][:, k, :],
                                           wg[1][:, k, :], k == 0, k == KD - 1)
                        if k == KD - 1:
                            mm.then_inc(g_done, 1)
                        if k % 2 == 1:
                            used(mm, k // 2)
                    for half in range(2):
                        cols = slice(half * HALF, (half + 1) * HALF)
                        for k in range(KD):
                            if k % 4 == 0:
                                pe.wait_ge(*lo_there(e, 4 + 2 * half + k // 4))
                            mm = split_product(pe, u_ps[:, half, 0:HALF], xT_hi[:, k, :], xT_lo[:, k, :],
                                               wu[0][:, k, cols], wu[1][:, k, cols], k == 0, k == KD - 1)
                            if k == KD - 1:
                                mm.then_inc(u_done, 1)
                            if k % 4 == 3:
                                used(mm, 4 + 2 * half + k // 4)
                    turn_h(b, 0)
                    turn_x(b + 1)
                    turn_h(b, 1)
                    pe.wait_ge(y_ready, b * 2 + 2)
                    for k in range(KF):
                        if k % 2 == 0:
                            pe.wait_ge(hT_split, b * 2 + (k // 2 + 1))
                        pe.wait_ge(*lo_there(e, 8 + k))
                        for half in range(2):
                            cols = slice(half * 512, (half + 1) * 512)
                            mm = split_product(pe, y_ps[:, half, :], hT_hi[:, k, :], hT_lo[:, k, :], wd[0][:, k, cols],
                                               wd[1][:, k, cols], k == 0, k == KF - 1)
                        if k == KF - 1:
                            mm.then_inc(y_done, 1)
                        used(mm, 8 + k)

                pe.sem_inc(x_turned, 1)
                pe.sem_inc(h_turned, 1)
                pe.wait_ge(ident_in, 16)
                turn_x(0)
                over_experts(pe, one_block)


def combine(nc, sem, y_d, final_g, h_sb, gates, dest, out):
    RING = 4
    AHEAD = RING - 1

    def over_rings(eng, tile):
        for s in range(RING):
            tile(s, s)
        with eng.Fori(1, TILES // RING - 1) as i:
            for s in range(RING):
                tile(i * RING + s, s)
        for s in range(RING):
            tile(TILES - RING + s, s)

    with ExitStack() as ctx:
        def sb(name, shape, dt=F32):
            return ctx.enter_context(nc.sbuf_tensor(name, shape, dt))

        g_bc = sb("gf_bc", [P, D])
        power = sb("power7", [P, 2])
        idx = sb("idx7", [P, RING, 2, 1], I32)
        gate = sb("gate7", [P, RING, 2, 1])
        y = sb("y7", [P, RING, 2, D])
        acc = sb("acc7", [P, 2, D])
        sq = sb("sq7", [P, D], BF16)
        ss = sb("ss7", [P, 2])
        var = sb("var7", [P, 2])
        rstd = sb("rstd7", [P, 2])
        o = sb("o7", [P, 2, D])

        const_in = sem("p7_const_in")
        power_ready = sem("p7_power_ready")
        idx_ready = sem("p7_idx_ready")
        gathering = sem("p7_gathering")
        y_in = [sem(f"p7_y_in{s}") for s in range(RING)]
        acc_step = sem("p7_acc_step")
        ss_ready = sem("p7_ss_ready")
        var_ready = sem("p7_var_ready")
        rstd_ready = sem("p7_rstd_ready")
        o_ready = sem("p7_o_ready")
        stored = [sem("p7_stored0"), sem("p7_stored1")]

        with nc.Block() as block:
            @block.sync
            def _(sp):
                sp.dma_start(g_bc[:, :], row_broadcast(final_g, D)).then_inc(const_in, 16)

                def tile(t, s):
                    sp.wait_ge(o_ready, t + 1)
                    sp.dma_start(out[bass.ts(t, P), :], o[:, s % 2, :]).then_inc(stored[s % 2], 16)

                over_rings(sp, tile)
                for s in range(2):
                    sp.wait_ge(stored[s], 8 * TILES)

            @block.gpsimd
            def _(pool):
                pool.memset(power[:, 0:1], -0.5).then_inc(power_ready, 1)
                pool.memset(power[:, 1:2], EPS).then_inc(power_ready, 1)
                pool.wait_ge(power_ready, 2)

                def gather(t, s):
                    if not (static(t) and t < RING):
                        pool.wait_ge(acc_step, t * 2 - (2 * RING - 2))
                    one = bass.ds(t, 1)
                    pool.tensor_copy(idx[:, s, :, :], dest[:, :, one]).then_inc(idx_ready, 1)
                    pool.tensor_copy(gate[:, s, :, :], gates[:, :, one]).then_inc(idx_ready, 1)
                    pool.wait_ge(idx_ready, t * 2 + 2)
                    pool.sem_inc(gathering, 1)
                    for k in range(2):
                        pool.indirect_dma_start(y[:, s, k, :], None, y_d,
                                                bass.IndirectOffsetOnAxis(ap=idx[:, s, k, :], axis=0))\
                            .then_inc(y_in[s], 16)

                def tile(t, s):
                    if not (static(t) and t >= TILES - AHEAD):
                        gather(t + AHEAD, (s + AHEAD) % RING)
                    b = s % 2
                    pool.wait_ge(ss_ready, t + 1)
                    pool.tensor_tensor(var[:, b:b + 1], ss[:, b:b + 1], power[:, 1:2], ALU.add).then_inc(var_ready, 1)
                    pool.wait_ge(var_ready, t + 1)
                    pool.tensor_tensor(rstd[:, b:b + 1], var[:, b:b + 1], power[:, 0:1], ALU.pow)\
                        .then_inc(rstd_ready, 1)

                for t in range(AHEAD):
                    gather(t, t)
                over_rings(pool, tile)

            @block.scalar
            def _(act):
                def tile(t, s):
                    act.wait_ge(acc_step, t * 2 + 2)
                    if not (static(t) and t < 2):
                        act.wait_ge(o_ready, t - 1)
                    b = s % 2
                    if not (static(t) and t == 0):
                        act.wait_ge(ss_ready, t)
                    act.activation(sq[:, :], acc[:, b, :], ACT.Square, scale=1.0 / math.sqrt(D),
                                   accum_out=ss[:, b:b + 1]).then_inc(ss_ready, 1)

                over_rings(act, tile)

            @block.vector
            def _(dve):
                def normalize(t, b):
                    dve.wait_ge(rstd_ready, t + 1)
                    if not (static(t) and t < 2):
                        dve.wait_ge(stored[b], (t - b) * 8)
                    dve.scalar_tensor_tensor(out=o[:, b, :], in0=acc[:, b, :], scalar=rstd[:, b:b + 1],
                                             in1=g_bc[:, :], op0=ALU.mult, op1=ALU.mult).then_inc(o_ready, 1)

                def tile(t, s):
                    b = s % 2
                    dve.wait_ge(y_in[s], (t - s) * (32 // RING) + 32)
                    if not (static(t) and t < 2):
                        dve.wait_ge(o_ready, t - 1)
                    h = h_sb[:, t:t + 1, :] if static(t) else h_sb[:, bass.ds(t, 1), :]
                    dve.scalar_tensor_tensor(out=acc[:, b:b + 1, :], in0=y[:, s, 0:1, :], scalar=gate[:, s, 0, :],
                                             in1=h, op0=ALU.mult, op1=ALU.add).then_inc(acc_step, 1)
                    dve.wait_ge(acc_step, t * 2 + 1)
                    dve.scalar_tensor_tensor(out=acc[:, b, :], in0=y[:, s, 1, :], scalar=gate[:, s, 1, :],
                                             in1=acc[:, b, :], op0=ALU.mult, op1=ALU.add).then_inc(acc_step, 1)
                    if not (static(t) and t == 0):
                        normalize(t - 1, 1 - b)

                dve.wait_ge(const_in, 16)
                over_rings(dve, tile)
                normalize(TILES - 1, 1)
def build(nc, x, norm1_g, w_in, lambda_q1, lambda_k1, lambda_q2, lambda_k2, subln_g, sinks, w_out, norm2_g,
          w_router_group, b_router_group, w_router_expert, b_router_expert, w_gate, w_up, w_down, final_g,
          rope, ident, causal, band, tables, out):
    qk_d = nc.dram_tensor("qk_scratch", [2, QK_BLOCKS, P, SEQ], F32).ap()
    v_d = nc.dram_tensor("v_scratch", [SEQ, V_COLS], F32).ap()
    mix_d = nc.dram_tensor("mix_scratch", [KD, P, SEQ], F32).ap()
    n2_d = nc.dram_tensor("n2_scratch", [SEQ, D], F32).ap()
    y_d = nc.dram_tensor("y_scratch", [(BLOCKS + 1) * P, D], F32).ap()
    with ExitStack() as ctx:
        def sb(name, shape, dt=F32):
            return ctx.enter_context(nc.sbuf_tensor(name, shape, dt))

        def sem(name):
            return ctx.enter_context(nc.semaphore(name))

        projection(nc, sem, x, norm1_g, w_in, rope, ident, qk_d, v_d)
        diff_attention(nc, sem, qk_d, v_d, (lambda_q1, lambda_k1, lambda_q2, lambda_k2), subln_g, ident, causal, mix_d,
                       y_d)
        with nc.sbuf_tensor("logits", [P, TILES, LOGITS], F32, side="right") as logits:
            with ExitStack() as wo:
                def right(name, shape, dt=F32):
                    return wo.enter_context(nc.sbuf_tensor(name, shape, dt, side="right"))

                wo_hi = right("wo_hi", [P, KD, D], F32R)
                wo_lo = right("wo_lo", [P, KD, D], F32R)
                wo_raw = right("wo_raw", [P, 2, D])
                wo_split = sem("wo_split")
                window_attention(nc, sem, qk_d, v_d, sinks, ident, band, mix_d, w_out, wo_hi, wo_lo, wo_raw, wo_split)
                h_sb = sb("h_sb", [P, TILES, D])
                gates = sb("gates", [P, 2, TILES])
                dest = sb("dest", [P, 2, TILES], I32)
                slots = sb("slots", [P, BLOCKS + 1], I32)
                starts = sb("starts", [P, N_EXPERTS + 1], I32)
                ends = sb("ends", [P, N_EXPERTS], I32)
                output_projection(nc, sem, x, mix_d, wo_hi, wo_lo, wo_split, norm2_g, w_router_group, b_router_group,
                                  w_router_expert, b_router_expert, ident, h_sb, logits, n2_d)
            wg = [sb(f"wg_{part}", [P, KD, FF], F32R) for part in ("hi", "lo")]
            wu = [sb(f"wu_{part}", [P, KD, FF], F32R) for part in ("hi", "lo")]
            raw = sb("raw_pieces", [P, RAW, PW])
            raw_in = [sem(f"raw_in{r}") for r in range(RAW)]
            hi_ready = {by: sem(f"hi_by_{by}") for by in ("act", "dve")}
            lo_ready = {by: sem(f"lo_by_{by}") for by in ("dve", "pool")}
            routing(nc, sem, logits, tables, gates, dest, slots, starts, ends, (w_gate, w_up, w_down), wg, wu, raw,
                    raw_in, hi_ready, lo_ready)
        experts(nc, sem, n2_d, w_gate, w_up, w_down, ident, wg, wu, raw, raw_in, hi_ready, lo_ready, slots,
                starts, ends, y_d)
        combine(nc, sem, y_d, final_g, h_sb, gates, dest, out)


def constants():
    inv = (1.0 / (10000.0 ** (np.arange(0, HD, 2, dtype=np.float32) / np.float32(HD)))).astype(np.float32)
    ang = np.arange(SEQ, dtype=np.float32)[:, None] * inv[None, :]
    c, s, q = np.cos(ang), np.sin(ang), np.float32(HD ** -0.5)
    rope = np.concatenate([c * q, c * q, -s * q, s * q, c, c, -s, s], axis=1).astype(np.float32)
    r = np.arange(P)
    eye = np.eye(P, dtype=np.float32)
    own = np.where(r[None, :] > r[:, None], NEG, 0.0)
    ahead = np.where(r[None, :] <= r[:, None], NEG, 0.0)
    none = np.full((P, P), NEG)
    tables = [r[:, None] < r[None, :], np.ones((P, P)), np.broadcast_to(r[None, :], (P, P)),
              r[:, None] + P * r[None, :]]
    return {
        "rope": rope,
        "ident": eye,
        "causal": np.stack([eye, own]).astype(np.float32),
        "band": np.stack([eye, none, own, ahead, own]).astype(np.float32),
        "tables": np.stack(tables).astype(np.float32),
    }


_INS = ["x", "norm1_g", "w_in", "lambda_q1", "lambda_k1", "lambda_q2", "lambda_k2", "subln_g", "sinks", "w_out",
        "norm2_g", "w_router_group", "b_router_group", "w_router_expert", "b_router_expert", "w_gate", "w_up",
        "w_down", "final_g"]


def kernel(**inputs):
    import concourse.bacc as _bacc
    from concourse.bass_utils import run_bass_kernel_spmd as _run

    nc = _bacc.Bacc("TRN2", target_bir_lowering=False, num_devices=1)
    arrays, args = {}, {}

    def declare(name, a):
        arrays[f"in_{name}"] = a
        args[name] = nc.dram_tensor(f"in_{name}", a.shape, mybir.dt.from_np(a.dtype), kind="ExternalInput").ap()

    for name in _INS:
        a = np.ascontiguousarray(inputs[name])
        declare(name, a if name == "final_g" else a[0])
    for name, a in constants().items():
        declare(name, a)
    out = nc.dram_tensor("out_0", [SEQ, D], F32, kind="ExternalOutput").ap()
    build(nc, out=out, **args)
    r = _run(nc, [arrays], core_ids=[0])
    return r.results[0]["out_0"].reshape(1, SEQ, D)
```
